# Optimizing a Trainium2 kernel written in Bass

```python
import jax, jax.numpy as jnp
from jax import lax
import numpy as np

D_MODEL = 1024
BATCH = 1
SEQ = 1024
DEPTH = 1
DEC_BATCH = 8
DEC_SEQ = 4
PAST_LEN = 256
PAGE_SIZE = 128

N_HEADS = 8
HEAD_DIM = 64
ATT_DIM = N_HEADS * HEAD_DIM
IDX_HEADS = 8
IDX_DIM = 64
TOPK_MAX = 256
D_CONV = D_MODEL // 2
CONV_W = 31
D_FF = ((8 * D_MODEL // 3 + 255) // 256) * 256
ROPE_THETA = 10000.0
Q_BLOCK = 128
EPS = 1e-6
N_MOD = 9
NEG = -1e30
N_IN = 2 * D_CONV + 3 * ATT_DIM + IDX_HEADS * IDX_DIM + IDX_DIM + IDX_HEADS + 2 * D_MODEL

kernel_name = 'macaron_conv_dsa_hybrid_step'

def rmsnorm(x, g):
    xf = x.astype(jnp.float32)
    y = xf * lax.rsqrt(jnp.mean(xf * xf, axis=-1, keepdims=True) + EPS)
    return (y * g.astype(jnp.float32)).astype(x.dtype)

def layernorm(x, g, b):
    xf = x.astype(jnp.float32)
    mu = jnp.mean(xf, axis=-1, keepdims=True)
    var = jnp.mean(jnp.square(xf - mu), axis=-1, keepdims=True)
    y = (xf - mu) * lax.rsqrt(var + EPS)
    return (y * g.astype(jnp.float32) + b.astype(jnp.float32)).astype(x.dtype)

def rope_tables(pos, dim):
    inv = ROPE_THETA ** (-jnp.arange(0, dim, 2, dtype=jnp.float32) / dim)
    ang = pos.astype(jnp.float32)[:, None] * inv[None, :]
    return jnp.cos(ang), jnp.sin(ang)

def apply_rope(x, cos, sin):
    c = cos[None, :, None, :].astype(x.dtype)
    s = sin[None, :, None, :].astype(x.dtype)
    x1, x2 = jnp.split(x, 2, axis=-1)
    return jnp.concatenate([x1 * c - x2 * s, x2 * c + x1 * s], axis=-1)

def ada(c, w_ada, b_ada):
    m = jax.nn.silu(c) @ w_ada + b_ada
    m = m.reshape(c.shape[0], 1, N_MOD, D_MODEL)
    return tuple(m[:, :, i] for i in range(N_MOD))

def modulate(x, g, shift, scale):
    return rmsnorm(x, g) * (1.0 + scale) + shift

def swiglu(h, wg, wu, wd):
    return (jax.nn.silu(h @ wg) * (h @ wu)) @ wd

def split_in(n, w_in, cos_h, sin_h, cos_i, sin_i):
    B, T = n.shape[0], n.shape[1]
    z = n @ w_in
    sizes = [D_CONV, D_CONV, ATT_DIM, ATT_DIM, ATT_DIM, IDX_HEADS * IDX_DIM, IDX_DIM, IDX_HEADS, D_MODEL, D_MODEL]
    cuts = [int(s) for s in np.cumsum(sizes)[:-1]]
    a_lin, a_gate, q, k, v, qi, ki, wi, g_c, g_a = jnp.split(z, cuts, axis=-1)
    u = a_lin * jax.nn.sigmoid(a_gate)
    q = apply_rope(q.reshape(B, T, N_HEADS, HEAD_DIM), cos_h, sin_h)
    k = apply_rope(k.reshape(B, T, N_HEADS, HEAD_DIM), cos_h, sin_h)
    v = v.reshape(B, T, N_HEADS, HEAD_DIM)
    qi = apply_rope(qi.reshape(B, T, IDX_HEADS, IDX_DIM), cos_i, sin_i)
    ki = apply_rope(ki.reshape(B, T, 1, IDX_DIM), cos_i, sin_i)[:, :, 0]
    wi = wi * (IDX_HEADS * IDX_DIM) ** -0.5
    return u, q, k, v, qi, ki, wi, g_c, g_a

def conv_branch(u_ext, w_dw, b_dw, ln_g, ln_b, w_conv_out):
    kern = w_dw[:, None, :].astype(u_ext.dtype)
    y = lax.conv_general_dilated(u_ext, kern, window_strides=(1,), padding='VALID',
                                 dimension_numbers=('NWC', 'WIO', 'NWC'),
                                 feature_group_count=D_CONV) + b_dw
    y = jax.nn.silu(layernorm(y, ln_g, ln_b))
    return y @ w_conv_out

def index_scores(qi, ki, wi):
    s = jnp.einsum('bqhd,bld->bqhl', qi.astype(jnp.float32), ki.astype(jnp.float32))
    return jnp.einsum('bqhl,bqh->bql', jax.nn.relu(s), wi.astype(jnp.float32))

def sparse_attend(q, kg, vg, valid):
    logits = jnp.einsum('bqhd,bqkhd->bhqk', q.astype(jnp.float32), kg.astype(jnp.float32)) * HEAD_DIM ** -0.5
    logits = jnp.where(valid[:, None], logits, NEG)
    p = jax.nn.softmax(logits, axis=-1).astype(vg.dtype)
    return jnp.einsum('bhqk,bqkhd->bqhd', p, vg)

def take_rows(a, idx):
    return jax.vmap(lambda aa, ii: aa[ii])(a, idx)

def dsa_prompt(q, k, v, qi, ki, wi):
    B, T = q.shape[0], q.shape[1]
    topk = min(TOPK_MAX, T // 4)
    nb = T // Q_BLOCK
    key_pos = jnp.arange(T)

    def to_blocks(a):
        return a.reshape((B, nb, Q_BLOCK) + a.shape[2:]).swapaxes(0, 1)

    def block(args):
        bi, qb, qib, wib = args
        qpos = bi * Q_BLOCK + jnp.arange(Q_BLOCK)
        s = index_scores(qib, ki, wib)
        s = jnp.where(key_pos[None, None, :] <= qpos[None, :, None], s, NEG)
        _, idx = lax.top_k(s, topk)
        valid = idx <= qpos[None, :, None]
        return sparse_attend(qb, take_rows(k, idx), take_rows(v, idx), valid)

    out = lax.map(block, (jnp.arange(nb), to_blocks(q), to_blocks(qi), to_blocks(wi)))
    return out.swapaxes(0, 1).reshape(B, T, N_HEADS, HEAD_DIM)

def dsa_sample(q, k_new, v_new, qi, ki_new, wi, cache_k, cache_v, cache_idx_k, page_table):
    DB, S = q.shape[0], q.shape[1]
    past = page_table.shape[1] * PAGE_SIZE
    L = past + S
    topk = min(TOPK_MAX, L // 4)
    ki_past = cache_idx_k[page_table].reshape(DB, past, IDX_DIM).astype(ki_new.dtype)
    ki_all = jnp.concatenate([ki_past, ki_new], axis=1)
    qpos = past + jnp.arange(S)
    key_pos = jnp.arange(L)
    s = index_scores(qi, ki_all, wi)
    s = jnp.where(key_pos[None, None, :] <= qpos[None, :, None], s, NEG)
    _, idx = lax.top_k(s, topk)
    idx_p = jnp.minimum(idx, past - 1)
    phys = take_rows(page_table, idx_p // PAGE_SIZE)
    slot = idx_p % PAGE_SIZE
    kp = cache_k[phys, slot].astype(k_new.dtype)
    vp = cache_v[phys, slot].astype(v_new.dtype)
    idx_n = jnp.clip(idx - past, 0, S - 1)
    is_past = (idx < past)[..., None, None]
    kg = jnp.where(is_past, kp, take_rows(k_new, idx_n))
    vg = jnp.where(is_past, vp, take_rows(v_new, idx_n))
    valid = idx <= qpos[None, :, None]
    return sparse_attend(q, kg, vg, valid)

def trunk_layer(x, c, pos, conv_prefix, attend, lp):
    B, T = x.shape[0], x.shape[1]
    s1, sc1, g1, s2, sc2, g2, s3, sc3, g3 = ada(c, lp['w_ada'], lp['b_ada'])
    h = x + 0.5 * g1 * swiglu(modulate(x, lp['g_ffn1'], s1, sc1), lp['w1_gate'], lp['w1_up'], lp['w1_down'])
    n = modulate(h, lp['g_mix'], s2, sc2)
    cos_h, sin_h = rope_tables(pos, HEAD_DIM)
    cos_i, sin_i = rope_tables(pos, IDX_DIM)
    u, q, k, v, qi, ki, wi, g_c, g_a = split_in(n, lp['w_in'], cos_h, sin_h, cos_i, sin_i)
    u_ext = jnp.concatenate([conv_prefix.astype(u.dtype), u], axis=1)
    conv_out = conv_branch(u_ext, lp['w_dw'], lp['b_dw'], lp['ln_g'], lp['ln_b'], lp['w_conv_out'])
    att = attend(q, k, v, qi, ki, wi).reshape(B, T, ATT_DIM) @ lp['w_attn_o']
    mix = (jax.nn.sigmoid(g_c) * conv_out + jax.nn.sigmoid(g_a) * att) @ lp['w_out']
    h = h + g2 * mix
    h = h + 0.5 * g3 * swiglu(modulate(h, lp['g_ffn2'], s3, sc3), lp['w2_gate'], lp['w2_up'], lp['w2_down'])
    new_conv = u_ext[:, -(CONV_W - 1):]
    return h, k, v, ki, new_conv

def setup_inputs(seed: int = 0) -> dict:
    key = jax.random.key(seed)
    ks = iter(jax.random.split(key, 40))
    nrm = lambda shape, scale: jax.random.normal(next(ks), shape, jnp.float32) * scale
    n_pages = PAST_LEN // PAGE_SIZE
    n_pool = (DEC_BATCH * n_pages * 5) // 4
    perm = jax.random.permutation(next(ks), n_pool)[: DEC_BATCH * n_pages]
    page_table = perm.reshape(DEC_BATCH, n_pages).astype(jnp.int32)
    gain = lambda shape: 1.0 + nrm(shape, 0.1)
    return {
        'x_prompt': nrm((BATCH, SEQ, D_MODEL), 1.0),
        'x_sample': nrm((DEC_BATCH, DEC_SEQ, D_MODEL), 1.0),
        'cache_k': nrm((DEPTH, n_pool, PAGE_SIZE, N_HEADS, HEAD_DIM), 1.0),
        'cache_v': nrm((DEPTH, n_pool, PAGE_SIZE, N_HEADS, HEAD_DIM), 1.0),
        'cache_idx_k': nrm((DEPTH, n_pool, PAGE_SIZE, IDX_DIM), 1.0),
        'state_conv': nrm((DEPTH, DEC_BATCH, CONV_W - 1, D_CONV), 0.5),
        'page_table': page_table,
        'c_prompt': nrm((BATCH, D_MODEL), 1.0),
        'c_sample': nrm((DEC_BATCH, D_MODEL), 1.0),
        'w_ada': nrm((DEPTH, D_MODEL, N_MOD * D_MODEL), D_MODEL ** -0.5),
        'b_ada': nrm((DEPTH, N_MOD * D_MODEL), 0.01),
        'g_ffn1': gain((DEPTH, D_MODEL)),
        'w1_gate': nrm((DEPTH, D_MODEL, D_FF), D_MODEL ** -0.5),
        'w1_up': nrm((DEPTH, D_MODEL, D_FF), D_MODEL ** -0.5),
        'w1_down': nrm((DEPTH, D_FF, D_MODEL), D_FF ** -0.5),
        'g_mix': gain((DEPTH, D_MODEL)),
        'w_in': nrm((DEPTH, D_MODEL, N_IN), D_MODEL ** -0.5),
        'w_dw': nrm((DEPTH, CONV_W, D_CONV), CONV_W ** -0.5),
        'b_dw': nrm((DEPTH, D_CONV), 0.01),
        'ln_g': gain((DEPTH, D_CONV)),
        'ln_b': nrm((DEPTH, D_CONV), 0.01),
        'w_conv_out': nrm((DEPTH, D_CONV, D_MODEL), D_CONV ** -0.5),
        'w_attn_o': nrm((DEPTH, ATT_DIM, D_MODEL), ATT_DIM ** -0.5),
        'w_out': nrm((DEPTH, D_MODEL, D_MODEL), D_MODEL ** -0.5),
        'g_ffn2': gain((DEPTH, D_MODEL)),
        'w2_gate': nrm((DEPTH, D_MODEL, D_FF), D_MODEL ** -0.5),
        'w2_up': nrm((DEPTH, D_MODEL, D_FF), D_MODEL ** -0.5),
        'w2_down': nrm((DEPTH, D_FF, D_MODEL), D_FF ** -0.5),
        'g_final': gain((D_MODEL,)),
    }

def reference(x_prompt, x_sample, cache_k, cache_v, cache_idx_k, state_conv, page_table, c_prompt, c_sample,
              w_ada, b_ada, g_ffn1, w1_gate, w1_up, w1_down, g_mix, w_in, w_dw, b_dw, ln_g, ln_b,
              w_conv_out, w_attn_o, w_out, g_ffn2, w2_gate, w2_up, w2_down, g_final):
    B, T = x_prompt.shape[0], x_prompt.shape[1]
    DB, S = x_sample.shape[0], x_sample.shape[1]
    past = page_table.shape[1] * PAGE_SIZE
    pos_p = jnp.arange(T)
    pos_s = past + jnp.arange(S)
    hp, hs = x_prompt, x_sample
    kp_l, vp_l, ip_l, cp_l, ks_l, vs_l, is_l, cs_l = [], [], [], [], [], [], [], []
    for l in range(DEPTH):
        lp = {'w_ada': w_ada[l], 'b_ada': b_ada[l], 'g_ffn1': g_ffn1[l], 'w1_gate': w1_gate[l],
              'w1_up': w1_up[l], 'w1_down': w1_down[l], 'g_mix': g_mix[l], 'w_in': w_in[l],
              'w_dw': w_dw[l], 'b_dw': b_dw[l], 'ln_g': ln_g[l], 'ln_b': ln_b[l],
              'w_conv_out': w_conv_out[l], 'w_attn_o': w_attn_o[l], 'w_out': w_out[l],
              'g_ffn2': g_ffn2[l], 'w2_gate': w2_gate[l], 'w2_up': w2_up[l], 'w2_down': w2_down[l]}
        zero_prefix = jnp.zeros((B, CONV_W - 1, D_CONV), hp.dtype)
        hp, kp, vp, ip, cp = trunk_layer(hp, c_prompt, pos_p, zero_prefix, dsa_prompt, lp)
        ck, cv, ci = cache_k[l], cache_v[l], cache_idx_k[l]
        attend_s = lambda q, k, v, qi, ki, wi: dsa_sample(q, k, v, qi, ki, wi, ck, cv, ci, page_table)
        hs, ks_, vs_, is_, cs = trunk_layer(hs, c_sample, pos_s, state_conv[l], attend_s, lp)
        kp_l.append(kp); vp_l.append(vp); ip_l.append(ip); cp_l.append(cp)
        ks_l.append(ks_); vs_l.append(vs_); is_l.append(is_); cs_l.append(cs)
    y_prompt = rmsnorm(hp, g_final)
    y_sample = rmsnorm(hs, g_final)
    return (y_prompt, y_sample,
            jnp.stack(kp_l), jnp.stack(vp_l), jnp.stack(ip_l), jnp.stack(cp_l),
            jnp.stack(ks_l), jnp.stack(vs_l), jnp.stack(is_l), jnp.stack(cs_l))


_drawn_inputs = setup_inputs


def setup_inputs(seed=0):
    import zlib

    import numpy as np

    out = dict(_drawn_inputs(seed))
    spreads = {}
    factors = {'b_ada': 4.044, 'b_dw': 8.0, 'ln_b': 30.84}
    for name, (base, spread) in spreads.items():
        noise = np.random.default_rng([zlib.crc32(name.encode()), seed]).standard_normal(out[name].shape)
        drawn = base * np.exp(spread * noise) if base else spread * noise
        out[name] = __import__('jax').numpy.asarray(drawn.astype(out[name].dtype))
    for name, factor in factors.items():
        out[name] = (out[name] * factor).astype(out[name].dtype)
    return out
```

```python
from contextlib import ExitStack

import numpy as np
import concourse.bass as bass
from concourse import mybir

ALU = mybir.AluOpType
ACT = mybir.ActivationFunctionType
AX_X = mybir.AxisListType.X
F32 = mybir.dt.float32
F32R = mybir.dt.float32r
U32 = mybir.dt.uint32
I32 = mybir.dt.int32

P = 128
D = 1024
KD = D // P
SEQ = 1024
NSEQ = 8
SNEW = 4
NSAMP = NSEQ * SNEW
TOK = SEQ + NSAMP
TC = TOK // 3
NTC = 3
PLAST = SEQ - 2 * TC
NCOND = 1 + NSEQ
NMOD = 9
D_FF = 2816
NPAIR = D_FF // (2 * P)
H = 8
HD = 64
ATT = H * HD
D_CONV = 512
CW = 31
HIST = CW - 1
TOPK = 256
PAST = 256
TOPK_S = (PAST + SNEW) // 4
N_IN = 5192
EPS = 1e-6
NEG = -1e30
TAKEN = -3e38
IS_TAKEN = -2e38
INIT_ADA = 28
ADA_TILES = NMOD * KD

RING = 3
NBANK = 6
FFN_ACC = 36
FFN_ENDS = (3, 6, 9, 12, 24, 36)
T_FFN1 = RING
T_Z = T_FFN1 + 6 * NPAIR
NZ = 41
T_MIX = T_Z + NZ
T_OUT = T_MIX + KD
T_FFN2 = T_OUT + KD
ACC_FFN1 = FFN_ACC
ACC_Z = ACC_FFN1 + FFN_ACC * NPAIR
ACC_MIX = ACC_Z + 3 * NZ
ACC_OUT = ACC_MIX + 6 * KD
ACC_FFN2 = ACC_OUT + 3 * KD
ACC_END = ACC_FFN2 + FFN_ACC * NPAIR

ROW_BADA, ROW_G1, ROW_GM, ROW_G2, ROW_GF, ROW_LNG, ROW_LNB, ROW_BDW = 0, 72, 80, 88, 96, 104, 108, 112
NROWS = 116

C_ID, C_CAUSAL, C_SEL, C_SELT, C_EPS = 0, 128, 256, 320, 576
NCONST = C_EPS + 2
SKEYS = PAST + NSAMP
C_SMASK, C_IOTA = NCONST, NCONST + SKEYS


def constants():
    c = np.zeros((P, C_IOTA + SKEYS), np.float32)
    c[:, C_ID:C_ID + P] = np.eye(P)
    q, k = np.arange(P)[:, None], np.arange(P)[None]
    c[:, C_CAUSAL:C_CAUSAL + P] = np.where(k <= q, 0.0, NEG)
    row = np.arange(NSAMP)
    new = np.arange(NSAMP)
    ok = (new[None] // SNEW == row[:, None] // SNEW) & (new[None] % SNEW <= row[:, None] % SNEW)
    c[:NSAMP, C_SMASK + PAST:C_SMASK + SKEYS] = np.where(ok, 0.0, NEG)
    for half in range(2):
        for p in range(P):
            to = (half * 4 + p // 32) * SNEW + p % SNEW
            c[p, C_SEL + 32 * half + to] = 1.0
            c[to, C_SELT + P * half + p] = 1.0
    c[:, C_EPS] = EPS
    c[:, C_IOTA:] = np.arange(SKEYS)
    pos = np.concatenate([np.arange(SEQ), np.tile(PAST + np.arange(SNEW), NSEQ)]).astype(np.float32)
    inv = np.float32(10000.0) ** (-np.arange(0, HD, 2, dtype=np.float32) / np.float32(HD))
    ang = (pos[None] * inv[:, None].astype(np.float32)).astype(np.float32)
    cos, sin = np.cos(ang), np.sin(ang)
    rope = np.stack([np.concatenate([cos] * 4), np.concatenate([-sin, sin] * 2)], 1)
    return c, np.ascontiguousarray(rope, np.float32)


def build(nc, a, out, consts, rope):
    no_layer = ("x_prompt", "x_sample", "page_table", "c_prompt", "c_sample", "g_final")
    L0 = {n: t[0] for n, t in a.items() if n not in no_layer}
    with ExitStack() as ctx:
        def sem(name):
            return ctx.enter_context(nc.semaphore(name))

        at = [16640]

        def place(name, shape, dt, offset=None):
            size = 4
            for s in shape[1:]:
                size *= s
            if offset is None:
                offset = at[0]
                at[0] += (size + 31) // 32 * 32
            assert offset + size <= 229368, (name, offset + size)
            return nc.alloc_sbuf_tensor_at(name, list(shape), dt, offset=offset)

        cst = place("cst", [P, NCONST], F32)
        ident = cst[:, C_ID:C_ID + P]
        eps = cst[:, C_EPS:C_EPS + 1]
        ones = place("ones", [P, P], F32)
        par = place("par", [P, NROWS], F32)
        taps = place("taps", [P, 4, CW], F32)
        ada = place("ada", [P, ADA_TILES, NCOND], F32)
        mod_a = place("mod_a", [P, 3, KD, NCOND], F32)
        ccol = place("ccol", [P, KD, NCOND], F32)
        raw = place("raw", [P, RING, 8 * P], F32)
        whi = place("whi", [P, RING, 8 * P], F32R)
        wlo = place("wlo", [P, RING, 8 * P], F32R)
        HB = at[0]
        assert HB + (3 * KD + 4) * TOK * 4 + 11264 + 32768 <= 229368
        NB = HB + KD * TOK * 4
        RB = NB + 2 * KD * TOK * 4
        h = place("h", [P, KD, TOK], F32, HB)
        nhi = place("nhi", [P, KD, TOK], F32R, NB)
        nlo = place("nlo", [P, KD, TOK], F32R, NB + KD * TOK * 4)
        hid_hi = place("hid_hi", [P, 2, TOK], F32R, RB)
        hid_lo = place("hid_lo", [P, 2, TOK], F32R, RB + 2 * TOK * 4)
        sq = place("sq", [P, KD, TC], F32, RB)
        rstd = place("rstd", [P, TOK], F32, RB + 16896)
        small = place("small", [P, KD, NSAMP], F32, RB + 16896)
        tmp = place("tmp", [P, 8, TC], F32, RB + 16896 + 4224)
        ada_raw = place("ada_raw", [P, 2, KD, 4 * P], F32, RB + 16896 + 4224 + 11264)
        xtok = place("xtok", [P, 9, D], F32, NB)
        prow = place("prow", [NROWS, P], F32, NB + 9 * D * 4)
        wrow = place("wrow", [CW, D_CONV], F32, NB + 9 * D * 4 + 512)
        crow = place("crow", [NCOND, D], F32, NB + 9 * D * 4 + 512 + 2048)
        csil = place("csil", [NCOND, D], F32, NB + 9 * D * 4 + 512 + 2048 + 4096)

        main = ctx.enter_context(nc.psum_tensor("main", [P, NBANK, 512], F32))
        aux = ctx.enter_context(nc.psum_tensor("aux", [P, 2, 512], F32))

        raw_ready = [sem(f"raw_ready{s}") for s in range(RING)]
        hi_done = sem("hi_done")
        split_done = sem("split_done")
        acc_done = sem("acc_done")
        consts_in = sem("consts_in")
        rows_in = sem("rows_in")
        x_in = [sem(f"x_in{t}") for t in range(3)]
        ones_set = sem("ones_set")
        csil_done = sem("csil_done")
        init_t = sem("init_t")
        init_e = sem("init_e")
        ada_in = [sem("ada_in0"), sem("ada_in1")]
        ada_mm = sem("ada_mm")
        ada_out = sem("ada_out")
        mod_set = sem("mod_set")
        ki_out, v_out = sem("ki_out"), sem("v_out")
        y_out = [sem(f"y_out{g}") for g in range(3)]
        fin_t = sem("fin_t")
        fin_act = sem("fin_act")
        fin_dve = sem("fin_dve")
        NORM_STEPS = {"sq": 6, "mm": 3, "sd": 3, "rs": 3, "ml": 6, "af": 6, "hi": 6, "lo": 6, "fix": 6}
        norm_sem = {k: sem(f"norm_{k}") for k in NORM_STEPS}
        ln_sem = {k: sem(f"ln_{k}") for k in ("sq", "mm", "sd", "rs", "ml", "af", "hi", "lo")}
        FFN_STEPS = {"gate_free": 3 + 6 * NPAIR, "up_free": 3 + 6 * NPAIR, "down_free": 24 + 24 * NPAIR,
                     "hid_hi": 6 * NPAIR, "hid_lo": 6 * NPAIR, "samp": 8 * NPAIR}
        ffn_sem = {k: sem(f"ffn_{k}") for k in FFN_STEPS}

        def norm_wait(eng, q, k, count):
            eng.wait_ge(norm_sem[k], "1m2f".index(q) * NORM_STEPS[k] + count)

        def ffn_wait(eng, q, k, count):
            eng.wait_ge(ffn_sem[k], "12".index(q) * FFN_STEPS[k] + count)

        def load_tile(sp, T, slot, loads):
            sp.wait_ge(split_done, T - RING + 1)
            for dst, src in loads(raw[:, slot]):
                sp.dma_start(dst, src).then_inc(raw_ready[slot], 16)

        def cols(w, c0, n=P):
            return lambda slot: [(slot.rearrange("p (k m) -> p k m", k=KD)[:, :, 0:n],
                                  w.rearrange("(k p) m -> p k m", p=P)[:, :, c0:c0 + n])]

        def split(pool, T, slot, turn, used):
            pool.wait_ge(raw_ready[slot], turn * 16)
            pool.wait_ge(acc_done, used)
            pool.nop(nofuse=True)
            pool.tensor_copy(whi[:, slot], raw[:, slot]).then_inc(hi_done, 1)
            pool.wait_ge(hi_done, T - RING + 1)
            pool.tensor_tensor(wlo[:, slot], raw[:, slot], whi[:, slot].bitcast(F32), ALU.subtract)\
                .then_inc(split_done, 1)

        def product(pe, bank, slot, chunks, hi, lo, m0, m=P, mstride=P, c0=0):
            n = len(chunks)
            for i, c in enumerate(chunks):
                w = slice(mstride * (c0 + i) + m0, mstride * (c0 + i) + m0 + m)
                pe.matmul(bank, whi[:, slot, w], hi(c), start=(i == 0), stop=False)
                pe.matmul(bank, whi[:, slot, w], lo(c), start=False, stop=False)
                last = pe.matmul(bank, wlo[:, slot, w], hi(c), start=False, stop=(i == n - 1))
            return last

        def tcs(t):
            return slice(t * TC, (t + 1) * TC)

        def sp_init(sp):
            sp.dma_start(cst[:, :], consts[:, 0:NCONST]).then_inc(consts_in, 16)
            rows = [(ROW_BADA, L0["b_ada"], 72), (ROW_G1, L0["g_ffn1"], 8), (ROW_GM, L0["g_mix"], 8),
                    (ROW_G2, L0["g_ffn2"], 8), (ROW_GF, a["g_final"], 8), (ROW_LNG, L0["ln_g"], 4),
                    (ROW_LNB, L0["ln_b"], 4), (ROW_BDW, L0["b_dw"], 4)]
            sp.dma_start(crow[0:1, :], a["c_prompt"]).then_inc(rows_in, 16)
            sp.dma_start(crow[1:NCOND, :], a["c_sample"]).then_inc(rows_in, 16)
            for r, src, n in rows:
                sp.dma_start(prow[r:r + n, :], src.rearrange("(r p) -> r p", p=P)).then_inc(rows_in, 16)
            sp.dma_start(wrow[:, :], L0["w_dw"]).then_inc(rows_in, 16)
            xp = a["x_prompt"][0].rearrange("(t p) d -> p t d", p=P)
            sp.dma_start(xtok[:, 0:4, :], xp[:, 0:4, :]).then_inc(x_in[0], 16)
            sp.dma_start(xtok[:, 4:8, :], xp[:, 4:8, :]).then_inc(x_in[1], 16)
            sp.dma_start(xtok[0:NSAMP, 8, :], a["x_sample"].rearrange("b s d -> (b s) d")).then_inc(x_in[2], 16)

        def ada_load(sp, g, slot, turn):
            sp.wait_ge(ada_mm, g + 1)
            sp.dma_start(ada_raw[:, slot], L0["w_ada"].rearrange("(k p) m -> p k m", p=P)
                         [:, :, bass.ts(g, 4 * P)]).then_inc(ada_in[slot], 16)

        NINIT = 1 + 1 + 1 + 18

        def pe_init(pe):
            pe.wait_ge(consts_in, 16)
            pe.wait_ge(rows_in, 11 * 16)
            pe.transpose(main[:, 0, 0:NROWS], prow[:, :], ident[0:NROWS, 0:NROWS]).then_inc(init_t, 1)
            for c in range(4):
                last = pe.transpose(main[:, 1, CW * c:CW * (c + 1)], wrow[:, bass.ts(c, P)], ident[0:CW, 0:CW])
            last.then_inc(init_t, 1)
            pe.wait_ge(csil_done, 1)
            for c in range(KD):
                last = pe.transpose(main[:, 2, NCOND * c:NCOND * (c + 1)], csil[:, bass.ts(c, P)],
                                    ident[0:NCOND, 0:NCOND])
            last.then_inc(init_t, 1)
            for t in range(9):
                n = P if t < 8 else NSAMP
                if t % 4 == 0:
                    pe.wait_ge(x_in[t // 4], 16)
                for half in range(2):
                    g = 3 + 2 * t + half
                    if g >= NBANK:
                        pe.wait_ge(init_e, g - NBANK + 1)
                    for c in range(4):
                        last = pe.transpose(main[:, g % NBANK, c * P:c * P + n],
                                            xtok[0:n, t, bass.ts(4 * half + c, P)], ident[0:n, 0:n])
                    last.then_inc(init_t, 1)

        def act_init(act):
            act.wait_ge(rows_in, 11 * 16)
            act.activation(csil[:, :], crow[:, :], ACT.Silu).then_inc(csil_done, 1)

        def dve_init(dve):
            dve.memset(ones[:, :], 1.0).then_inc(ones_set, 1)
            dve.wait_ge(init_t, 1)
            dve.tensor_copy(par[:, :], main[:, 0, 0:NROWS]).then_inc(init_e, 1)
            dve.wait_ge(init_t, 2)
            dve.tensor_copy(taps[:, :, :], main[:, 1, 0:4 * CW].rearrange("p (c k) -> p c k", c=4)).then_inc(init_e, 1)
            dve.wait_ge(init_t, 3)
            dve.tensor_copy(ccol[:, :, :], main[:, 2, 0:KD * NCOND].rearrange("p (c k) -> p c k", c=KD))\
                .then_inc(init_e, 1)
            for g in range(3, NINIT):
                t, half = (g - 3) // 2, (g - 3) % 2
                n = P if t < 8 else NSAMP
                dve.wait_ge(init_t, g + 1)
                dve.tensor_copy(h[:, 4 * half:4 * half + 4, t * P:t * P + n],
                                main[:, g % NBANK, :].rearrange("p (c n) -> p c n", c=4)[:, :, 0:n]).then_inc(init_e, 1)

        def pe_ada(pe, g, slot, turn):
            pe.wait_ge(ada_in[slot], 16 * turn)
            pe.wait_ge(ada_out, g + 1)
            for t in range(4):
                for k in range(KD):
                    last = pe.matmul(aux[:, 0, NCOND * t:NCOND * (t + 1)], ada_raw[:, slot, k, bass.ts(t, P)],
                                     ccol[:, k, :], start=(k == 0), stop=(k == KD - 1))
            last.then_inc(ada_mm, 1)

        def dve_ada(dve, g):
            dve.wait_ge(ada_mm, g + 3)
            dve.tensor_tensor(ada[:, bass.ts(g, 4), :], aux[:, 0, 0:4 * NCOND].rearrange("p (t n) -> p t n", t=4),
                              par[:, bass.ts(g, 4)].unsqueeze(2).to_broadcast([P, 4, NCOND]), ALU.add)\
                .then_inc(ada_out, 1)

        def dve_mod(dve, i, grow, count):
            dve.wait_ge(ada_out, count + 1)
            s0 = (3 * i + 1) * KD
            dve.scalar_tensor_tensor(mod_a[:, i], ada[:, s0:s0 + KD, :], 1.0,
                                     par[:, grow:grow + KD].unsqueeze(2).to_broadcast([P, KD, NCOND]),
                                     ALU.add, ALU.mult).then_inc(mod_set, 1)

        def dve_half_gate(dve, i):
            g0 = (3 * i + 2) * KD
            dve.tensor_scalar(ada[:, g0:g0 + KD, :], ada[:, g0:g0 + KD, :], 0.5, None, ALU.mult).then_inc(mod_set, 1)

        def by_seq(ap):
            return ap.rearrange("p c (b s) -> p c b s", b=NSEQ)

        def cond(ap, c0, n):
            return ap[:, c0:c0 + n, 1:NCOND].unsqueeze(3).to_broadcast([P, n, NSEQ, SNEW])

        def norm(q, i, after_act=None, after_dve=None, after_pe=None):
            s = norm_sem
            a_of = None if i is None else mod_a[:, i]
            b_of = None if i is None else ada[:, 3 * i * KD:(3 * i + 1) * KD, :]

            def pe(pe):
                pe.wait_ge(ones_set, 1)
                for t in range(NTC):
                    norm_wait(pe, q, "sq", 2 * t + 2)
                    if t == 2:
                        norm_wait(pe, q, "sd", 1)
                    for c in range(KD):
                        last = pe.matmul(aux[:, t % 2, 0:TC], ones[:, :], sq[:, c, :], start=(c == 0), stop=(c == KD - 1))
                    last.then_inc(s["mm"], 1)
                    if after_pe and t:
                        after_pe(pe, t - 1)
                if after_pe:
                    after_pe(pe, NTC - 1)

            def act(act):
                def square(t):
                    if t:
                        norm_wait(act, q, "mm", t)
                    act.activation(sq[:, 0:4, :], h[:, 0:4, tcs(t)], ACT.Square).then_inc(s["sq"], 1)

                square(0)
                for t in range(NTC):
                    norm_wait(act, q, "mm", t + 1)
                    act.activation(rstd[:, tcs(t)], aux[:, t % 2, 0:TC], ACT.Sqrt, scale=1.0 / D, bias=eps)\
                        .then_inc(s["sd"], 1)
                    if t < 2:
                        square(t + 1)
                    n = TC if t < 2 else PLAST
                    for half in range(2):
                        g = 2 * t + half
                        norm_wait(act, q, "ml", g + 1)
                        for c in range(4 * half, 4 * half + 4):
                            if i is None:
                                last = act.activation(tmp[:, c, :], tmp[:, c, :], ACT.Copy,
                                                      scale=par[:, ROW_GF + c:ROW_GF + c + 1])
                            else:
                                last = act.activation(tmp[:, c, 0:n], tmp[:, c, 0:n], ACT.Identity,
                                                      scale=a_of[:, c, 0:1], bias=b_of[:, c, 0:1])
                        last.then_inc(s["af"], 1)
                        if i is not None:
                            norm_wait(act, q, "af", g + 1)
                            if t == 2:
                                norm_wait(act, q, "fix", 3 * half + 3)
                            act.activation(nhi[:, 4 * half:4 * half + 4, tcs(t)], tmp[:, 4 * half:4 * half + 4, :],
                                           ACT.Copy).then_inc(s["hi"], 1)
                    if after_act:
                        after_act(act, t)

            def dve(dve):
                def square(t):
                    if t:
                        norm_wait(dve, q, "mm", t)
                    dve.tensor_tensor(sq[:, 4:8, :], h[:, 4:8, tcs(t)], h[:, 4:8, tcs(t)], ALU.mult)\
                        .then_inc(s["sq"], 1)

                square(0)
                for t in range(NTC):
                    norm_wait(dve, q, "sd", t + 1)
                    dve.reciprocal(rstd[:, tcs(t)], rstd[:, tcs(t)]).then_inc(s["rs"], 1)
                    if t < 2:
                        square(t + 1)
                    norm_wait(dve, q, "rs", t + 1)
                    for half in range(2):
                        g = 2 * t + half
                        c4 = slice(4 * half, 4 * half + 4)
                        if t and i is not None:
                            norm_wait(dve, q, "lo", g - 1)
                        if t and i is None:
                            dve.wait_ge(fin_t, 6 * t)
                        dve.tensor_tensor(tmp[:, c4, :], h[:, c4, tcs(t)],
                                          rstd[:, tcs(t)].unsqueeze(1).to_broadcast([P, 4, TC]), ALU.mult)\
                            .then_inc(s["ml"], 1)
                        if t == 2 and i is not None:
                            norm_wait(dve, q, "ml", g + 1)
                            v = by_seq(tmp[:, c4, PLAST:TC])
                            for k, (m, op) in enumerate(((a_of, ALU.mult), (b_of, ALU.add))):
                                for_each = dve.tensor_tensor(v, v, cond(m, 4 * half, 4), op)
                                for_each.then_inc(s["fix"], 1 if k == 0 else 2)
                                if k == 0:
                                    norm_wait(dve, q, "fix", 3 * half + 1)
                    if i is not None:
                        for half in range(2):
                            g = 2 * t + half
                            c4 = slice(4 * half, 4 * half + 4)
                            norm_wait(dve, q, "hi", g + 1)
                            dve.tensor_tensor(nlo[:, c4, tcs(t)], tmp[:, c4, :], nhi[:, c4, tcs(t)].bitcast(F32),
                                              ALU.subtract).then_inc(s["lo"], 1)
                    if after_dve:
                        after_dve(dve, t)

            def ready(pe, t):
                norm_wait(pe, q, "lo", 2 * t + 2)
            return {"pe": pe, "act": act, "dve": dve, "ready": ready}

        norm_m = norm("m", 1)

        def ffn(q, T0, A0, wg, wu, wd, i, nrm, with_ada):
            f = ffn_sem
            gate = ada[:, (3 * i + 2) * KD:(3 * i + 3) * KD, :]
            order = ((0, wg, 0), (1, wu, 0), (2, wg, 1), (3, wu, 1))

            def sp(sp):
                with sp.Fori(0, NPAIR) as j:
                    for k, w, sub in order:
                        load_tile(sp, T0 + 6 * j + k, k % RING,
                                  lambda slot, w=w, sub=sub: [(slot.rearrange("p (k m) -> p k m", k=KD),
                                      w.rearrange("(k p) m -> p k m", p=P)[:, :, bass.ds((2 * j + sub) * P, P)])])
                    for k, half in ((4, 0), (5, 1)):
                        load_tile(sp, T0 + 6 * j + k, k % RING,
                                  lambda slot, half=half: [(slot.rearrange("p (f m) -> p f m", f=2),
                                      wd[bass.ds(j * 2 * P, 2 * P), 512 * half:512 * half + 512]
                                      .rearrange("(f p) m -> p f m", p=P))])
                    if with_ada:
                        g = INIT_ADA // 4 + j
                        sp.wait_ge(ada_mm, g + 2)
                        sp.dma_start(ada_raw[:, 1], L0["w_ada"].rearrange("(k p) m -> p k m", p=P)
                                     [:, :, bass.ds(g * 4 * P, 4 * P)]).then_inc(ada_in[1], 16)

            def pool(pool):
                if not with_ada:
                    pool.wait_ge(acc_done, A0 - 3)
                with pool.Fori(0, NPAIR) as j:
                    for k in range(6):
                        end = A0 + FFN_ENDS[k - 3] if k >= 3 else A0 + FFN_ENDS[k + 3] - FFN_ACC
                        split(pool, T0 + 6 * j + k, k % RING, turn(T0 + k) + 2 * j, 36 * j + end)

            def pe(pe):
                with pe.Fori(0, NPAIR) as j:
                    for sub in range(2):
                        for part, base in (("gate_free", 0), ("up_free", 3)):
                            k = 2 * sub + (base > 0)
                            pe.wait_ge(split_done, T0 + 6 * j + k + 1)
                            for t in range(NTC):
                                if sub == 0:
                                    ffn_wait(pe, q, "down_free", 24 * j + 19 + base + t)
                                else:
                                    ffn_wait(pe, q, part, 3 * (2 * j + 1) + t + 1)
                                if k == 0:
                                    nrm["ready"](pe, t)
                                product(pe, main[:, base + t, 0:TC], k % RING, range(KD),
                                        lambda c: nhi[:, c, tcs(t)], lambda c: nlo[:, c, tcs(t)], 0)\
                                    .then_inc(acc_done, 1)
                    if with_ada:
                        pe_ada(pe, INIT_ADA // 4 + j, 1, INIT_ADA // 8 + 1 + j)
                    for half in range(2):
                        pe.wait_ge(split_done, T0 + 6 * j + 4 + half + 1)
                        for t in range(NTC):
                            if half == 0:
                                ffn_wait(pe, q, "hid_lo", 6 * j + 3 + t + 1)
                            for m in range(4):
                                d = 12 * half + 4 * t + m
                                if d < 3:
                                    ffn_wait(pe, q, "gate_free", 6 * j + 7 + d)
                                elif d < 6:
                                    ffn_wait(pe, q, "up_free", 6 * j + 4 + d)
                                else:
                                    ffn_wait(pe, q, "down_free", 24 * j + d + 19)
                                product(pe, main[:, d % NBANK, 0:TC], (4 + half) % RING, range(2),
                                        lambda c: hid_hi[:, c, tcs(t)], lambda c: hid_lo[:, c, tcs(t)],
                                        m * P, mstride=512).then_inc(acc_done, 1)

            def act(act):
                act.drain().then_inc(f["gate_free"], 3)
                with act.Fori(0, NPAIR) as j:
                    for sub in range(2):
                        for t in range(NTC):
                            act.wait_ge(acc_done, A0 + 36 * j + 6 * sub + t + 1)
                            act.activation(tmp[:, t, :], main[:, t, 0:TC], ACT.Silu).then_inc(f["gate_free"], 1)
                            ffn_wait(act, q, "up_free", 3 + 6 * j + 3 * sub + t + 1)
                            act.activation(hid_hi[:, sub, tcs(t)], tmp[:, 3 + t, :], ACT.Copy).then_inc(f["hid_hi"], 1)

            def dve(dve):
                dve.drain().then_inc(f["up_free"], 3)
                dve.drain().then_inc(f["down_free"], 24)
                with dve.Fori(0, NPAIR) as j:
                    for sub in range(2):
                        for t in range(NTC):
                            dve.wait_ge(acc_done, A0 + 36 * j + 6 * sub + 3 + t + 1)
                            ffn_wait(dve, q, "gate_free", 3 + 6 * j + 3 * sub + t + 1)
                            dve.tensor_tensor(tmp[:, 3 + t, :], main[:, 3 + t, 0:TC], tmp[:, t, :], ALU.mult)\
                                .then_inc(f["up_free"], 1)
                            ffn_wait(dve, q, "hid_hi", 6 * j + 3 * sub + t + 1)
                            dve.tensor_tensor(hid_lo[:, sub, tcs(t)], tmp[:, 3 + t, :],
                                              hid_hi[:, sub, tcs(t)].bitcast(F32), ALU.subtract)\
                                .then_inc(f["hid_lo"], 1)
                    if with_ada:
                        dve_ada(dve, INIT_ADA // 4 + j)
                    for d in range(24):
                        half, t, m = d // 12, d % 12 // 4, d % 4
                        c = 4 * half + m
                        n = TC if t < 2 else PLAST
                        dve.wait_ge(acc_done, A0 + 36 * j + 12 + d + 1)
                        ffn_wait(dve, q, "down_free", 24 * j + d + 1)
                        if t == 2:
                            dve.tensor_tensor(small[:, c, :].rearrange("p (b s) -> p b s", b=NSEQ),
                                              main[:, d % NBANK, PLAST:TC].rearrange("p (b s) -> p b s", b=NSEQ),
                                              gate[:, c, 1:NCOND].unsqueeze(2).to_broadcast([P, NSEQ, SNEW]),
                                              ALU.mult).then_inc(f["samp"], 1)
                            ffn_wait(dve, q, "samp", 8 * j + 4 * half + m + 1)
                            dve.tensor_tensor(h[:, c, SEQ:TOK], h[:, c, SEQ:TOK], small[:, c, :], ALU.add)
                        dve.scalar_tensor_tensor(h[:, c, t * TC:t * TC + n], main[:, d % NBANK, 0:n], gate[:, c, 0:1],
                                                 h[:, c, t * TC:t * TC + n], ALU.mult, ALU.add)\
                            .then_inc(f["down_free"], 1)
            return {"sp": sp, "pool": pool, "pe": pe, "act": act, "dve": dve}

        w_in = L0["w_in"]
        qi = place("qi", [P, 4, TOK], F32, HB)
        conv_y = place("conv_y", [P, 4, TOK], F32, HB)
        zraw = place("zraw", [P, 2, TOK], F32, HB + 16896)
        zsw = place("zsw", [P, 2, TOK], F32, HB + 25344)
        pick = place("pick", [P, 36 * P], F32, RB)
        UB = RB + 36 * P * 4
        uext = place("uext", [P, 4, HIST + SEQ], F32, UB)
        ipage = place("ipage", [P, 2 * NSEQ, P], F32, UB)
        kis = place("kis", [P, 2, SKEYS], F32, UB + 8192)
        rs = place("rs", [P, 2, SKEYS], F32, UB + 10496)
        qib = place("qib", [P, 4, NSEQ, 32], F32, UB + 12800)
        uext_s = place("uext_s", [P, 4, NSEQ, HIST + SNEW], F32, UB + 16896)
        rot = place("rot", [P, 2, TOK], F32, UB + 21248)
        kiw = place("kiw", [72, TOK], F32, UB + 29696)
        ki_b = place("ki_b", [P, TOK], F32, UB + 33920)
        rbuf = place("rbuf", [P, 2, 512], F32, UB + 38144)
        state_tok = place("state_tok", [P, 2, D_CONV], F32, UB + 38144)
        kw_tok = place("kw_tok", [P, 9, 72], F32, UB + 42240)
        unew = place("unew", [P, 4, NSAMP], F32, UB + 42240)
        wabs = place("wabs", [P, 8, H], F32, UB + 44832)
        wsgn = place("wsgn", [P, 8, H], F32, UB + 45088)
        wr = place("wr", [P, 2], F32, UB + 45344)
        wra = place("wra", [P, 2], F32, UB + 45376)
        wrs = place("wrs", [P, 2], F32, UB + 45408)
        top8 = place("top8", [P, 8], F32, UB + 45440)
        at8 = place("at8", [NSAMP, 8], U32, UB + 45472)
        atf = place("atf", [NSAMP, 1], F32, UB + 45504)
        pick_s = place("pick_s", [NSAMP, SKEYS], F32, UB + 45536)
        one_s = place("one_s", [NSAMP, SKEYS], F32, UB + 29696)

        def dram(name, shape):
            return nc.dram_tensor(name, list(shape), F32, kind="Internal").ap()

        h_d, q_d, k_d, v_d = (dram(n, [P, c, TOK]) for n, c in (("h_d", KD), ("q_d", 4), ("k_d", 4), ("v_d", 4)))
        gate_d = dram("gate_d", [P, 2 * KD, TOK])
        w_d = dram("w_d", [NSEQ, H, SNEW])

        z_free = sem("z_free")
        swap_in = [sem("swap_in0"), sem("swap_in1")]
        rope_tab = sem("rope_tab")
        rope_a = sem("rope_a")
        rope_b = sem("rope_b")
        z_out = [sem("z_out0"), sem("z_out1")]
        glu = sem("glu")
        h_out = sem("h_out")
        page_in = sem("page_in")
        state_in = sem("state_in")
        kib_in = sem("kib_in")
        w_out_d = sem("w_out_d")
        wr_in = sem("wr_in")
        kw_t = sem("kw_t")
        kw_e = sem("kw_e")
        st_t = sem("st_t")
        st_e = sem("st_e")
        pg_t = sem("pg_t")
        pg_e = sem("pg_e")
        si_prep = sem("si_prep")
        si_mm = sem("si_mm")
        si_r = sem("si_r")
        si_s = sem("si_s")
        si_sel = sem("si_sel")
        wprep = sem("wprep")
        idx_mm = sem("idx_mm")
        idx_act = sem("idx_act")
        idx_dve = sem("idx_dve")
        tk = sem("tk")
        picked = sem("picked")
        cv = sem("cv")
        uzero = sem("uzero")

        def off(b):
            return P * (b * (b + 1) // 2)

        PIECES = [(b, hh, c0, min(512, P * (b + 1) - c0)) for b in range(2, 8) for hh in range(H)
                  for c0 in range(0, P * (b + 1), 512)]
        ZCOL = [3072] + [2560 + P * i for i in range(4)] + [1024 + P * i for i in range(12)] \
            + [512 * (i % 2) + P * (i // 2) for i in range(8)] + [3144 + P * i for i in range(16)]
        Z_Q, Z_V, Z_GLU, Z_GATE = 5, 13, 17, 25

        def m1_sp(sp):
            for L in range(3):
                load_tile(sp, T_Z + L, L % RING, cols(w_in, ZCOL[L], 72 if L == 0 else P))
            ffn_wait(sp, "1", "down_free", 24 * NPAIR + 24)
            sp.dma_start(h_d, h[:, :, :]).then_inc(h_out, 16)
            sp.wait_ge(ada_mm, ADA_TILES // 4 + 2)
            sp.dma_start(rot[:, :, :], rope).then_inc(rope_tab, 16)
            sp.dma_start(ki_b[0:NSAMP, 0:2 * SKEYS], consts[0:NSAMP, C_SMASK:C_SMASK + 2 * SKEYS])\
                .then_inc(rope_tab, 16)
            for g in range(2):
                sp.dma_start(state_tok[0:4 * HIST, g, :],
                             L0["state_conv"][4 * g:4 * g + 4].rearrange("b r d -> (b r) d")).then_inc(state_in, 16)
            norm_wait(sp, "m", "lo", 6)
            for b in range(NSEQ):
                for pg in range(2):
                    page = sp.value_load(a["page_table"][b:b + 1, pg:pg + 1], min_val=0,
                                         max_val=L0["cache_idx_k"].shape[0] - 1)
                    for twice in range(2):
                        sp.dma_start(ipage[:, 2 * b + pg, HD * twice:HD * (twice + 1)],
                                     L0["cache_idx_k"][bass.ds(page, 1), :, :].rearrange("o p d -> (o p) d"))\
                            .then_inc(page_in, 16)
            for L in range(3, Z_Q):
                load_tile(sp, T_Z + L, L % RING, cols(w_in, ZCOL[L]))
            sp.wait_ge(w_out_d, 16)
            sp.dma_start(wr[:, :], w_d.rearrange("(t b) h s -> (b h s) t", t=2),
                         allow_slow_non_contiguous=True).then_inc(wr_in, 16)
            for L in range(Z_Q, NZ):
                load_tile(sp, T_Z + L, L % RING, cols(w_in, ZCOL[L]))

        def m1_pool(pool):
            def post(L):
                s = L % 2
                if Z_Q <= L < Z_V:
                    n = L - Z_Q
                    pool.wait_ge(swap_in[s], SWAPS[L])
                    pool.wait_ge(z_free, 6 + 3 * L + 3)
                    pool.tensor_tensor(zsw[:, s, :], zsw[:, s, :], rot[:, 1, :], ALU.mult).then_inc(rope_b, 1)
                    pool.tensor_tensor(zraw[:, s, :], zraw[:, s, :], rot[:, 0, :], ALU.mult).then_inc(rope_b, 1)
                    pool.wait_ge(rope_b, 3 * n + 2)
                    pool.tensor_tensor(zraw[:, s, :], zraw[:, s, :], zsw[:, s, :], ALU.add).then_inc(rope_b, 1)
                elif Z_GLU <= L < Z_GATE and (L - Z_GLU) % 2:
                    c = (L - Z_GLU) // 2
                    pool.wait_ge(z_free, 6 + 3 * L + 3)
                    if c == 0:
                        pool.wait_ge(si_sel, 2)
                        pool.memset(uext[:, :, 0:HIST], 0.0).then_inc(uzero, 1)
                    pool.tensor_tensor(uext[:, c, HIST:], zraw[:, 1, 0:SEQ], zraw[:, 0, 0:SEQ], ALU.mult)\
                        .then_inc(glu, 1)
                    if c == 0:
                        pool.wait_ge(ki_out, 32)
                        pool.wait_ge(wprep, 6)
                    pool.tensor_tensor(unew[:, c, :], zraw[:, 1, SEQ:TOK], zraw[:, 0, SEQ:TOK], ALU.mult)\
                        .then_inc(glu, 1)
                    pool.tensor_tensor(uext_s[:, c, :, HIST:],
                                       zraw[:, 1, SEQ:TOK].rearrange("p (b s) -> p b s", b=NSEQ),
                                       zraw[:, 0, SEQ:TOK].rearrange("p (b s) -> p b s", b=NSEQ), ALU.mult)\
                        .then_inc(glu, 1)

            def one(L):
                used = ACC_Z + 3 * L - 6 if L >= 3 else ACC_Z - FFN_ACC + FFN_ENDS[3 + L]
                split(pool, T_Z + L, (T_Z + L) % RING, (T_Z + L) // RING, used)

            for L in range(28):
                one(L)
                if L >= 3:
                    post(L - 3)
            with pool.Fori(0, 4) as i:
                for k in range(3):
                    L = 28 + k
                    split(pool, T_Z + L + 3 * i, (T_Z + L) % RING, (T_Z + L) // RING + i, ACC_Z + 3 * L - 6 + 9 * i)
            one(40)

        SWAPS = {}
        n_swap = [0, 0]
        for L in range(Z_V):
            n_swap[L % 2] += 16 * (2 if L == 0 else 4)
            SWAPS[L] = n_swap[L % 2]

        def z_product(pe, L, T, slot, V, parity, m=P):
            pe.wait_ge(split_done, T + 1)
            for t in range(NTC):
                pe.wait_ge(z_free, V + t + 1)
                product(pe, main[0:m, 3 * parity + t, 0:TC], slot, range(KD),
                        lambda c: nhi[:, c, tcs(t)], lambda c: nlo[:, c, tcs(t)], 0, m=m).then_inc(acc_done, 1)

        def m1_pe(pe):
            ffn_wait(pe, "1", "down_free", 24 * NPAIR + 24)
            for L in range(Z_Q):
                if L == 0:
                    for t in range(NTC):
                        norm_m["ready"](pe, t)
                z_product(pe, L, T_Z + L, L % RING, 3 * L, L % 2, 72 if L == 0 else P)
            pe.wait_ge(z_free, 6 + 3 * Z_Q)
            pe.wait_ge(state_in, 32)
            for g in range(2):
                for c in range(4):
                    last = pe.transpose(main[:, 3 * g, bass.ts(c, 4 * HIST)], state_tok[0:4 * HIST, g, bass.ts(c, P)],
                                        ident[0:4 * HIST, 0:4 * HIST])
                last.then_inc(st_t, 1)
            pe.wait_ge(rope_a, 3)
            for t in range(9):
                n = P if t < 8 else NSAMP
                last = pe.transpose(aux[0:n, t // 5, bass.ts(t % 5, 72)], kiw[:, t * P:t * P + n], ident[0:72, 0:72])
                if t in (4, 8):
                    last.then_inc(kw_t, 1)
            pe.wait_ge(page_in, 16 * 4 * NSEQ)
            pe.wait_ge(si_prep, 4 + 9)
            for b in range(NSEQ):
                if b >= 2:
                    pe.wait_ge(pg_e, b - 1)
                for pg in range(2):
                    last = pe.transpose(main[:, 4 + b % 2, bass.ts(pg, P)], ipage[:, 2 * b + pg, :], ident)
                last.then_inc(pg_t, 1)
                pe.wait_ge(pg_e, b + 1)
                for c in range(4):
                    last = pe.matmul(main[32 * (b % 4):32 * (b % 4) + 32, b // 4 + 1, 0:SKEYS], qib[:, c, b, :],
                                     kis[:, b % 2, :], start=(c == 0), stop=(c == 3))
                last.then_inc(si_mm, 1)
            pe.wait_ge(st_e, 2)
            for half in range(2):
                pe.wait_ge(si_s, half + 1)
                last = pe.matmul(main[0:NSAMP, 0, 0:SKEYS], cst[:, C_SEL + 32 * half:C_SEL + 32 * half + 32],
                                 rs[:, half, :], start=(half == 0), stop=(half == 1))
            last.then_inc(si_sel, 1)
            pe.wait_ge(rope_a, 3 * Z_Q)
            pe.wait_ge(kib_in, 16)
            pe.wait_ge(kw_e, 3)
            for n, (b, hh, c0, w) in enumerate(PIECES):
                if n >= 2:
                    pe.wait_ge(idx_act, n - 1)
                lo = HD * (hh % 2)
                keys = kiw[0:HD, c0:c0 + w] if lo == 0 else ki_b[HD:P, c0:c0 + w]
                pe.matmul(aux[:, n % 2, 0:w], qi[lo:lo + HD, hh // 2, bass.ts(b, P)], keys, start=True, stop=True)\
                    .then_inc(idx_mm, 1)
            pe.wait_ge(si_sel, 2)
            pe.wait_ge(pg_e, NSEQ)
            pe.wait_ge(si_r, 2)
            with pe.Fori(0, 6) as i:
                for k in range(6):
                    L = Z_Q + k
                    z_product(pe, L, T_Z + L + 6 * i, (T_Z + L) % RING, 3 * L + 18 * i, L % 2)

        def evac(act, dst, L, i, func, src_rows=P, n=3):
            for t in range(NTC):
                act.wait_ge(acc_done, ACC_Z + 3 * L + t + 1 + i)
                act.activation(dst[0:src_rows, tcs(t)], main[0:src_rows, 3 * (L % 2) + t, 0:TC], func)\
                    .then_inc(z_free, 1)

        def swap(act, s, rows):
            for r in range(0, rows, 32):
                o = r + 32 if r % 64 == 0 else r - 32
                act.dma_start(zsw[r:r + 32, s, :], zraw[o:o + 32, s, :]).then_inc(swap_in[s], 16)

        def m1_act(act):
            act.wait_ge(h_out, 16)
            act.drain().then_inc(z_free, 6)
            for L in range(Z_Q):
                if L >= 2:
                    act.wait_ge(rope_a, 3 * (L - 1))
                for t in range(NTC):
                    act.wait_ge(acc_done, ACC_Z + 3 * L + t + 1)
                    if L == 0:
                        act.activation(kiw[64:72, tcs(t)], main[64:72, t, 0:TC], ACT.Copy).then_inc(wprep, 1)
                    n = 64 if L == 0 else P
                    act.activation(zraw[0:n, L % 2, tcs(t)], main[0:n, 3 * (L % 2) + t, 0:TC], ACT.Copy)\
                        .then_inc(z_free, 1)
                act.wait_ge(z_free, 6 + 3 * L + 3)
                swap(act, L % 2, 64 if L == 0 else P)
                if L == 0:
                    act.wait_ge(wprep, 3)
                    act.dma_start(w_d.rearrange("b h s -> h b s"),
                                  kiw[64:72, SEQ:TOK].rearrange("h (b s) -> h b s", b=NSEQ)).then_inc(w_out_d, 16)
                if L == 1:
                    act.wait_ge(rope_a, 3)
                    act.dma_start(ki_b[HD:P, :], kiw[0:HD, :]).then_inc(kib_in, 16)
            for g in range(2):
                act.wait_ge(st_t, g + 1)
                act.activation(uext_s[:, :, 4 * g:4 * g + 4, 0:HIST],
                               main[:, 3 * g, 0:16 * HIST].rearrange("p (c b r) -> p c b r", c=4, b=4), ACT.Copy)\
                    .then_inc(st_e, 1)
            for g, n in ((0, 5), (1, 4)):
                act.wait_ge(kw_t, g + 1)
                act.activation(kw_tok[:, 5 * g:5 * g + (5 if g == 0 else 3), :],
                               aux[:, g, 0:72 * (5 if g == 0 else 3)].rearrange("p (t c) -> p t c", c=72), ACT.Copy)\
                    .then_inc(kw_e, 1)
            act.activation(kw_tok[0:NSAMP, 8, :], aux[0:NSAMP, 1, 216:288], ACT.Copy).then_inc(kw_e, 1)
            act.wait_ge(kw_e, 3)
            act.dma_start(out[4][0, 0].rearrange("(t p) d -> p t d", p=P), kw_tok[:, 0:8, 0:HD]).then_inc(ki_out, 16)
            act.dma_start(out[8][0].rearrange("b s d -> (b s) d"), kw_tok[0:NSAMP, 8, 0:HD]).then_inc(ki_out, 16)
            for b in range(NSEQ):
                act.wait_ge(pg_t, b + 1)
                if b >= 2:
                    act.wait_ge(si_mm, b - 1)
                act.activation(kis[:, b % 2, 0:PAST], main[:, 4 + b % 2, 0:PAST], ACT.Copy).then_inc(pg_e, 1)
                if b % 4 == 3:
                    act.wait_ge(si_mm, b + 1)
                    if b == 3:
                        act.wait_ge(si_prep, 4 + 9 + 2)
                    act.activation(rs[:, b // 4, :], main[:, b // 4 + 1, 0:SKEYS], ACT.Relu,
                                   scale=wra[:, b // 4:b // 4 + 1]).then_inc(si_r, 1)
            act.wait_ge(wprep, 3 + 3)
            for n, (b, hh, c0, w) in enumerate(PIECES):
                act.wait_ge(idx_mm, n + 1)
                if n >= 2:
                    act.wait_ge(idx_dve, n - 1)
                act.activation(rbuf[:, n % 2, 0:w], aux[:, n % 2, 0:w], ACT.Relu, scale=wabs[:, b, hh:hh + 1])\
                    .then_inc(idx_act, 1)

            def store(L, dst):
                act.dma_start(dst, zraw[:, L % 2, :]).then_inc(z_out[L % 2], 16)

            act.wait_ge(rope_a, 3 * Z_Q)
            for L in range(Z_Q, Z_GLU):
                s = L % 2
                if L >= Z_Q + 2:
                    act.wait_ge(z_out[s], 16 * ((L - Z_Q) // 2))
                evac(act, zraw[:, s, :], L, 0, ACT.Copy)
                if L < Z_V:
                    act.wait_ge(z_free, 6 + 3 * L + 3)
                    swap(act, s, P)
                if L > Z_Q and L - 1 < Z_V:
                    act.wait_ge(rope_b, 3 * (L - 1 - Z_Q) + 3)
                    n = L - 1 - Z_Q
                    store(L - 1, (q_d if n < 4 else k_d)[:, n % 4, :])
                if L >= Z_V:
                    act.wait_ge(z_free, 6 + 3 * L + 3)
                    store(L, v_d[:, L - Z_V, :])
            act.wait_ge(z_out[0], 16 * 6)
            act.wait_ge(z_out[1], 16 * 6)
            for c in range(4):
                L = Z_GLU + 2 * c
                if c:
                    act.wait_ge(glu, 3 * c)
                evac(act, zraw[:, 1, :], L, 0, ACT.Copy)
                evac(act, zraw[:, 0, :], L + 1, 0, ACT.Sigmoid)
            act.wait_ge(glu, 12)
            with act.Fori(0, KD) as i:
                for k in range(2):
                    L = Z_GATE + k
                    s = L % 2
                    act.wait_ge(z_out[s], 16 * 6 + 16 * i)
                    evac(act, zraw[:, s, :], L, 6 * i, ACT.Sigmoid)
                    act.wait_ge(z_free, 6 + 3 * L + 3 + 6 * i)
                    act.dma_start(gate_d[:, bass.ds(2 * i + k, 1), :].rearrange("p o n -> p (o n)"), zraw[:, s, :])\
                        .then_inc(z_out[s], 16)

        def m1_dve(dve):
            dve.wait_ge(rope_tab, 32)
            for L in range(Z_Q):
                s, n = L % 2, HD if L == 0 else P
                dst = kiw[0:HD, :] if L == 0 else qi[:, L - 1, :]
                dve.wait_ge(swap_in[s], SWAPS[L])
                dve.tensor_tensor(zsw[0:n, s, :], zsw[0:n, s, :], rot[0:n, 1, :], ALU.mult).then_inc(rope_a, 1)
                dve.wait_ge(z_free, 6 + 3 * L + 3)
                dve.tensor_tensor(dst, zraw[0:n, s, :], rot[0:n, 0, :], ALU.mult).then_inc(rope_a, 1)
                dve.wait_ge(rope_a, 3 * L + 2)
                dve.tensor_tensor(dst, dst, zsw[0:n, s, :], ALU.add).then_inc(rope_a, 1)
            dve.wait_ge(kib_in, 16)
            for s in range(2):
                dve.tensor_copy(kis[0:HD, s, PAST:SKEYS], kiw[0:HD, SEQ:TOK]).then_inc(si_prep, 1)
                dve.tensor_copy(kis[HD:P, s, PAST:SKEYS], ki_b[HD:P, SEQ:TOK]).then_inc(si_prep, 1)
            dve.memset(qib[:, :, :, :], 0.0).then_inc(si_prep, 1)
            dve.wait_ge(si_prep, 5)
            dve.wait_ge(rope_a, 3 * Z_Q)
            for c in range(4):
                for p in range(2):
                    r, hh = slice(HD * p, HD * p + HD), 2 * c + p
                    dve.tensor_copy(qib[r, c, :, SNEW * hh:SNEW * (hh + 1)],
                                    qi[r, c, SEQ:TOK].rearrange("p (b s) -> p b s", b=NSEQ)).then_inc(si_prep, 1)
            scale = float(np.float32((H * HD) ** -0.5))
            dve.wait_ge(wr_in, 16)
            dve.scalar_tensor_tensor(wra[:, :], wr[:, :], -1.0, wr[:, :], ALU.mult, ALU.max).then_inc(si_prep, 1)
            dve.tensor_scalar(wrs[:, :], wr[:, :], 0.0, 2.0 * scale, ALU.is_ge, ALU.mult).then_inc(si_prep, 1)
            dve.wait_ge(si_prep, 15)
            dve.tensor_scalar(wrs[:, :], wrs[:, :], scale, None, ALU.subtract).then_inc(si_prep, 1)
            dve.wait_ge(kw_e, 2)
            dve.scalar_tensor_tensor(wabs[:, :, :], kw_tok[:, 0:8, HD:72], -1.0, kw_tok[:, 0:8, HD:72],
                                     ALU.mult, ALU.max)\
                .then_inc(wprep, 1)
            dve.tensor_scalar(wsgn[:, :, :], kw_tok[:, 0:8, HD:72], 0.0, 2.0 * scale, ALU.is_ge, ALU.mult).then_inc(wprep, 1)
            dve.wait_ge(wprep, 5)
            dve.tensor_scalar(wsgn[:, :, :], wsgn[:, :, :], scale, None, ALU.subtract).then_inc(wprep, 1)
            dve.wait_ge(si_prep, 16)
            for half in range(2):
                dve.wait_ge(si_r, half + 1)
                dve.tensor_scalar(rs[:, half, :], rs[:, half, :], wrs[:, half:half + 1], None, ALU.mult)\
                    .then_inc(si_s, 1)
            dve.wait_ge(si_sel, 1)
            dve.tensor_tensor(pick_s[:, :], main[0:NSAMP, 0, 0:SKEYS], ki_b[0:NSAMP, 0:SKEYS], ALU.add)\
                .then_inc(si_sel, 1)
            dve.wait_ge(wprep, 6)
            for n, (b, hh, c0, w) in enumerate(PIECES):
                dst, r = pick[:, off(b) + c0:off(b) + c0 + w], rbuf[:, n % 2, 0:w]
                dve.wait_ge(idx_act, n + 1)
                if hh == 0:
                    dve.tensor_scalar(dst, r, wsgn[:, b, hh:hh + 1], None, ALU.mult).then_inc(idx_dve, 1)
                else:
                    dve.wait_ge(idx_dve, n)
                    dve.scalar_tensor_tensor(dst, r, wsgn[:, b, hh:hh + 1], dst, ALU.mult, ALU.add)\
                        .then_inc(idx_dve, 1)
            dve.wait_ge(idx_dve, len(PIECES))
            for b in range(2, 8):
                d = pick[:, off(b) + P * b:off(b) + P * (b + 1)]
                dve.tensor_tensor(d, d, cst[:, C_CAUSAL:C_CAUSAL + P], ALU.add).then_inc(idx_dve, 1)
            dve.tensor_copy(pick[:, 0:P], cst[:, C_CAUSAL:C_CAUSAL + P]).then_inc(idx_dve, 1)
            dve.memset(pick[:, P:2 * P], 0.0).then_inc(idx_dve, 1)
            dve.tensor_copy(pick[:, 2 * P:3 * P], cst[:, C_CAUSAL:C_CAUSAL + P]).then_inc(idx_dve, 1)
            dve.wait_ge(idx_dve, len(PIECES) + 9)
            dve.wait_ge(si_sel, 2)
            dve.drain().then_inc(tk, 1)
            base = 1

            def round8(scores, n, count):
                dve.wait_ge(tk, count)
                dve.nop(nofuse=True)
                dve.max(top8[0:n, :], scores).then_inc(tk, 1)
                dve.wait_ge(tk, count + 1)
                dve.nop(nofuse=True)

            with dve.Fori(0, TOPK_S // 8) as i:
                round8(pick_s[:, :], NSAMP, base + 2 * i)
                dve.match_replace(pick_s[:, :], top8[0:NSAMP, :], pick_s[:, :], TAKEN).then_inc(tk, 1)
            base += 2 * (TOPK_S // 8)
            round8(pick_s[:, :], NSAMP, base)
            dve.max_index(at8[:, :], top8[0:NSAMP, :], pick_s[:, :]).then_inc(tk, 1)
            dve.wait_ge(tk, base + 2)
            dve.tensor_copy(atf[:, :], at8[:, 0:1]).then_inc(tk, 1)
            dve.wait_ge(tk, base + 3)
            dve.tensor_scalar(one_s[:, :], ki_b[0:NSAMP, SKEYS:2 * SKEYS], atf[:, 0:1], -NEG,
                              ALU.is_equal, ALU.mult).then_inc(tk, 1)
            dve.tensor_scalar(pick_s[:, :], pick_s[:, :], IS_TAKEN, NEG, ALU.is_gt, ALU.mult).then_inc(tk, 1)
            dve.wait_ge(tk, base + 5)
            dve.tensor_tensor(pick_s[:, :], pick_s[:, :], one_s[:, :], ALU.add).then_inc(tk, 1)
            base += 6
            for b in range(2, 8):
                scores = pick[:, off(b):off(b + 1)]
                with dve.Fori(0, TOPK // 8) as i:
                    round8(scores, P, base + 2 * i)
                    dve.match_replace(scores, top8[:, :], scores, TAKEN).then_inc(tk, 1)
                base += 2 * (TOPK // 8)
                dve.wait_ge(tk, base)
                dve.tensor_scalar(scores, scores, IS_TAKEN, NEG, ALU.is_gt, ALU.mult).then_inc(tk, 1)
                base += 1
            dve.wait_ge(uzero, 1)
            base = 1
            dve.drain().then_inc(cv, 1)
            dve.wait_ge(st_e, 2)
            for c in range(4):
                bias = par[:, ROW_BDW + c:ROW_BDW + c + 1]
                yp_, ys_ = conv_y[:, c, 0:SEQ], conv_y[:, c, SEQ:TOK].rearrange("p (b s) -> p b s", b=NSEQ)
                dve.wait_ge(glu, 3 * c + 3)
                dve.tensor_scalar(yp_, uext[:, c, 0:SEQ], taps[:, c, 0:1], bias, ALU.mult, ALU.add).then_inc(cv, 1)
                dve.tensor_scalar(ys_, uext_s[:, c, :, 0:SNEW], taps[:, c, 0:1], bias, ALU.mult, ALU.add)\
                    .then_inc(cv, 1)
                with dve.Fori(1, CW) as k:
                    dve.wait_ge(cv, base + 2 * k - 1)
                    dve.scalar_tensor_tensor(yp_, uext[:, c, bass.ds(k, SEQ)], taps[:, c, bass.ds(k, 1)], yp_,
                                             ALU.mult, ALU.add).then_inc(cv, 1)
                    dve.wait_ge(cv, base + 2 * k)
                    dve.scalar_tensor_tensor(ys_, uext_s[:, c, :, bass.ds(k, SNEW)], taps[:, c, bass.ds(k, 1)], ys_,
                                             ALU.mult, ALU.add).then_inc(cv, 1)
                base += 2 * CW
            CV_END[0] = base

        CV_END = [0]

        qa = place("qa", [P, 4, TOK], F32, NB)
        ka = place("ka", [P, 4, TOK], F32, NB + 16896)
        vtok = place("vtok", [P, 8, ATT], F32, NB + 33792)
        vnew = place("vnew", [NSAMP, ATT], F32, NB + 50176)
        lb = place("lb", [P, 2, SEQ], F32, NB + 52224)
        kts = place("kts", [P, 4, SKEYS], F32, NB + 52224)
        sqc = place("sqc", [P, 4, TC], F32, NB + 52224)
        rstd_c = place("rstd_c", [P, TOK], F32, NB + 60416)
        vraw = place("vraw", [P, 4, TOK], F32, HB + 16896)
        kpg = place("kpg", [P, 2, 2, ATT], F32, HB + 16896)
        vpg = place("vpg", [P, 2, 2, ATT], F32, HB + 25088)
        conv_hi = place("conv_hi", [P, 4, TOK], F32R, HB + 16896)
        conv_lo = place("conv_lo", [P, 4, TOK], F32R, HB)
        o_hi = place("o_hi", [P, 4, TOK], F32R, UB)
        o_lo = place("o_lo", [P, 4, TOK], F32R, UB + 16896)
        pt = place("pt", [P, 2, 8, P], F32, UB + 33792)
        kst = place("kst", [P, 2, ATT], F32, UB + 33792)
        ust = place("ust", [NSAMP, 2, D_CONV], F32, UB + 37888)
        qb = place("qb", [P, 4, NSEQ, 32], F32, UB + 33792)
        pts = place("pts", [P, 2, 3, P], F32, UB + 37888)
        otok = place("otok", [P, ATT], F32, UB + 41984)
        ls = place("ls", [P, 2, SKEYS], F32, UB + 41984)
        mx = place("mx", [P, 2], F32, UB + 44320)
        nb = place("nb", [P, 2], F32, UB + 44352)
        sums = place("sums", [P, 2, H], F32, UB + 44384)
        rinv = place("rinv", [P, 2, H], F32, UB + 44448)
        mixt = place("mixt", [P, 2, 2, TC], F32, UB + 33792)
        gates = place("gates", [P, 2, 2, TOK], F32, RB)

        q_in, k_in, v_in = sem("q_in"), sem("k_in"), sem("v_in")
        kv_t, kv_e = sem("kv_t"), sem("kv_e")
        kst_out = [sem("kst_out0"), sem("kst_out1")]
        u_t, u_e, u_out = sem("u_t"), sem("u_e"), sem("u_out")
        sa_q = sem("sa_q")
        kp_in = [sem("kp_in0"), sem("kp_in1")]
        vp_in = [sem("vp_in0"), sem("vp_in1")]
        kp_t, kp_e, sl_mm = sem("kp_t"), sem("kp_e"), sem("sl_mm")
        ss = sem("ss")
        se = sem("se")
        sp_t, sp_e, so_mm, so_e = sem("sp_t"), sem("sp_e"), sem("so_mm"), sem("so_e")
        ln_y, ln_s = sem("ln_y"), sem("ln_sum")
        qk_mm, at_l, at_nb, at_e = sem("qk_mm"), sem("at_l"), sem("at_nb"), sem("at_e")
        pt_t, pt_e, pv_mm = sem("pt_t"), sem("pt_e"), sem("pv_mm")
        at_r, at_o, ot_mm, o_h, o_l = sem("at_r"), sem("at_o"), sem("ot_mm"), sem("o_h"), sem("o_l")
        g_in = [sem("g_in0"), sem("g_in1")]
        mix_free, mix_a, mix_hi, mix_lo = sem("mix_free"), sem("mix_a"), sem("mix_hi"), sem("mix_lo")
        h_in = [sem("h_in0"), sem("h_in1")]
        out_free, out_s = sem("out_free"), sem("out_s")
        NQ = 8 * H
        PARTS = [(n, p) for n in range(NQ) for p in range(1 + (n // H >= 4))]
        LAST_PART = {n: max(i for i, x in enumerate(PARTS) if x[0] == n) + 1 for n in range(NQ)}
        CV_TOTAL = 1 + 4 * 2 * CW
        TK_SAMPLE = 1 + 2 * (TOPK_S // 8) + 6
        ZDONE = ACC_Z + 3 * NZ
        cond_gate = ada[:, 5 * KD:6 * KD, :]

        def mix_load(m):
            def loads(slot):
                v = slot.rearrange("p (k m) -> p k m", k=KD)
                return [(v[:, 4 * i:4 * i + 4, :], w.rearrange("(k p) m -> p k m", p=P)[:, :, bass.ts(m, P)])
                        for i, w in enumerate((L0["w_conv_out"], L0["w_attn_o"]))]
            return loads

        def m2_sp(sp):
            for m in range(3):
                load_tile(sp, T_MIX + m, (T_MIX + m) % RING, mix_load(m))
            sp.wait_ge(acc_done, ZDONE)
            sp.wait_ge(z_out[0], 16 * 14)
            sp.wait_ge(z_out[1], 16 * 14)
            sp.dma_start(vraw[:, :, :], v_d).then_inc(v_in, 16)
            sp.dma_start(ka[:, :, :], k_d).then_inc(k_in, 16)
            sp.dma_start(qa[:, :, :], q_d).then_inc(q_in, 16)
            sp.dma_start(out[9][0][:, 0:HIST - SNEW, :], L0["state_conv"][:, SNEW:HIST, :]).then_inc(u_out, 16)

            def pages(b, cache, dst, done):
                for pg in range(2):
                    page = sp.value_load(a["page_table"][b:b + 1, pg:pg + 1], min_val=0,
                                         max_val=cache.shape[0] - 1)
                    sp.dma_start(dst[:, pg, :], cache[bass.ds(page, 1)].rearrange("o p h d -> (o p) (h d)"))\
                        .then_inc(done, 16)

            sp.wait_ge(kv_t, 18)
            for b in range(NSEQ):
                if b >= 2:
                    sp.wait_ge(kp_t, 2 * (b - 1))
                pages(b, L0["cache_k"], kpg[:, b % 2], kp_in[b % 2])
            for b in range(NSEQ):
                if b >= 2:
                    sp.wait_ge(so_mm, b - 1)
                pages(b, L0["cache_v"], vpg[:, b % 2], vp_in[b % 2])
            for m in range(3, KD):
                gate_load(sp, m - 3)
                load_tile(sp, T_MIX + m, (T_MIX + m) % RING, mix_load(m))
            for m in range(KD - 3, KD):
                gate_load(sp, m)
                load_tile(sp, T_OUT + m - 5, (T_OUT + m - 5) % RING, cols(L0["w_out"], P * (m - 5)))
            sp.wait_ge(acc_done, ACC_OUT)
            sp.dma_start(h[:, 0:2, :], h_d[:, 0:2, :]).then_inc(h_in[0], 16)
            sp.dma_start(h[:, 2:KD, :], h_d[:, 2:KD, :]).then_inc(h_in[1], 16)
            for m in range(3, KD):
                load_tile(sp, T_OUT + m, (T_OUT + m) % RING, cols(L0["w_out"], P * m))

        def gate_load(sp, m):
            if m < 2:
                sp.wait_ge(pt_t, len(PARTS))
            else:
                sp.wait_ge(mix_free, 3 + 3 * (m - 1))
            for i in range(2):
                sp.dma_start(gates[:, m % 2, i, :], gate_d[:, KD * i + m, :]).then_inc(g_in[m % 2], 16)

        def turn(T):
            return T // RING + len([x for x in range(T_MIX, T_MIX + KD) if x <= T and x % RING == T % RING])

        def m2_pool(pool):
            for m in range(KD):
                T = T_MIX + m
                used = ACC_Z + 3 * (NZ - 3 + m) + 3 if m < 3 else ACC_MIX + 6 * (m - 3) + 6
                split(pool, T, T % RING, turn(T), used)
            for m in range(KD):
                T = T_OUT + m
                used = ACC_MIX + 6 * (KD - 3 + m) + 6 if m < 3 else ACC_OUT + 3 * (m - 3) + 3
                split(pool, T, T % RING, turn(T), used)

        def m2_pe(pe):
            pe.wait_ge(z_free, 6 + 3 * NZ)
            pe.wait_ge(v_in, 16)
            pe.wait_ge(k_in, 16)
            for g in range(18):
                t, src = g // 2, (vraw, ka)[g % 2]
                n = P if t < 8 else NSAMP
                if g >= NBANK:
                    pe.wait_ge(kv_e, g - NBANK + 1)
                for c in range(4):
                    last = pe.transpose(main[0:n, g % NBANK, bass.ts(c, P)], src[:, c, t * P:t * P + n], ident)
                last.then_inc(kv_t, 1)
            pe.wait_ge(glu, 12)
            pe.wait_ge(kv_e, 14)
            for c in range(4):
                last = pe.transpose(main[0:HIST, 0, bass.ts(c, P)], uext[:, c, SEQ:SEQ + HIST], ident)
            last.then_inc(u_t, 1)
            for c in range(4):
                last = pe.transpose(main[0:NSAMP, 1, bass.ts(c, P)], unew[:, c, :], ident)
            last.then_inc(u_t, 1)
            pe.wait_ge(kv_e, 18)
            pe.wait_ge(u_e, 2)
            pe.wait_ge(sa_q, 13)
            pe.wait_ge(tk, TK_SAMPLE)
            for half in range(2):
                pe.matmul(main[:, 4 + half, 0:SKEYS], cst[0:NSAMP, C_SELT + P * half:C_SELT + P * (half + 1)],
                          pick_s[:, :], start=True, stop=False, skip_group_check=True)
            for b in range(NSEQ):
                pe.wait_ge(kp_in[b % 2], 32 * (b // 2 + 1))
                for pg in range(2):
                    if b:
                        pe.wait_ge(kp_e, 2 * (b - 1) + pg + 1)
                    for c in range(4):
                        last = pe.transpose(main[:, pg, bass.ts(c, P)], kpg[:, b % 2, pg, bass.ts(c, P)], ident)
                    last.then_inc(kp_t, 1)
                pe.wait_ge(kp_e, 2 * b + 2)
                for c in range(4):
                    last = pe.matmul(main[32 * (b % 4):32 * (b % 4) + 32, 4 + b // 4, 0:SKEYS], qb[:, c, b, :],
                                     kts[:, c, :], start=False, stop=(c == 3), skip_group_check=True)
                last.then_inc(sl_mm, 1)
            for half in range(2):
                pe.wait_ge(ss, 8 * half + 4)
                if half:
                    pe.wait_ge(sp_e, 2)
                for k in range(3):
                    n = P if k < 2 else NSAMP
                    last = pe.transpose(main[0:n, 2, bass.ts(k, P)], ls[:, half, k * P:k * P + n], ident)
                last.then_inc(sp_t, 1)
            pe.wait_ge(sp_e, 4)
            for b in range(NSEQ):
                pe.wait_ge(vp_in[b % 2], 32 * (b // 2 + 1))
                for c in range(4):
                    col = 32 * (b % 4) + 8 * c
                    o = main[:, 3, 64 * c + 8 * b:64 * c + 8 * b + 8]
                    for k in range(2):
                        pe.matmul(o, vpg[:, b % 2, k, bass.ts(c, P)], pts[:, b // 4, k, col:col + 8],
                                  start=(k == 0), stop=False)
                    last = pe.matmul(o, vnew[:, bass.ts(c, P)], pts[0:NSAMP, b // 4, 2, col:col + 8],
                                     start=False, stop=True)
                last.then_inc(so_mm, 1)
            for t in range(NTC):
                if t == 0:
                    pe.wait_ge(cv, CV_TOTAL)
                for c in range(4):
                    last = pe.matmul(main[:, t, 0:TC], ones[:, :], conv_y[:, c, tcs(t)], start=(c == 0), stop=(c == 3))
                last.then_inc(ln_s, 1)
            for t in range(NTC):
                pe.wait_ge(ln_sem["sq"], t + 1)
                if t == 0:
                    pe.wait_ge(so_e, 4)
                for c in range(4):
                    last = pe.matmul(main[:, 3 + t, 0:TC], ones[:, :], sqc[:, c, :], start=(c == 0), stop=(c == 3))
                last.then_inc(ln_sem["mm"], 1)
            pe.wait_ge(ln_sem["sd"], 3)
            pe.wait_ge(ln_y, 3)

            def logits(n):
                b, hh = n // H, n % H
                lo = HD * (hh % 2)
                if n >= 2:
                    pe.wait_ge(at_l, n - 1)
                for c0 in range(0, P * (b + 1), 512):
                    w = min(512, P * (b + 1) - c0)
                    last = pe.matmul(main[:, 2 * (n % 2) + c0 // 512, 0:w], qa[lo:lo + HD, hh // 2, bass.ts(b, P)],
                                     ka[lo:lo + HD, hh // 2, c0:c0 + w], start=True, stop=True)
                last.then_inc(qk_mm, 1)

            def turn_weights(n):
                b = n // H
                pe.wait_ge(at_e, n + 1)
                for i, (m, part) in enumerate(PARTS):
                    if m != n:
                        continue
                    before = [j for j in range(i) if PARTS[j][1] == part]
                    if before:
                        pe.wait_ge(pt_e, before[-1] + 1)
                    for k in range(4 * part, min(4 * part + 4, b + 1)):
                        last = pe.transpose(main[:, 4 + part, bass.ts(k % 4, P)], lb[:, n % 2, bass.ts(k, P)], ident)
                    last.then_inc(pt_t, 1)

            def values(n):
                b, hh = n // H, n % H
                pe.wait_ge(pt_e, LAST_PART[n])
                if hh == 0 and b:
                    pe.wait_ge(at_o, b)
                for k in range(b + 1):
                    last = pe.matmul(aux[:, 0, bass.ts(hh, HD)], pt[:, n % 2, k, :], vtok[:, k, bass.ts(hh, HD)],
                                     start=(k == 0), stop=(k == b))
                last.then_inc(pv_mm, 1)

            def turn_out(b):
                pe.wait_ge(at_o, b + 1)
                if b:
                    pe.wait_ge(o_l, b)
                for c in range(4):
                    last = pe.transpose(aux[:, 1, bass.ts(c, P)], otok[:, bass.ts(c, P)], ident)
                last.then_inc(ot_mm, 1)

            logits(0)
            for n in range(NQ + 3):
                if n + 1 < NQ:
                    logits(n + 1)
                if n < NQ:
                    turn_weights(n)
                if 1 <= n <= NQ:
                    values(n - 1)
                if n % H == 2 and n > H:
                    turn_out(n // H - 1)

            pe.wait_ge(o_l, 8)
            pe.wait_ge(ln_sem["lo"], 3)
            pe.wait_ge(so_e, 4)

            def mix_tile(T, slot, free):
                pe.wait_ge(split_done, T + 1)
                for t in range(NTC):
                    pe.wait_ge(mix_free, free + t + 1)
                    for i, (xh, xl) in enumerate(((conv_hi, conv_lo), (o_hi, o_lo))):
                        product(pe, main[:, (ACC_MIX + 2 * t + i) % NBANK, 0:TC], slot, range(4),
                                lambda c: xh[:, c, tcs(t)], lambda c: xl[:, c, tcs(t)], 0, c0=4 * i)\
                            .then_inc(acc_done, 1)

            with pe.Fori(0, 2) as i:
                for k in range(3):
                    mix_tile(T_MIX + k + 3 * i, (T_MIX + k) % RING, 3 * k + 9 * i)
            for k in (6, 7):
                mix_tile(T_MIX + k, (T_MIX + k) % RING, 3 * k)
            pe.wait_ge(mix_lo, 2 + 3 * KD)

            def out_tile(T, k, m):
                back = (1, 3, 2)[k]
                pe.wait_ge(split_done, T + 1)
                for t in range(NTC):
                    pe.wait_ge(out_free, 9 + 3 * m - 3 * back + t + 1)
                    product(pe, main[:, 3 * (k % 2) + t, 0:TC], (T_OUT + k) % RING, range(KD),
                            lambda c: nhi[:, c, tcs(t)], lambda c: nlo[:, c, tcs(t)], 0).then_inc(acc_done, 1)

            with pe.Fori(0, 2) as i:
                for k in range(3):
                    out_tile(T_OUT + k + 3 * i, k, k + 3 * i)
            for m in (6, 7):
                out_tile(T_OUT + m, m % 3, m)

        def m2_act(act):
            act.wait_ge(tk, TK_SAMPLE)
            for g in range(18):
                t = g // 2
                n = P if t < 8 else NSAMP
                act.wait_ge(kv_t, g + 1)
                src = main[0:n, g % NBANK, :]
                if g % 2 == 0:
                    dst = vtok[:, t, :] if t < 8 else vnew[:, :]
                    act.activation(dst, src, ACT.Copy).then_inc(kv_e, 1)
                    act.wait_ge(kv_e, g + 1)
                    act.dma_start(out[3][0, 0, t * P:(t + 1) * P].rearrange("t h d -> t (h d)") if t < 8 else
                                  out[7][0].rearrange("b s h d -> (b s) (h d)"), dst).then_inc(v_out, 16)
                else:
                    dst = kst[0:n, t % 2, :]
                    if t >= 2:
                        act.wait_ge(kst_out[t % 2], 16 * (t // 2))
                    act.activation(dst, src, ACT.Copy).then_inc(kv_e, 1)
                    act.wait_ge(kv_e, g + 1)
                    act.dma_start(out[2][0, 0, t * P:(t + 1) * P].rearrange("t h d -> t (h d)") if t < 8 else
                                  out[6][0].rearrange("b s h d -> (b s) (h d)"), dst).then_inc(kst_out[t % 2], 16)
            for i, n in enumerate((HIST, NSAMP)):
                act.wait_ge(u_t, i + 1)
                act.activation(ust[0:n, i, :], main[0:n, i, :], ACT.Copy).then_inc(u_e, 1)
            act.wait_ge(u_e, 2)
            act.dma_start(out[5][0, 0], ust[0:HIST, 0, :]).then_inc(u_out, 16)
            for b in range(NSEQ):
                act.dma_start(out[9][0, b, HIST - SNEW:HIST, :], ust[SNEW * b:SNEW * (b + 1), 1, :])\
                    .then_inc(u_out, 16)
            act.wait_ge(sa_q, 13)
            for b in range(NSEQ):
                for pg in range(2):
                    act.wait_ge(kp_t, 2 * b + pg + 1)
                    if b and pg == 0:
                        act.wait_ge(sl_mm, b)
                    act.activation(kts[:, :, bass.ts(pg, P)], main[:, pg, :].rearrange("p (c n) -> p c n", c=4),
                                   ACT.Copy).then_inc(kp_e, 1)
            for half in range(2):
                act.wait_ge(ss, 8 * half + 2)
                act.activation(ls[:, half, :], main[:, 4 + half, 0:SKEYS], ACT.Exp, bias=nb[:, half:half + 1],
                               scale=HD ** -0.5, accum_out=sums[:, 0, half:half + 1]).then_inc(se, 1)
            act.wait_ge(u_out, 16 * (NSEQ + 2))
            for half in range(2):
                act.wait_ge(sp_t, half + 1)
                act.activation(pts[:, half, 0:2, :], main[:, 2, 0:2 * P].rearrange("p (k n) -> p k n", k=2), ACT.Copy)\
                    .then_inc(sp_e, 1)
                act.activation(pts[0:NSAMP, half, 2, :], main[0:NSAMP, 2, 2 * P:3 * P], ACT.Copy).then_inc(sp_e, 1)
            act.wait_ge(so_mm, NSEQ)
            act.wait_ge(cv, CV_TOTAL)
            for p in range(2):
                r = slice(HD * p, HD * (p + 1))
                act.activation(o_hi[r, :, SEQ:TOK].rearrange("p c (b s) -> p c b s", b=NSEQ),
                               main[r, 3, 0:256].rearrange("p (c b g s) -> p c b g s", c=4, b=NSEQ, g=2)[:, :, :, p, :],
                               ACT.Copy).then_inc(so_e, 1)
            for t in range(NTC):
                act.wait_ge(ln_y, t + 1)
                if t:
                    act.wait_ge(ln_sem["mm"], t)
                act.activation(sqc[:, :, :], conv_y[:, :, tcs(t)], ACT.Square).then_inc(ln_sem["sq"], 1)
                act.wait_ge(ln_sem["mm"], t + 1)
                act.activation(rstd_c[:, tcs(t)], main[:, 3 + t, 0:TC], ACT.Sqrt, scale=1.0 / D_CONV, bias=eps)\
                    .then_inc(ln_sem["sd"], 1)
            for t in range(NTC):
                act.wait_ge(ln_sem["ml"], t + 1)
                for c in range(4):
                    last = act.activation(conv_y[:, c, tcs(t)], conv_y[:, c, tcs(t)], ACT.Silu,
                                          scale=par[:, ROW_LNG + c:ROW_LNG + c + 1],
                                          bias=par[:, ROW_LNB + c:ROW_LNB + c + 1])
                last.then_inc(ln_sem["af"], 1)
                act.wait_ge(ln_sem["af"], t + 1)
                act.activation(conv_hi[:, :, tcs(t)], conv_y[:, :, tcs(t)], ACT.Copy).then_inc(ln_sem["hi"], 1)

            def turned(n):
                for i, (m, part) in enumerate(PARTS):
                    if m != n:
                        continue
                    if part == 0 and n >= 2:
                        act.wait_ge(pv_mm, n - 1)
                    act.wait_ge(pt_t, i + 1)
                    k0, k1 = 4 * part, min(4 * part + 4, n // H + 1)
                    act.activation(pt[:, n % 2, k0:k1, :],
                                   main[:, 4 + part, 0:P * (k1 - k0)].rearrange("p (k n) -> p k n", n=P), ACT.Copy)\
                        .then_inc(pt_e, 1)

            for n in range(NQ + 4):
                if n < NQ:
                    b, hh = n // H, n % H
                    act.wait_ge(at_nb, n + 1)
                    if hh == 0 and b >= 2:
                        act.wait_ge(at_r, b - 1)
                    act.activation(lb[:, n % 2, 0:P * (b + 1)], lb[:, n % 2, 0:P * (b + 1)], ACT.Exp,
                                   bias=nb[:, n % 2:n % 2 + 1], scale=HD ** -0.5,
                                   accum_out=sums[:, b % 2, hh:hh + 1]).then_inc(at_e, 1)
                if 1 <= n <= NQ:
                    turned(n - 1)
                if n % H == 3 and n > H:
                    b = n // H - 1
                    act.wait_ge(ot_mm, b + 1)
                    act.activation(o_hi[:, :, bass.ts(b, P)], aux[:, 1, :].rearrange("p (c n) -> p c n", c=4), ACT.Copy)\
                        .then_inc(o_h, 1)
            with act.Fori(0, KD // 2) as i:
                for k in range(2):
                    for t in range(NTC):
                        act.wait_ge(mix_a, 18 * i + 9 * k + 3 * t + 3)
                        act.activation(nhi[:, bass.ds(2 * i + k, 1), tcs(t)].rearrange("p o n -> p (o n)"),
                                       mixt[:, (3 * k + t) % 2, 0, :], ACT.Copy).then_inc(mix_hi, 1)

        def m2_dve(dve):
            dve.wait_ge(k_in, 16)
            dve.wait_ge(q_in, 16)
            dve.wait_ge(kst_out[0], 16 * 5)
            dve.wait_ge(kst_out[1], 16 * 4)
            dve.memset(qb[:, :, :, :], 0.0).then_inc(sa_q, 1)
            dve.wait_ge(sa_q, 1)
            for c in range(4):
                dve.tensor_copy(kts[:, c, PAST:SKEYS], ka[:, c, SEQ:TOK]).then_inc(sa_q, 1)
                for p in range(2):
                    r, hh = slice(HD * p, HD * p + HD), 2 * c + p
                    dve.tensor_copy(qb[r, c, :, SNEW * hh:SNEW * (hh + 1)],
                                    qa[r, c, SEQ:TOK].rearrange("p (b s) -> p b s", b=NSEQ)).then_inc(sa_q, 1)
            for half in range(2):
                dve.wait_ge(sl_mm, 4 * half + 4)
                dve.reduce_max(mx[:, half:half + 1], main[:, 4 + half, 0:SKEYS], AX_X).then_inc(ss, 1)
                dve.wait_ge(ss, 8 * half + 1)
                dve.tensor_scalar(nb[:, half:half + 1], mx[:, half:half + 1], -HD ** -0.5, None, ALU.mult)\
                    .then_inc(ss, 1)
                dve.wait_ge(se, half + 1)
                dve.reciprocal(rinv[:, 0, half:half + 1], sums[:, 0, half:half + 1]).then_inc(ss, 1)
                dve.wait_ge(ss, 8 * half + 3)
                dve.tensor_scalar(ls[:, half, :], ls[:, half, :], rinv[:, 0, half:half + 1], None, ALU.mult)\
                    .then_inc(ss, 5 if half == 0 else 1)
            dve.wait_ge(so_e, 2)
            for p in range(2):
                r = slice(HD * p, HD * (p + 1))
                dve.tensor_tensor(o_lo[r, :, SEQ:TOK].rearrange("p c (b s) -> p c b s", b=NSEQ),
                                  main[r, 3, 0:256].rearrange("p (c b g s) -> p c b g s", c=4, b=NSEQ, g=2)[:, :, :, p, :],
                                  o_hi[r, :, SEQ:TOK].bitcast(F32).rearrange("p c (b s) -> p c b s", b=NSEQ),
                                  ALU.subtract).then_inc(so_e, 1)
            for t in range(NTC):
                dve.wait_ge(ln_s, t + 1)
                y = conv_y[:, :, tcs(t)]
                dve.scalar_tensor_tensor(y, main[:, t, 0:TC].unsqueeze(1).to_broadcast([P, 4, TC]), -1.0 / D_CONV, y,
                                         ALU.mult, ALU.add).then_inc(ln_y, 1)
            for t in range(NTC):
                dve.wait_ge(ln_sem["sd"], t + 1)
                dve.reciprocal(rstd_c[:, tcs(t)], rstd_c[:, tcs(t)]).then_inc(ln_sem["rs"], 1)
                dve.wait_ge(ln_sem["rs"], t + 1)
                y = conv_y[:, :, tcs(t)]
                dve.tensor_tensor(y, y, rstd_c[:, tcs(t)].unsqueeze(1).to_broadcast([P, 4, TC]), ALU.mult)\
                    .then_inc(ln_sem["ml"], 1)
            for t in range(NTC):
                dve.wait_ge(ln_sem["hi"], t + 1)
                dve.tensor_tensor(conv_lo[:, :, tcs(t)], conv_y[:, :, tcs(t)], conv_hi[:, :, tcs(t)].bitcast(F32),
                                  ALU.subtract).then_inc(ln_sem["lo"], 1)
            for n in range(NQ + 5):
                if n < NQ:
                    b = n // H
                    w = P * (b + 1)
                    dve.wait_ge(qk_mm, n + 1)
                    if n >= 2:
                        dve.wait_ge(pt_t, LAST_PART[n - 2])
                        dve.wait_ge(at_nb, n - 1)
                    dve.tensor_tensor_reduce(lb[:, n % 2, 0:w],
                                             main[:, 2 * (n % 2):2 * (n % 2) + 2, :].rearrange("p a n -> p (a n)")[:, 0:w],
                                             pick[:, off(b):off(b + 1)], 1.0, 3 * NEG, ALU.add, ALU.max,
                                             mx[:, n % 2:n % 2 + 1]).then_inc(at_l, 1)
                    dve.wait_ge(at_l, n + 1)
                    dve.tensor_scalar(nb[:, n % 2:n % 2 + 1], mx[:, n % 2:n % 2 + 1], -HD ** -0.5, None, ALU.mult)\
                        .then_inc(at_nb, 1)
                if n % H == 1 and n > H:
                    b = n // H - 1
                    dve.wait_ge(at_e, H * (b + 1))
                    dve.reciprocal(rinv[:, b % 2, :], sums[:, b % 2, :]).then_inc(at_r, 1)
                    dve.wait_ge(at_r, b + 1)
                    dve.wait_ge(pv_mm, H * (b + 1))
                    if b:
                        dve.wait_ge(ot_mm, b)
                    dve.tensor_tensor(otok[:, :].rearrange("p (h d) -> p h d", h=H),
                                      aux[:, 0, :].rearrange("p (h d) -> p h d", h=H),
                                      rinv[:, b % 2, :].unsqueeze(2).to_broadcast([P, H, HD]), ALU.mult)\
                        .then_inc(at_o, 1)
                if n % H == 4 and n > H:
                    b = n // H - 1
                    dve.wait_ge(o_h, b + 1)
                    dve.tensor_tensor(o_lo[:, :, bass.ts(b, P)], aux[:, 1, :].rearrange("p (c n) -> p c n", c=4),
                                      o_hi[:, :, bass.ts(b, P)].bitcast(F32), ALU.subtract).then_inc(o_l, 1)
            dve.wait_ge(o_l, 8)
            dve.drain().then_inc(mix_free, 3)
            dve.drain().then_inc(mix_lo, 2)
            with dve.Fori(0, KD // 2) as i:
                for k in range(2):
                    dve.wait_ge(g_in[k], 32 * i + 32)
                    for t in range(NTC):
                        s = (3 * k + t) % 2
                        x, y = mixt[:, s, 0, :], mixt[:, s, 1, :]
                        at = 18 * i + 9 * k + 3 * t
                        dve.wait_ge(acc_done, ACC_MIX + 12 * i + 6 * k + 2 * t + 2)
                        dve.wait_ge(mix_lo, 6 * i + 3 * k + t + 1)
                        dve.tensor_tensor(x, main[:, (ACC_MIX + 2 * t) % NBANK, 0:TC], gates[:, k, 0, tcs(t)], ALU.mult)\
                            .then_inc(mix_a, 1)
                        dve.tensor_tensor(y, main[:, (ACC_MIX + 2 * t + 1) % NBANK, 0:TC], gates[:, k, 1, tcs(t)],
                                          ALU.mult).then_inc(mix_free, 1)
                        dve.wait_ge(mix_free, 3 + 6 * i + 3 * k + t + 1)
                        dve.wait_ge(mix_a, at + 1)
                        dve.tensor_tensor(x, x, y, ALU.add).then_inc(mix_a, 2)
                        dve.wait_ge(mix_hi, 6 * i + 3 * k + t + 1)
                        m = 2 * i + k
                        dve.tensor_tensor(nlo[:, bass.ds(m, 1), tcs(t)].rearrange("p o n -> p (o n)"), x,
                                          nhi[:, bass.ds(m, 1), tcs(t)].bitcast(F32).rearrange("p o n -> p (o n)"),
                                          ALU.subtract).then_inc(mix_lo, 1)
            dve.drain().then_inc(out_free, 9)

            def out_tile(k, m, at):
                for t in range(NTC):
                    n = TC if t < 2 else PLAST
                    bank = main[:, 3 * (k % 2) + t, :]
                    dve.wait_ge(acc_done, ACC_OUT + at + t + 1)
                    hm = h[:, bass.ds(m, 1), :].rearrange("p o n -> p (o n)")
                    gm = cond_gate[:, bass.ds(m, 1), :].rearrange("p o n -> p (o n)")
                    sm = small2[:, bass.ds(m, 1), :].rearrange("p o n -> p (o n)")
                    if t == 2:
                        dve.tensor_tensor(sm.rearrange("p (b s) -> p b s", b=NSEQ),
                                          bank[:, PLAST:TC].rearrange("p (b s) -> p b s", b=NSEQ),
                                          gm[:, 1:NCOND].unsqueeze(2).to_broadcast([P, NSEQ, SNEW]), ALU.mult)\
                            .then_inc(out_s, 1)
                        dve.wait_ge(out_s, m + 1)
                        dve.tensor_tensor(hm[:, SEQ:TOK], hm[:, SEQ:TOK], sm, ALU.add)
                    dve.scalar_tensor_tensor(hm[:, t * TC:t * TC + n], bank[:, 0:n], gm[:, 0:1],
                                             hm[:, t * TC:t * TC + n], ALU.mult, ALU.add).then_inc(out_free, 1)

            dve.wait_ge(h_in[0], 16)
            dve.wait_ge(h_in[1], 16)
            with dve.Fori(0, 2) as i:
                for k in range(3):
                    out_tile(k, k + 3 * i, 3 * k + 9 * i)
            for m in (6, 7):
                out_tile(m % 3, m, 3 * m)
            dve.wait_ge(out_free, 9 + 3 * KD)

        small2 = place("small2", [P, KD, NSAMP], F32, UB + 41984)

        ytok = place("ytok", [P, 3, D], F32, NB)
        SEGS = [(0, 128), (128, 128), (256, 96)]
        yp, ys = out[0][0], out[1].rearrange("b s d -> (b s) d")

        def final_pe(pe, t):
            norm_wait(pe, "f", "af", 2 * t + 2)
            for g, (o, n) in enumerate(SEGS):
                for half in range(2):
                    if t:
                        pe.wait_ge((fin_act, fin_dve)[half], 3 * (t - 1) + g + 1)
                    for c in range(4):
                        last = pe.transpose(main[0:n, 2 * g + half, bass.ts(c, P)],
                                            tmp[:, 4 * half + c, o:o + n], ident)
                    last.then_inc(fin_t, 1)

        def final_act(act, t):
            for g, (o, n) in enumerate(SEGS):
                act.wait_ge(fin_t, 6 * t + 2 * g + 1)
                if t:
                    act.wait_ge(y_out[g], 16 * t)
                act.activation(ytok[0:n, g, 0:512], main[0:n, 2 * g, :], ACT.Copy).then_inc(fin_act, 1)

        def final_dve(dve, t):
            for g, (o, n) in enumerate(SEGS):
                dve.wait_ge(fin_t, 6 * t + 2 * g + 2)
                if t:
                    dve.wait_ge(y_out[g], 16 * t)
                dve.tensor_copy(ytok[0:n, g, 512:D], main[0:n, 2 * g + 1, :]).then_inc(fin_dve, 1)

        def final_sp(sp):
            for t in range(NTC):
                for g, (o, n) in enumerate(SEGS):
                    sp.wait_ge(fin_act, 3 * t + g + 1)
                    sp.wait_ge(fin_dve, 3 * t + g + 1)
                    tok = t * TC + o
                    n = min(n, SEQ - tok)
                    sp.dma_start(yp[tok:tok + n, :], ytok[0:n, g, :]).then_inc(y_out[g], 16)
                    if tok + n == SEQ:
                        sp.dma_start(ys, ytok[n:n + NSAMP, g, :]).then_inc(y_out[g], 16)
            for g in range(3):
                sp.wait_ge(y_out[g], 16 * (3 + (g == 2)))
            sp.wait_ge(v_out, 16 * 9)

        norm1, norm3, norm_f = norm("1", 0), norm("2", 2), norm("f", None, final_act, final_dve, final_pe)
        ffn1 = ffn("1", T_FFN1, ACC_FFN1, L0["w1_gate"], L0["w1_up"], L0["w1_down"], 0, norm1, True)
        ffn2 = ffn("2", T_FFN2, ACC_FFN2, L0["w2_gate"], L0["w2_up"], L0["w2_down"], 2, norm3, False)

        block = ctx.enter_context(nc.Block())

        @block.sync
        def _(sp):
            sp_init(sp)
            for g in range(INIT_ADA // 4):
                ada_load(sp, g, g % 2, g // 2 + 1)
            ffn1["sp"](sp)
            m1_sp(sp)
            m2_sp(sp)
            ffn2["sp"](sp)
            final_sp(sp)

        @block.gpsimd
        def _(pool):
            pool.drain().then_inc(split_done, RING)
            ffn1["pool"](pool)
            m1_pool(pool)
            m2_pool(pool)
            ffn2["pool"](pool)

        @block.tensor
        def _(pe):
            pe.drain().then_inc(acc_done, FFN_ACC)
            pe.drain().then_inc(ada_mm, 2)
            pe_init(pe)
            for g in range(INIT_ADA // 4):
                pe_ada(pe, g, g % 2, g // 2 + 1)
            norm1["pe"](pe)
            ffn1["pe"](pe)
            norm_m["pe"](pe)
            m1_pe(pe)
            m2_pe(pe)
            norm3["pe"](pe)
            ffn2["pe"](pe)
            norm_f["pe"](pe)

        @block.scalar
        def _(act):
            act_init(act)
            act.wait_ge(init_e, NINIT)
            act.wait_ge(consts_in, 16)
            act.wait_ge(mod_set, 1)
            norm1["act"](act)
            ffn1["act"](act)
            ffn_wait(act, "1", "down_free", 24 * NPAIR + 24)
            act.wait_ge(mod_set, 5)
            norm_m["act"](act)
            m1_act(act)
            m2_act(act)
            act.wait_ge(out_free, 9 + 3 * KD)
            norm3["act"](act)
            ffn2["act"](act)
            ffn_wait(act, "2", "down_free", 24 * NPAIR + 24)
            norm_f["act"](act)

        @block.vector
        def _(dve):
            dve.drain().then_inc(ada_out, 1)
            dve_init(dve)
            dve.wait_ge(init_e, NINIT)
            for g in range(INIT_ADA // 4):
                dve_ada(dve, g)
            dve_mod(dve, 0, ROW_G1, INIT_ADA // 4)
            dve.wait_ge(mod_set, 1)
            dve_half_gate(dve, 0)
            dve.wait_ge(mod_set, 2)
            norm1["dve"](dve)
            ffn1["dve"](dve)
            ffn_wait(dve, "1", "down_free", 24 * NPAIR + 24)
            dve_mod(dve, 1, ROW_GM, ADA_TILES // 4)
            dve_mod(dve, 2, ROW_G2, ADA_TILES // 4)
            dve_half_gate(dve, 2)
            dve.wait_ge(mod_set, 5)
            norm_m["dve"](dve)
            m1_dve(dve)
            m2_dve(dve)
            norm3["dve"](dve)
            ffn2["dve"](dve)
            ffn_wait(dve, "2", "down_free", 24 * NPAIR + 24)
            norm_f["dve"](dve)


_INS = ["x_prompt", "x_sample", "cache_k", "cache_v", "cache_idx_k", "state_conv", "page_table", "c_prompt",
        "c_sample", "w_ada", "b_ada", "g_ffn1", "w1_gate", "w1_up", "w1_down", "g_mix", "w_in", "w_dw", "b_dw",
        "ln_g", "ln_b", "w_conv_out", "w_attn_o", "w_out", "g_ffn2", "w2_gate", "w2_up", "w2_down", "g_final"]
_OUTS = [(1, SEQ, D), (NSEQ, SNEW, D), (1, 1, SEQ, H, HD), (1, 1, SEQ, H, HD), (1, 1, SEQ, HD),
         (1, 1, HIST, D_CONV), (1, NSEQ, SNEW, H, HD), (1, NSEQ, SNEW, H, HD), (1, NSEQ, SNEW, HD),
         (1, NSEQ, HIST, D_CONV)]


def kernel(**inputs):
    import concourse.bacc as bacc
    from concourse.bass_utils import run_bass_kernel_spmd

    nc = bacc.Bacc("TRN2", target_bir_lowering=False, num_devices=1)
    arrays = {f"in_{name}": np.ascontiguousarray(inputs[name]) for name in _INS}
    arrays["in_consts"], arrays["in_rope"] = constants()
    ins = {n: nc.dram_tensor(n, a.shape, mybir.dt.from_np(a.dtype), kind="ExternalInput").ap()
           for n, a in arrays.items()}
    outs = [nc.dram_tensor(f"out_{i}", shape, F32, kind="ExternalOutput").ap() for i, shape in enumerate(_OUTS)]
    build(nc, {n: ins[f"in_{n}"] for n in _INS}, outs, ins["in_consts"], ins["in_rope"])
    r = run_bass_kernel_spmd(nc, [arrays], core_ids=[0])
    return tuple(r.results[0][f"out_{i}"] for i in range(len(_OUTS)))
```

```python
from contextlib import ExitStack

import numpy as np
import concourse.bass as bass
from concourse import mybir

ALU = mybir.AluOpType
ACT = mybir.ActivationFunctionType
AX_X = mybir.AxisListType.X
F32 = mybir.dt.float32
F32R = mybir.dt.float32r
U32 = mybir.dt.uint32
I32 = mybir.dt.int32

P = 128
D = 1024
KD = D // P
SEQ = 1024
NSEQ = 8
SNEW = 4
NSAMP = NSEQ * SNEW
TOK = SEQ + NSAMP
TC = TOK // 3
NTC = 3
PLAST = SEQ - 2 * TC
NCOND = 1 + NSEQ
NMOD = 9
D_FF = 2816
NPAIR = D_FF // (2 * P)
H = 8
HD = 64
ATT = H * HD
D_CONV = 512
CW = 31
HIST = CW - 1
TOPK = 256
PAST = 256
TOPK_S = (PAST + SNEW) // 4
N_IN = 5192
EPS = 1e-6
NEG = -1e30
TAKEN = -3e38
IS_TAKEN = -2e38
INIT_ADA = 28
ADA_TILES = NMOD * KD
ADA_NORM1 = 4

RING = 3
NBANK = 6
FFN_ACC = 36
FFN_ENDS = (5, 6, 9, 12, 24, 36)
T_FFN1 = RING
T_Z = T_FFN1 + 6 * NPAIR
NZ = 41
T_MIX = T_Z + NZ
T_OUT = T_MIX + KD
T_FFN2 = T_OUT + KD
ACC_FFN1 = FFN_ACC
ACC_Z = ACC_FFN1 + FFN_ACC * NPAIR
ACC_MIX = ACC_Z + 3 * NZ
ACC_OUT = ACC_MIX + 6 * KD
ACC_FFN2 = ACC_OUT + 3 * KD
ACC_END = ACC_FFN2 + FFN_ACC * NPAIR

ROW_BADA, ROW_G1, ROW_GM, ROW_G2, ROW_GF, ROW_LNG, ROW_LNB, ROW_BDW = 0, 72, 80, 88, 96, 104, 108, 112
NROWS = 116

C_ID, C_CAUSAL, C_SEL, C_SELT, C_EPS, C_HEAD = 0, 128, 256, 320, 576, 578
NCONST = C_HEAD + H
SKEYS = PAST + NSAMP
C_SMASK, C_IOTA = NCONST, NCONST + SKEYS


def constants():
    c = np.zeros((P, C_IOTA + SKEYS), np.float32)
    c[:, C_ID:C_ID + P] = np.eye(P)
    q, k = np.arange(P)[:, None], np.arange(P)[None]
    c[:, C_CAUSAL:C_CAUSAL + P] = np.where(k <= q, 0.0, NEG)
    row = np.arange(NSAMP)
    new = np.arange(NSAMP)
    ok = (new[None] // SNEW == row[:, None] // SNEW) & (new[None] % SNEW <= row[:, None] % SNEW)
    c[:NSAMP, C_SMASK + PAST:C_SMASK + SKEYS] = np.where(ok, 0.0, NEG)
    for half in range(2):
        for p in range(P):
            to = (half * 4 + p // 32) * SNEW + p % SNEW
            c[p, C_SEL + 32 * half + to] = 1.0
            c[to, C_SELT + P * half + p] = 1.0
    c[:, C_EPS] = EPS
    c[:, C_HEAD:C_HEAD + H] = (np.arange(P)[:, None] % 32) // SNEW == np.arange(H)[None]
    c[:, C_IOTA:] = np.arange(SKEYS)
    pos = np.concatenate([np.arange(SEQ), np.tile(PAST + np.arange(SNEW), NSEQ)]).astype(np.float32)
    inv = np.float32(10000.0) ** (-np.arange(0, HD, 2, dtype=np.float32) / np.float32(HD))
    ang = (pos[None] * inv[:, None].astype(np.float32)).astype(np.float32)
    cos, sin = np.cos(ang), np.sin(ang)
    rope = np.stack([np.concatenate([cos] * 4), np.concatenate([-sin, sin] * 2)], 1)
    return c, np.ascontiguousarray(rope, np.float32)


def build(nc, a, out, consts, rope):
    no_layer = ("x_prompt", "x_sample", "page_table", "c_prompt", "c_sample", "g_final")
    L0 = {n: t[0] for n, t in a.items() if n not in no_layer}
    with ExitStack() as ctx:
        def sem(name):
            return ctx.enter_context(nc.semaphore(name))

        at = [16640]

        def place(name, shape, dt, offset=None):
            size = 4
            for s in shape[1:]:
                size *= s
            if offset is None:
                offset = at[0]
                at[0] += (size + 31) // 32 * 32
            assert offset + size <= 229368, (name, offset + size)
            return nc.alloc_sbuf_tensor_at(name, list(shape), dt, offset=offset)

        cst = place("cst", [P, NCONST], F32)
        ident = cst[:, C_ID:C_ID + P]
        eps = cst[:, C_EPS:C_EPS + 1]
        ones = place("ones", [P, P], F32)
        par = place("par", [P, NROWS], F32)
        taps = place("taps", [P, 4, CW], F32)
        ada = place("ada", [P, ADA_TILES, NCOND], F32)
        mod_a = place("mod_a", [P, 3, KD, NCOND], F32)
        ccol = place("ccol", [P, KD, NCOND], F32)
        raw = place("raw", [P, RING, 8 * P], F32)
        whi = place("whi", [P, RING, 8 * P], F32R)
        wlo = place("wlo", [P, RING, 8 * P], F32R)
        HB = at[0]
        assert HB + (3 * KD + 4) * TOK * 4 + 11264 + 32768 <= 229368
        NB = HB + KD * TOK * 4
        RB = NB + 2 * KD * TOK * 4
        h = place("h", [P, KD, TOK], F32, HB)
        nhi = place("nhi", [P, KD, TOK], F32R, NB)
        nlo = place("nlo", [P, KD, TOK], F32R, NB + KD * TOK * 4)
        hid_hi = place("hid_hi", [P, 2, TOK], F32R, RB)
        hid_lo = place("hid_lo", [P, 2, TOK], F32R, RB + 2 * TOK * 4)
        sq = place("sq", [P, KD, TC], F32, RB)
        rstd = place("rstd", [P, TOK], F32, RB + 16896)
        small = place("small", [P, KD, NSAMP], F32, RB + 16896)
        tmp = place("tmp", [P, 8, TC], F32, RB + 16896 + 4224)
        ada_rows = [place("ada_row", [NCOND, 4 * P], F32, RB + 8 * TC * 4),
                    place("ada_row_f", [NCOND, 4 * P], F32, RB + 16896 + 4224 + 6 * TC * 4)]
        ada_raw = place("ada_raw", [P, 2, KD, 4 * P], F32, RB + 16896 + 4224 + 11264)
        ada_hi = place("ada_hi", [P, KD, 4 * P], F32R, RB + 16896 + 4224 + 11264)
        ada_lo = place("ada_lo", [P, KD, 4 * P], F32R, RB + 16896 + 4224 + 11264 + 16384)
        assert at[0] == HB
        at[0] = RB + 16896 + 4224 + 11264 + 32768
        ccol_hi = place("ccol_hi", [P, KD, NCOND], F32R)
        ccol_lo = place("ccol_lo", [P, KD, NCOND], F32R)
        xtok = place("xtok", [P, 9, D], F32, NB)
        prow = place("prow", [NROWS, P], F32, NB + 9 * D * 4)
        wrow = place("wrow", [CW, D_CONV], F32, NB + 9 * D * 4 + 512)
        crow = place("crow", [NCOND, D], F32, NB + 9 * D * 4 + 512 + 2048)
        csil = place("csil", [NCOND, D], F32, NB + 9 * D * 4 + 512 + 2048 + 4096)

        main = ctx.enter_context(nc.psum_tensor("main", [P, NBANK, 512], F32))
        aux = ctx.enter_context(nc.psum_tensor("aux", [P, 2, 512], F32))

        raw_ready = [sem(f"raw_ready{s}") for s in range(RING)]
        hi_done = sem("hi_done")
        split_done = sem("split_done")
        acc_done = sem("acc_done")
        consts_in = sem("consts_in")
        rows_in = sem("rows_in")
        x_in = [sem(f"x_in{t}") for t in range(3)]
        ones_set = sem("ones_set")
        csil_done = sem("csil_done")
        init_t = sem("init_t")
        init_e = sem("init_e")
        ada_in = [sem("ada_in0"), sem("ada_in1")]
        ada_mm = sem("ada_mm")
        c_split = sem("c_split")
        ada_s = sem("ada_s")
        ada_l = sem("ada_l")
        ada_copy = sem("ada_copy")
        ada_t = sem("ada_t")
        ada_out = sem("ada_out")
        mod_set = sem("mod_set")
        ki_out, v_out = sem("ki_out"), sem("v_out")
        y_out = [sem(f"y_out{g}") for g in range(3)]
        fin_t = sem("fin_t")
        fin_act = sem("fin_act")
        fin_dve = sem("fin_dve")
        NORM_STEPS = {"sq": 6, "mm": 3, "sd": 3, "rs": 3, "ml": 6, "af": 6, "hi": 6, "lo": 6, "fix": 6}
        norm_sem = {k: sem(f"norm_{k}") for k in NORM_STEPS}
        ln_sem = {k: sem(f"ln_{k}") for k in ("sq", "mm", "sd", "rs", "ml", "af", "hi", "lo")}
        FFN_STEPS = {"gate_free": 3 + 6 * NPAIR, "up_free": 3 + 6 * NPAIR, "down_free": 24 + 24 * NPAIR,
                     "hid_hi": 6 * NPAIR, "hid_lo": 6 * NPAIR, "samp": 8 * NPAIR}
        ffn_sem = {k: sem(f"ffn_{k}") for k in FFN_STEPS}

        def norm_wait(eng, q, k, count):
            eng.wait_ge(norm_sem[k], "1m2f".index(q) * NORM_STEPS[k] + count)

        def ffn_wait(eng, q, k, count):
            eng.wait_ge(ffn_sem[k], "12".index(q) * FFN_STEPS[k] + count)

        def load_tile(sp, T, slot, loads):
            sp.wait_ge(split_done, T - RING + 1)
            for dst, src in loads(raw[:, slot]):
                sp.dma_start(dst, src).then_inc(raw_ready[slot], 16)

        def cols(w, c0, n=P):
            return lambda slot: [(slot.rearrange("p (k m) -> p k m", k=KD)[:, :, 0:n],
                                  w.rearrange("(k p) m -> p k m", p=P)[:, :, c0:c0 + n])]

        def split(pool, T, slot, turn, used):
            pool.wait_ge(raw_ready[slot], turn * 16)
            pool.wait_ge(acc_done, used)
            pool.nop(nofuse=True)
            pool.tensor_copy(whi[:, slot], raw[:, slot]).then_inc(hi_done, 1)
            pool.wait_ge(hi_done, T - RING + 1)
            pool.tensor_tensor(wlo[:, slot], raw[:, slot], whi[:, slot].bitcast(F32), ALU.subtract)\
                .then_inc(split_done, 1)

        def product(pe, bank, slot, chunks, hi, lo, m0, m=P, mstride=P, c0=0):
            n = len(chunks)
            for i, c in enumerate(chunks):
                w = slice(mstride * (c0 + i) + m0, mstride * (c0 + i) + m0 + m)
                pe.matmul(bank, whi[:, slot, w], hi(c), start=(i == 0), stop=False)
                pe.matmul(bank, whi[:, slot, w], lo(c), start=False, stop=False)
                last = pe.matmul(bank, wlo[:, slot, w], hi(c), start=False, stop=(i == n - 1))
            return last

        def tcs(t):
            return slice(t * TC, (t + 1) * TC)

        def sp_init(sp):
            sp.dma_start(cst[:, :], consts[:, 0:NCONST]).then_inc(consts_in, 16)
            rows = [(ROW_BADA, L0["b_ada"], 72), (ROW_G1, L0["g_ffn1"], 8), (ROW_GM, L0["g_mix"], 8),
                    (ROW_G2, L0["g_ffn2"], 8), (ROW_GF, a["g_final"], 8), (ROW_LNG, L0["ln_g"], 4),
                    (ROW_LNB, L0["ln_b"], 4), (ROW_BDW, L0["b_dw"], 4)]
            sp.dma_start(crow[0:1, :], a["c_prompt"]).then_inc(rows_in, 16)
            sp.dma_start(crow[1:NCOND, :], a["c_sample"]).then_inc(rows_in, 16)
            for r, src, n in rows:
                sp.dma_start(prow[r:r + n, :], src.rearrange("(r p) -> r p", p=P)).then_inc(rows_in, 16)
            sp.dma_start(wrow[:, :], L0["w_dw"]).then_inc(rows_in, 16)
            xp = a["x_prompt"][0].rearrange("(t p) d -> p t d", p=P)
            sp.dma_start(xtok[:, 0:4, :], xp[:, 0:4, :]).then_inc(x_in[0], 16)
            sp.dma_start(xtok[:, 4:8, :], xp[:, 4:8, :]).then_inc(x_in[1], 16)
            sp.dma_start(xtok[0:NSAMP, 8, :], a["x_sample"].rearrange("b s d -> (b s) d")).then_inc(x_in[2], 16)

        def ada_load(sp, g, slot, turn):
            sp.wait_ge(ada_mm, g + 1)
            sp.dma_start(ada_raw[:, slot], L0["w_ada"].rearrange("(k p) m -> p k m", p=P)
                         [:, :, bass.ts(g, 4 * P)]).then_inc(ada_in[slot], 16)

        NINIT = 1 + 1 + 1 + 18

        def pe_init(pe):
            pe.wait_ge(consts_in, 16)
            pe.wait_ge(rows_in, 11 * 16)
            pe.transpose(main[:, 0, 0:NROWS], prow[:, :], ident[0:NROWS, 0:NROWS]).then_inc(init_t, 1)
            for c in range(4):
                last = pe.transpose(main[:, 1, CW * c:CW * (c + 1)], wrow[:, bass.ts(c, P)], ident[0:CW, 0:CW])
            last.then_inc(init_t, 1)
            pe.wait_ge(csil_done, 1)
            for c in range(KD):
                last = pe.transpose(main[:, 2, NCOND * c:NCOND * (c + 1)], csil[:, bass.ts(c, P)],
                                    ident[0:NCOND, 0:NCOND])
            last.then_inc(init_t, 1)
            for t in range(9):
                n = P if t < 8 else NSAMP
                if t % 4 == 0:
                    pe.wait_ge(x_in[t // 4], 16)
                for half in range(2):
                    g = 3 + 2 * t + half
                    if g >= NBANK:
                        pe.wait_ge(init_e, g - NBANK + 1)
                    for c in range(4):
                        last = pe.transpose(main[:, g % NBANK, c * P:c * P + n],
                                            xtok[0:n, t, bass.ts(4 * half + c, P)], ident[0:n, 0:n])
                    last.then_inc(init_t, 1)

        def act_init(act):
            act.wait_ge(rows_in, 11 * 16)
            act.activation(csil[:, :], crow[:, :], ACT.Silu).then_inc(csil_done, 1)

        def dve_init(dve):
            dve.memset(ones[:, :], 1.0).then_inc(ones_set, 1)
            dve.wait_ge(init_t, 1)
            dve.tensor_copy(par[:, :], main[:, 0, 0:NROWS]).then_inc(init_e, 1)
            dve.wait_ge(init_t, 2)
            dve.tensor_copy(taps[:, :, :], main[:, 1, 0:4 * CW].rearrange("p (c k) -> p c k", c=4)).then_inc(init_e, 1)
            dve.wait_ge(init_t, 3)
            dve.tensor_copy(ccol[:, :, :], main[:, 2, 0:KD * NCOND].rearrange("p (c k) -> p c k", c=KD))\
                .then_inc(init_e, 1)
            dve.wait_ge(init_e, 3)
            dve.tensor_copy(ccol_hi[:, :, :], ccol[:, :, :]).then_inc(c_split, 1)
            dve.wait_ge(c_split, 1)
            dve.tensor_tensor(ccol_lo[:, :, :], ccol[:, :, :], ccol_hi[:, :, :].bitcast(F32), ALU.subtract)\
                .then_inc(c_split, 1)
            for g in range(3, NINIT):
                t, half = (g - 3) // 2, (g - 3) % 2
                n = P if t < 8 else NSAMP
                dve.wait_ge(init_t, g + 1)
                dve.tensor_copy(h[:, 4 * half:4 * half + 4, t * P:t * P + n],
                                main[:, g % NBANK, :].rearrange("p (c n) -> p c n", c=4)[:, :, 0:n]).then_inc(init_e, 1)

        def pe_ada(pe, g, slot, turn, bank):
            pe.wait_ge(ada_in[slot], 16 * turn)
            pe.wait_ge(ada_copy, g + 1)
            for k in range(KD):
                last = pe.matmul(bank[0:NCOND, :], ccol[:, k, :], ada_raw[:, slot, k, :],
                                 start=(k == 0), stop=(k == KD - 1))
            last.then_inc(ada_mm, 1)

        def pe_ada_split(pe, g, bank):
            pe.wait_ge(ada_copy, g + 1)
            pe.wait_ge(ada_l, 4 * (g - INIT_ADA // 4) + 4)
            for k in range(KD):
                pe.matmul(bank[0:NCOND, :], ccol_hi[:, k, :], ada_hi[:, k, :], start=(k == 0), stop=False)
                pe.matmul(bank[0:NCOND, :], ccol_lo[:, k, :], ada_hi[:, k, :], start=False, stop=False)
                last = pe.matmul(bank[0:NCOND, :], ccol_hi[:, k, :], ada_lo[:, k, :], start=False, stop=(k == KD - 1))
            last.then_inc(ada_mm, 1)

        def act_ada_hi(act, g, i):
            if i == 0:
                act.wait_ge(ada_in[1], 16 * (INIT_ADA // 8 + 1 + g - INIT_ADA // 4))
                act.wait_ge(ada_mm, g + 2)
            act.activation(ada_hi[:, 2 * i:2 * i + 2, :], ada_raw[:, 1, 2 * i:2 * i + 2, :], ACT.Copy).then_inc(ada_s, 1)

        def dve_ada_lo(dve, g, i):
            dve.wait_ge(ada_s, 4 * (g - INIT_ADA // 4) + i + 1)
            dve.tensor_tensor(ada_lo[:, 2 * i:2 * i + 2, :], ada_raw[:, 1, 2 * i:2 * i + 2, :],
                              ada_hi[:, 2 * i:2 * i + 2, :].bitcast(F32), ALU.subtract).then_inc(ada_l, 1)

        def act_ada(act, g, bank, row):
            act.wait_ge(ada_mm, g + 3)
            act.wait_ge(ada_t, g + 1)
            act.activation(row[:, :], bank[0:NCOND, :], ACT.Copy).then_inc(ada_copy, 1)

        def pe_ada_turn(pe, g, bank, row):
            pe.wait_ge(ada_copy, g + 2)
            pe.wait_ge(ada_out, g + 1)
            pe.nop(nofuse=True)
            for t in range(4):
                last = pe.transpose(bank[:, NCOND * t:NCOND * (t + 1)], row[:, bass.ts(t, P)],
                                    ident[0:NCOND, 0:NCOND])
            last.then_inc(ada_t, 1)

        def dve_ada(dve, g, bank):
            dve.wait_ge(ada_t, g + 2)
            dve.tensor_tensor(ada[:, bass.ts(g, 4), :], bank[:, 0:4 * NCOND].rearrange("p (t n) -> p t n", t=4),
                              par[:, bass.ts(g, 4)].unsqueeze(2).to_broadcast([P, 4, NCOND]), ALU.add)\
                .then_inc(ada_out, 1)

        def dve_mod(dve, i, grow, count):
            dve.wait_ge(ada_out, count + 1)
            s0 = (3 * i + 1) * KD
            dve.scalar_tensor_tensor(mod_a[:, i], ada[:, s0:s0 + KD, :], 1.0,
                                     par[:, grow:grow + KD].unsqueeze(2).to_broadcast([P, KD, NCOND]),
                                     ALU.add, ALU.mult).then_inc(mod_set, 1)

        def dve_half_gate(dve, i):
            g0 = (3 * i + 2) * KD
            dve.tensor_scalar(ada[:, g0:g0 + KD, :], ada[:, g0:g0 + KD, :], 0.5, None, ALU.mult).then_inc(mod_set, 1)

        def by_seq(ap):
            return ap.rearrange("p c (b s) -> p c b s", b=NSEQ)

        def cond(ap, c0, n):
            return ap[:, c0:c0 + n, 1:NCOND].unsqueeze(3).to_broadcast([P, n, NSEQ, SNEW])

        def norm(q, i, after_act=None, after_dve=None, after_pe=None, beside=None):
            s = norm_sem
            a_of = None if i is None else mod_a[:, i]
            b_of = None if i is None else ada[:, 3 * i * KD:(3 * i + 1) * KD, :]

            def pe(pe, ts=range(NTC)):
                pe.wait_ge(ones_set, 1)
                for t in ts:
                    norm_wait(pe, q, "sq", 2 * t + 2)
                    if t == 2:
                        norm_wait(pe, q, "sd", 1)
                    for c in range(KD):
                        last = pe.matmul(aux[:, t % 2, 0:TC], ones[:, :], sq[:, c, :], start=(c == 0), stop=(c == KD - 1))
                    last.then_inc(s["mm"], 1)
                    if after_pe and t:
                        after_pe(pe, t - 1)
                    if beside:
                        beside["pe"](pe, t)
                if after_pe:
                    after_pe(pe, NTC - 1)

            def pe_start(pe):
                pe_sums(pe, range(NTC - 1))

            def pe_last(pe):
                pe_sums(pe, range(NTC - 1, NTC))

            def act(act):
                def square(t):
                    if t:
                        norm_wait(act, q, "mm", t)
                    act.activation(sq[:, 0:4, :], h[:, 0:4, tcs(t)], ACT.Square).then_inc(s["sq"], 1)

                square(0)
                for t in range(NTC):
                    norm_wait(act, q, "mm", t + 1)
                    act.activation(rstd[:, tcs(t)], aux[:, t % 2, 0:TC], ACT.Sqrt, scale=1.0 / D, bias=eps)\
                        .then_inc(s["sd"], 1)
                    if t < 2:
                        square(t + 1)
                    if beside:
                        beside["act"](act, t)
                    n = TC if t < 2 else PLAST
                    for half in range(2):
                        g = 2 * t + half
                        norm_wait(act, q, "ml", g + 1)
                        for c in range(4 * half, 4 * half + 4):
                            if i is None:
                                last = act.activation(tmp[:, c, :], tmp[:, c, :], ACT.Copy,
                                                      scale=par[:, ROW_GF + c:ROW_GF + c + 1])
                            else:
                                last = act.activation(tmp[:, c, 0:n], tmp[:, c, 0:n], ACT.Identity,
                                                      scale=a_of[:, c, 0:1], bias=b_of[:, c, 0:1])
                        last.then_inc(s["af"], 1)
                        if i is not None:
                            norm_wait(act, q, "af", g + 1)
                            if t == 2:
                                norm_wait(act, q, "fix", 3 * half + 3)
                            act.activation(nhi[:, 4 * half:4 * half + 4, tcs(t)], tmp[:, 4 * half:4 * half + 4, :],
                                           ACT.Copy).then_inc(s["hi"], 1)
                    if after_act:
                        after_act(act, t)

            def dve(dve):
                def square(t):
                    if t:
                        norm_wait(dve, q, "mm", t)
                    dve.tensor_tensor(sq[:, 4:8, :], h[:, 4:8, tcs(t)], h[:, 4:8, tcs(t)], ALU.mult)\
                        .then_inc(s["sq"], 1)

                square(0)
                for t in range(NTC):
                    norm_wait(dve, q, "sd", t + 1)
                    dve.reciprocal(rstd[:, tcs(t)], rstd[:, tcs(t)]).then_inc(s["rs"], 1)
                    if t < 2:
                        square(t + 1)
                    norm_wait(dve, q, "rs", t + 1)
                    for half in range(2):
                        g = 2 * t + half
                        c4 = slice(4 * half, 4 * half + 4)
                        if t and i is not None:
                            norm_wait(dve, q, "lo", g - 1)
                        if t and i is None:
                            dve.wait_ge(fin_t, 6 * t)
                        dve.tensor_tensor(tmp[:, c4, :], h[:, c4, tcs(t)],
                                          rstd[:, tcs(t)].unsqueeze(1).to_broadcast([P, 4, TC]), ALU.mult)\
                            .then_inc(s["ml"], 1)
                        if t == 2 and i is not None:
                            norm_wait(dve, q, "ml", g + 1)
                            v = by_seq(tmp[:, c4, PLAST:TC])
                            for k, (m, op) in enumerate(((a_of, ALU.mult), (b_of, ALU.add))):
                                for_each = dve.tensor_tensor(v, v, cond(m, 4 * half, 4), op)
                                for_each.then_inc(s["fix"], 1 if k == 0 else 2)
                                if k == 0:
                                    norm_wait(dve, q, "fix", 3 * half + 1)
                    if beside:
                        beside["dve"](dve, t)
                    if i is not None:
                        for half in range(2):
                            g = 2 * t + half
                            c4 = slice(4 * half, 4 * half + 4)
                            norm_wait(dve, q, "hi", g + 1)
                            dve.tensor_tensor(nlo[:, c4, tcs(t)], tmp[:, c4, :], nhi[:, c4, tcs(t)].bitcast(F32),
                                              ALU.subtract).then_inc(s["lo"], 1)
                    if after_dve:
                        after_dve(dve, t)

            def ready(pe, t):
                norm_wait(pe, q, "lo", 2 * t + 2)
            def pe_end(pe):
                if beside:
                    beside["pe_end"](pe)

            pe_sums = pe
            return {"pe": pe, "pe_start": pe_start, "pe_last": pe_last, "pe_end": pe_end, "act": act, "dve": dve, "ready": ready}

        norm_m = norm("m", 1)

        def ffn(q, T0, A0, wg, wu, wd, i, nrm, with_ada):
            f = ffn_sem
            gate = ada[:, (3 * i + 2) * KD:(3 * i + 3) * KD, :]
            order = ((0, wg, 0), (1, wu, 0), (2, wg, 1), (3, wu, 1))

            def sp(sp):
                with sp.Fori(0, NPAIR) as j:
                    for k, w, sub in order:
                        load_tile(sp, T0 + 6 * j + k, k % RING,
                                  lambda slot, w=w, sub=sub: [(slot.rearrange("p (k m) -> p k m", k=KD),
                                      w.rearrange("(k p) m -> p k m", p=P)[:, :, bass.ds((2 * j + sub) * P, P)])])
                    for k, half in ((4, 0), (5, 1)):
                        load_tile(sp, T0 + 6 * j + k, k % RING,
                                  lambda slot, half=half: [(slot.rearrange("p (f m) -> p f m", f=2),
                                      wd[bass.ds(j * 2 * P, 2 * P), 512 * half:512 * half + 512]
                                      .rearrange("(f p) m -> p f m", p=P))])
                    if with_ada:
                        g = INIT_ADA // 4 + j
                        sp.wait_ge(ada_mm, g + 2)
                        sp.dma_start(ada_raw[:, 1], L0["w_ada"].rearrange("(k p) m -> p k m", p=P)
                                     [:, :, bass.ds(g * 4 * P, 4 * P)]).then_inc(ada_in[1], 16)

            def pool(pool):
                if not with_ada:
                    pool.wait_ge(acc_done, A0 - 3)
                with pool.Fori(0, NPAIR) as j:
                    for k in range(6):
                        end = A0 + FFN_ENDS[k - 3] if k >= 3 else A0 + FFN_ENDS[k + 3] - FFN_ACC
                        split(pool, T0 + 6 * j + k, k % RING, turn(T0 + k) + 2 * j, 36 * j + end)

            def pe_up(pe, j, k, t):
                base = 3 * (k % 2)
                pe.wait_ge(split_done, T0 + 6 * j + k + 1)
                if k < 2:
                    ffn_wait(pe, q, "down_free", 24 * j + 19 + base + t)
                    nrm["ready"](pe, t)
                else:
                    ffn_wait(pe, q, ("gate_free", "up_free")[k % 2], 3 * (2 * j + 1) + t + 1)
                product(pe, main[:, base + t, 0:TC], k % RING, range(KD),
                        lambda c: nhi[:, c, tcs(t)], lambda c: nlo[:, c, tcs(t)], 0).then_inc(acc_done, 1)

            def pe_step(pe, j, first):
                for t in range(NTC):
                    pe_up(pe, j, 0, t)
                    if first and t == 0:
                        nrm["pe_last"](pe)
                    if first and t == 1:
                        nrm["pe_end"](pe)
                    pe_up(pe, j, 1, t)
                for k in (2, 3):
                    for t in range(NTC):
                        pe_up(pe, j, k, t)
                for half in range(2):
                    if with_ada and half:
                        if first:
                            pe.wait_ge(c_split, 2)
                        pe_ada_split(pe, INIT_ADA // 4 + j, aux[:, 0])
                    pe.wait_ge(split_done, T0 + 6 * j + 4 + half + 1)
                    for t in range(NTC):
                        if half == 0:
                            ffn_wait(pe, q, "hid_lo", 6 * j + 3 + t + 1)
                        for m in range(4):
                            d = 12 * half + 4 * t + m
                            if d < 3:
                                ffn_wait(pe, q, "gate_free", 6 * j + 7 + d)
                            elif d < 6:
                                ffn_wait(pe, q, "up_free", 6 * j + 4 + d)
                            else:
                                ffn_wait(pe, q, "down_free", 24 * j + d + 19)
                            product(pe, main[:, d % NBANK, 0:TC], (4 + half) % RING, range(2),
                                    lambda c: hid_hi[:, c, tcs(t)], lambda c: hid_lo[:, c, tcs(t)],
                                    m * P, mstride=512).then_inc(acc_done, 1)
                if with_ada:
                    pe_ada_turn(pe, INIT_ADA // 4 + j, aux[:, 1], ada_rows[1])

            def pe(pe):
                nrm["pe_start"](pe)
                pe_step(pe, 0, True)
                with pe.Fori(1, NPAIR) as j:
                    pe_step(pe, j, False)

            def up_done(j, sub, t, up):
                return A0 + 36 * j + (2 * t + up + 1 if sub == 0 else 6 + 3 * up + t + 1)

            def act_free(act):
                act.drain().then_inc(f["gate_free"], 3)

            def dve_free(dve):
                dve.drain().then_inc(f["up_free"], 3)
                dve.drain().then_inc(f["down_free"], 24)

            def act(act):
                norm_wait(act, q, "lo", 6)
                with act.Fori(0, NPAIR) as j:
                    for sub in range(2):
                        for t in range(NTC):
                            act.wait_ge(acc_done, up_done(j, sub, t, 0))
                            act.activation(tmp[:, t, :], main[:, t, 0:TC], ACT.Silu).then_inc(f["gate_free"], 1)
                            ffn_wait(act, q, "up_free", 3 + 6 * j + 3 * sub + t + 1)
                            act.activation(hid_hi[:, sub, tcs(t)], tmp[:, 3 + t, :], ACT.Copy).then_inc(f["hid_hi"], 1)
                    if with_ada:
                        for i in range(4):
                            act_ada_hi(act, INIT_ADA // 4 + j, i)
                        act_ada(act, INIT_ADA // 4 + j, aux[:, 0], ada_rows[1])

            def dve(dve):
                with dve.Fori(0, NPAIR) as j:
                    for sub in range(2):
                        for t in range(NTC):
                            dve.wait_ge(acc_done, up_done(j, sub, t, 1))
                            ffn_wait(dve, q, "gate_free", 3 + 6 * j + 3 * sub + t + 1)
                            dve.tensor_tensor(tmp[:, 3 + t, :], main[:, 3 + t, 0:TC], tmp[:, t, :], ALU.mult)\
                                .then_inc(f["up_free"], 1)
                            ffn_wait(dve, q, "hid_hi", 6 * j + 3 * sub + t + 1)
                            dve.tensor_tensor(hid_lo[:, sub, tcs(t)], tmp[:, 3 + t, :],
                                              hid_hi[:, sub, tcs(t)].bitcast(F32), ALU.subtract)\
                                .then_inc(f["hid_lo"], 1)
                    for d in range(24):
                        if with_ada and 2 <= d < 6:
                            dve_ada_lo(dve, INIT_ADA // 4 + j, d - 2)
                        half, t, m = d // 12, d % 12 // 4, d % 4
                        c = 4 * half + m
                        n = TC if t < 2 else PLAST
                        dve.wait_ge(acc_done, A0 + 36 * j + 12 + d + 1)
                        ffn_wait(dve, q, "down_free", 24 * j + d + 1)
                        if t == 2:
                            dve.tensor_tensor(small[:, c, :].rearrange("p (b s) -> p b s", b=NSEQ),
                                              main[:, d % NBANK, PLAST:TC].rearrange("p (b s) -> p b s", b=NSEQ),
                                              gate[:, c, 1:NCOND].unsqueeze(2).to_broadcast([P, NSEQ, SNEW]),
                                              ALU.mult).then_inc(f["samp"], 1)
                            ffn_wait(dve, q, "samp", 8 * j + 4 * half + m + 1)
                            dve.tensor_tensor(h[:, c, SEQ:TOK], h[:, c, SEQ:TOK], small[:, c, :], ALU.add)
                        dve.scalar_tensor_tensor(h[:, c, t * TC:t * TC + n], main[:, d % NBANK, 0:n], gate[:, c, 0:1],
                                                 h[:, c, t * TC:t * TC + n], ALU.mult, ALU.add)\
                            .then_inc(f["down_free"], 1)
                    if with_ada:
                        dve_ada(dve, INIT_ADA // 4 + j, aux[:, 1])
            return {"sp": sp, "pool": pool, "pe": pe, "act": act, "dve": dve, "act_free": act_free,
                    "dve_free": dve_free}

        w_in = L0["w_in"]
        qi = place("qi", [P, 4, TOK], F32, HB)
        conv_y = place("conv_y", [P, 4, TOK], F32, HB)
        zraw = place("zraw", [P, 2, TOK], F32, HB + 16896)
        zsw = place("zsw", [P, 2, TOK], F32, HB + 25344)
        pick = place("pick", [P, 36 * P], F32, RB)
        UB = RB + 36 * P * 4
        uext = place("uext", [P, 4, HIST + SEQ], F32, UB)
        ipage = place("ipage", [P, 2 * NSEQ, P], F32, UB + 21504)
        kis = place("kis", [P, 2, SKEYS], F32, UB + 8448)
        rs = place("rs", [P, 2, SKEYS], F32, UB + 10752)
        qib = place("qib", [P, 4, NSEQ, 32], F32, UB + 13056)
        uext_s = place("uext_s", [P, 4, NSEQ, HIST + SNEW], F32, UB + 17152)
        rot = place("rot", [P, 2, TOK], F32, UB)
        kiw = place("kiw", [72, TOK], F32, UB + 29696)
        ki_b = place("ki_b", [P, TOK], F32, UB + 33920)
        rbuf = place("rbuf", [P, 2, 512], F32, UB + 38144)
        conv_p = place("conv_p", [P, NSEQ, SNEW, CW], F32, UB + 38144)
        state_tok = place("state_tok", [P, 2, D_CONV], F32, UB + 38144)
        kw_tok = place("kw_tok", [P, 9, 72], F32, UB + 42240)
        unew = place("unew", [P, 4, NSAMP], F32, UB + 42240)
        wabs = place("wabs", [P, 8, H], F32, UB + 44832)
        wsgn = place("wsgn", [P, 8, H], F32, UB + 45088)
        wr = place("wr", [P, 2], F32, UB + 45344)
        wra = place("wra", [P, 2], F32, UB + 45376)
        wrs = place("wrs", [P, 2], F32, UB + 45408)
        top8 = place("top8", [P, 8], F32, UB + 45440)
        at8 = place("at8", [NSAMP, 8], U32, UB + 45472)
        atf = place("atf", [NSAMP, 1], F32, UB + 45504)
        pick_s = place("pick_s", [NSAMP, SKEYS], F32, UB + 45536)
        one_s = place("one_s", [NSAMP, SKEYS], F32, UB + 29696)

        def dram(name, shape):
            return nc.dram_tensor(name, list(shape), F32, kind="Internal").ap()

        h_d, q_d, k_d, v_d = (dram(n, [P, c, TOK]) for n, c in (("h_d", KD), ("q_d", 4), ("k_d", 4), ("v_d", 4)))
        gate_d = dram("gate_d", [P, 2 * KD, TOK])
        w_d = dram("w_d", [NSEQ, H, SNEW])

        z_free = sem("z_free")
        swap_in = [sem("swap_in0"), sem("swap_in1")]
        rope_tab = sem("rope_tab")
        rope_a = sem("rope_a")
        rope_b = sem("rope_b")
        z_out = [sem("z_out0"), sem("z_out1")]
        glu = sem("glu")
        h_out = sem("h_out")
        page_in = sem("page_in")
        state_in = sem("state_in")
        kib_in = sem("kib_in")
        w_out_d = sem("w_out_d")
        wr_in = sem("wr_in")
        kw_t = sem("kw_t")
        kw_e = sem("kw_e")
        st_t = sem("st_t")
        st_e = sem("st_e")
        pg_t = sem("pg_t")
        pg_e = sem("pg_e")
        si_prep = sem("si_prep")
        si_mm = sem("si_mm")
        si_r = sem("si_r")
        si_s = sem("si_s")
        si_sel = sem("si_sel")
        wprep = sem("wprep")
        idx_mm = sem("idx_mm")
        idx_act = sem("idx_act")
        idx_set = sem("idx_set")
        idx_sum = sem("idx_sum")
        tk = sem("tk")
        cv = sem("cv")
        uzero = sem("uzero")

        def off(b):
            return P * (b * (b + 1) // 2)

        PIECES = [(b, hh, c0, min(512, P * (b + 1) - c0)) for b in range(2, 8) for hh in range(H)
                  for c0 in range(0, P * (b + 1), 512)]
        PIECE0 = {b: [i for i, x in enumerate(PIECES) if x[0] == b][0] for b in range(2, 8)}

        def pieces(b, hh):
            return [(n, c0, w) for n, (bb, h_, c0, w) in enumerate(PIECES) if (bb, h_) == (b, hh)]

        ZCOL = [3072] + [2560 + P * i for i in range(4)] + [1024 + P * i for i in range(12)] \
            + [512 * (i % 2) + P * (i // 2) for i in range(8)] + [3144 + P * i for i in range(16)]
        Z_Q, Z_V, Z_GLU, Z_GATE = 5, 13, 17, 25
        Z_LOOP = 29

        BESIDE = {3: 10, 4: 12, 5: 15, 6: 17, 7: 18}
        AFTER, first = {}, 0
        for b in range(3, 8):
            for hh in range(H):
                AFTER.setdefault(first + hh * BESIDE[b] // H, []).extend(pieces(b, hh))
            first += BESIDE[b]

        def with_tile(L, t):
            return AFTER.get(3 * (L - Z_Q) + t, [])
        assert first == 3 * (Z_LOOP - Z_Q)

        def m1_sp(sp):
            for L in range(3):
                load_tile(sp, T_Z + L, L % RING, cols(w_in, ZCOL[L], 72 if L == 0 else P))
            ffn_wait(sp, "1", "down_free", 24 * NPAIR + 24)
            sp.dma_start(h_d, h[:, :, :]).then_inc(h_out, 16)
            sp.wait_ge(ada_mm, ADA_TILES // 4 + 2)
            sp.dma_start(ki_b[0:NSAMP, 0:2 * SKEYS], consts[0:NSAMP, C_SMASK:C_SMASK + 2 * SKEYS])\
                .then_inc(rope_tab, 16)
            for g in range(2):
                sp.dma_start(state_tok[0:4 * HIST, g, :],
                             L0["state_conv"][4 * g:4 * g + 4].rearrange("b r d -> (b r) d")).then_inc(state_in, 16)
            for L in range(3, Z_Q):
                load_tile(sp, T_Z + L, L % RING, cols(w_in, ZCOL[L]))
            for b in range(NSEQ):
                for pg in range(2):
                    page = sp.value_load(a["page_table"][b:b + 1, pg:pg + 1], min_val=0,
                                         max_val=L0["cache_idx_k"].shape[0] - 1)
                    sp.dma_start(ipage[:, 2 * b + pg, :].rearrange("p (t d) -> p t d", t=2),
                                 L0["cache_idx_k"][bass.ds(page, 1), :, :].rearrange("o p d -> (o p) d")
                                 .unsqueeze(1).to_broadcast([P, 2, HD])).then_inc(page_in, 16)
            norm_wait(sp, "m", "lo", 6)
            sp.dma_start(rot[:, :, :], rope).then_inc(rope_tab, 16)
            sp.wait_ge(w_out_d, 16)
            sp.dma_start(wr[:, :], w_d.rearrange("(t b) h s -> (b h s) t", t=2),
                         allow_slow_non_contiguous=True).then_inc(wr_in, 16)
            for L in range(Z_Q, NZ):
                load_tile(sp, T_Z + L, L % RING, cols(w_in, ZCOL[L]))

        def m1_pool(pool):
            def post(L):
                s = L % 2
                if Z_Q <= L < Z_V:
                    n = L - Z_Q
                    pool.wait_ge(swap_in[s], SWAPS[L])
                    pool.wait_ge(z_free, 6 + 3 * L + 3)
                    pool.tensor_tensor(zsw[:, s, :], zsw[:, s, :], rot[:, 1, :], ALU.mult).then_inc(rope_b, 1)
                    pool.tensor_tensor(zraw[:, s, :], zraw[:, s, :], rot[:, 0, :], ALU.mult).then_inc(rope_b, 1)
                    pool.wait_ge(rope_b, 3 * n + 2)
                    pool.tensor_tensor(zraw[:, s, :], zraw[:, s, :], zsw[:, s, :], ALU.add).then_inc(rope_b, 1)
                elif Z_GLU <= L < Z_GATE and (L - Z_GLU) % 2:
                    c = (L - Z_GLU) // 2
                    pool.wait_ge(z_free, 6 + 3 * L + 3)
                    if c == 0:
                        pool.wait_ge(si_sel, 2)
                        pool.memset(uext[:, :, 0:HIST], 0.0).then_inc(uzero, 1)
                    pool.tensor_tensor(uext[:, c, HIST:], zraw[:, 1, 0:SEQ], zraw[:, 0, 0:SEQ], ALU.mult)\
                        .then_inc(glu, 1)
                    if c == 0:
                        pool.wait_ge(ki_out, 32)
                        pool.wait_ge(wprep, 6)
                    pool.tensor_tensor(unew[:, c, :], zraw[:, 1, SEQ:TOK], zraw[:, 0, SEQ:TOK], ALU.mult)\
                        .then_inc(glu, 1)
                    pool.tensor_tensor(uext_s[:, c, :, HIST:],
                                       zraw[:, 1, SEQ:TOK].rearrange("p (b s) -> p b s", b=NSEQ),
                                       zraw[:, 0, SEQ:TOK].rearrange("p (b s) -> p b s", b=NSEQ), ALU.mult)\
                        .then_inc(glu, 1)

            def one(L):
                used = ACC_Z + max(5, 3 * L - 6) if L >= 3 else ACC_Z - FFN_ACC + FFN_ENDS[3 + L]
                split(pool, T_Z + L, (T_Z + L) % RING, (T_Z + L) // RING, used)

            for L in range(28):
                one(L)
                if L >= 3:
                    post(L - 3)
            with pool.Fori(0, 4) as i:
                for k in range(3):
                    L = 28 + k
                    split(pool, T_Z + L + 3 * i, (T_Z + L) % RING, (T_Z + L) // RING + i, ACC_Z + 3 * L - 6 + 9 * i)
            one(40)

        SWAPS = {}
        n_swap = [0, 0]
        for L in range(Z_V):
            n_swap[L % 2] += 16 * (2 if L == 0 else 4)
            SWAPS[L] = n_swap[L % 2]

        def z_product(pe, L, T, slot, V, parity, m=P, then=None, ts=range(NTC)):
            pe.wait_ge(split_done, T + 1)
            for t in ts:
                pe.wait_ge(z_free, V + t + 1)
                product(pe, main[0:m, 3 * parity + t, 0:TC], slot, range(KD),
                        lambda c: nhi[:, c, tcs(t)], lambda c: nlo[:, c, tcs(t)], 0, m=m).then_inc(acc_done, 1)
                if then:
                    then(t)

        def m1_pe(pe):
            ffn_wait(pe, "1", "down_free", 24 * NPAIR + 24)
            norm_m["pe_start"](pe)
            for t in range(NTC):
                for L in range(2):
                    norm_m["ready"](pe, t)
                    z_product(pe, L, T_Z + L, L % RING, 3 * L, L % 2, 72 if L == 0 else P, ts=(t,))
                    if L == 0 and t == 0:
                        norm_m["pe_last"](pe)
            for L in range(2, Z_Q):
                z_product(pe, L, T_Z + L, L % RING, 3 * L, L % 2)
            pe.wait_ge(z_free, 6 + 3 * Z_Q)
            pe.wait_ge(state_in, 32)
            for g in range(2):
                for c in range(4):
                    last = pe.transpose(main[:, 3 * g, bass.ts(c, 4 * HIST)], state_tok[0:4 * HIST, g, bass.ts(c, P)],
                                        ident[0:4 * HIST, 0:4 * HIST])
                last.then_inc(st_t, 1)
            pe.wait_ge(rope_a, 3)
            for t in range(9):
                n = P if t < 8 else NSAMP
                last = pe.transpose(aux[0:n, t // 5, bass.ts(t % 5, 72)], kiw[:, t * P:t * P + n], ident[0:72, 0:72])
                if t in (4, 8):
                    last.then_inc(kw_t, 1)
            pe.wait_ge(page_in, 16 * 2 * NSEQ)
            for b in range(NSEQ):
                if b >= 2:
                    pe.wait_ge(pg_e, b - 1)
                for pg in range(2):
                    last = pe.transpose(main[:, 4 + b % 2, bass.ts(pg, P)], ipage[:, 2 * b + pg, :], ident)
                last.then_inc(pg_t, 1)
                pe.wait_ge(pg_e, b + 1)
                if b == 0:
                    pe.wait_ge(si_prep, 4 + 9)
                for c in range(4):
                    last = pe.matmul(main[32 * (b % 4):32 * (b % 4) + 32, b // 4 + 1, 0:SKEYS], qib[:, c, b, :],
                                     kis[:, b % 2, :], start=(c == 0), stop=(c == 3))
                last.then_inc(si_mm, 1)
            pe.wait_ge(st_e, 2)
            for half in range(2):
                pe.wait_ge(si_s, half + 1)
                last = pe.matmul(main[0:NSAMP, 0, 0:SKEYS], cst[:, C_SEL + 32 * half:C_SEL + 32 * half + 32],
                                 rs[:, half, :], start=(half == 0), stop=(half == 1))
            last.then_inc(si_sel, 1)
            pe.wait_ge(rope_a, 3 * Z_Q)
            pe.wait_ge(kib_in, 16)
            pe.wait_ge(kw_e, 3)
            def score(n):
                b, hh, c0, w = PIECES[n]
                if n >= 2:
                    pe.wait_ge(idx_act, n - 1)
                lo = HD * (hh % 2)
                keys = kiw[0:HD, c0:c0 + w] if lo == 0 else ki_b[HD:P, c0:c0 + w]
                pe.matmul(aux[:, n % 2, 0:w], qi[lo:lo + HD, hh // 2, bass.ts(b, P)], keys, start=True, stop=True)\
                    .then_inc(idx_mm, 1)

            for n in range(PIECE0[3]):
                score(n)
            pe.wait_ge(si_sel, 2)
            pe.wait_ge(pg_e, NSEQ)
            pe.wait_ge(si_r, 2)
            for L in range(Z_Q, Z_LOOP):
                def then(t):
                    for n, _, _ in with_tile(L, t):
                        score(n)
                z_product(pe, L, T_Z + L, (T_Z + L) % RING, 3 * L, L % 2, then=then)
            with pe.Fori(0, 2) as i:
                for k in range(6):
                    L = Z_LOOP + k
                    z_product(pe, L, T_Z + L + 6 * i, (T_Z + L) % RING, 3 * L + 18 * i, L % 2)

        def evac(act, dst, L, i, func, src_rows=P, then=None):
            for t in range(NTC):
                act.wait_ge(acc_done, ACC_Z + 3 * L + t + 1 + i)
                act.activation(dst[0:src_rows, tcs(t)], main[0:src_rows, 3 * (L % 2) + t, 0:TC], func)\
                    .then_inc(z_free, 1)
                if then:
                    for n, _, _ in with_tile(L, t):
                        then(n)

        def swap(act, s, rows):
            for r in range(0, rows, 32):
                o = r + 32 if r % 64 == 0 else r - 32
                act.dma_start(zsw[r:r + 32, s, :], zraw[o:o + 32, s, :]).then_inc(swap_in[s], 16)

        def m1_act(act):
            act.wait_ge(h_out, 16)
            for L in range(Z_Q):
                if L >= 2:
                    act.wait_ge(rope_a, 3 * (L - 1))
                for t in range(NTC):
                    act.wait_ge(acc_done, ACC_Z + (2 * t + L + 1 if L < 2 else 3 * L + t + 1))
                    if L == 0:
                        act.activation(kiw[64:72, tcs(t)], main[64:72, t, 0:TC], ACT.Copy).then_inc(wprep, 1)
                    n = 64 if L == 0 else P
                    act.activation(zraw[0:n, L % 2, tcs(t)], main[0:n, 3 * (L % 2) + t, 0:TC], ACT.Copy)\
                        .then_inc(z_free, 1)
                act.wait_ge(z_free, 6 + 3 * L + 3)
                swap(act, L % 2, 64 if L == 0 else P)
                if L == 0:
                    act.wait_ge(wprep, 3)
                    act.dma_start(w_d.rearrange("b h s -> h b s"),
                                  kiw[64:72, SEQ:TOK].rearrange("h (b s) -> h b s", b=NSEQ)).then_inc(w_out_d, 16)
                if L == 1:
                    act.wait_ge(rope_a, 3)
                    act.dma_start(ki_b[HD:P, :], kiw[0:HD, :]).then_inc(kib_in, 16)
            for g in range(2):
                act.wait_ge(st_t, g + 1)
                act.activation(uext_s[:, :, 4 * g:4 * g + 4, 0:HIST],
                               main[:, 3 * g, 0:16 * HIST].rearrange("p (c b r) -> p c b r", c=4, b=4), ACT.Copy)\
                    .then_inc(st_e, 1)
            for g, n in ((0, 5), (1, 4)):
                act.wait_ge(kw_t, g + 1)
                act.activation(kw_tok[:, 5 * g:5 * g + (5 if g == 0 else 3), :],
                               aux[:, g, 0:72 * (5 if g == 0 else 3)].rearrange("p (t c) -> p t c", c=72), ACT.Copy)\
                    .then_inc(kw_e, 1)
            act.activation(kw_tok[0:NSAMP, 8, :], aux[0:NSAMP, 1, 216:288], ACT.Copy).then_inc(kw_e, 1)
            act.wait_ge(kw_e, 3)
            act.dma_start(out[4][0, 0].rearrange("(t p) d -> p t d", p=P), kw_tok[:, 0:8, 0:HD]).then_inc(ki_out, 16)
            act.dma_start(out[8][0].rearrange("b s d -> (b s) d"), kw_tok[0:NSAMP, 8, 0:HD]).then_inc(ki_out, 16)
            for b in range(NSEQ):
                act.wait_ge(pg_t, b + 1)
                if b >= 2:
                    act.wait_ge(si_mm, b - 1)
                act.activation(kis[:, b % 2, 0:PAST], main[:, 4 + b % 2, 0:PAST], ACT.Copy).then_inc(pg_e, 1)
                if b % 4 == 3:
                    act.wait_ge(si_mm, b + 1)
                    if b == 3:
                        act.wait_ge(si_prep, 4 + 9 + 2)
                    act.activation(rs[:, b // 4, :], main[:, b // 4 + 1, 0:SKEYS], ACT.Relu,
                                   scale=wra[:, b // 4:b // 4 + 1]).then_inc(si_r, 1)
            act.wait_ge(wprep, 3 + 3)

            def weigh(n):
                b, hh, c0, w = PIECES[n]
                act.wait_ge(idx_mm, n + 1)
                if n >= 2:
                    act.wait_ge(idx_sum, n)
                act.activation(rbuf[:, n % 2, 0:w], aux[:, n % 2, 0:w], ACT.Relu, scale=wabs[:, b, hh:hh + 1])\
                    .then_inc(idx_act, 1)
            for n in range(PIECE0[3]):
                weigh(n)

            def store(L, dst):
                act.dma_start(dst, zraw[:, L % 2, :]).then_inc(z_out[L % 2], 16)

            act.wait_ge(rope_a, 3 * Z_Q)
            for L in range(Z_Q, Z_GLU):
                s = L % 2
                if L >= Z_Q + 2:
                    act.wait_ge(z_out[s], 16 * ((L - Z_Q) // 2))
                evac(act, zraw[:, s, :], L, 0, ACT.Copy, then=weigh)
                if L < Z_V:
                    act.wait_ge(z_free, 6 + 3 * L + 3)
                    swap(act, s, P)
                if L > Z_Q and L - 1 < Z_V:
                    act.wait_ge(rope_b, 3 * (L - 1 - Z_Q) + 3)
                    n = L - 1 - Z_Q
                    store(L - 1, (q_d if n < 4 else k_d)[:, n % 4, :])
                if L >= Z_V:
                    act.wait_ge(z_free, 6 + 3 * L + 3)
                    store(L, v_d[:, L - Z_V, :])
            act.wait_ge(z_out[0], 16 * 6)
            act.wait_ge(z_out[1], 16 * 6)
            for c in range(4):
                L = Z_GLU + 2 * c
                if c:
                    act.wait_ge(glu, 3 * c)
                evac(act, zraw[:, 1, :], L, 0, ACT.Copy, then=weigh)
                evac(act, zraw[:, 0, :], L + 1, 0, ACT.Sigmoid, then=weigh)
            act.wait_ge(glu, 12)
            def gate(L, i, then=None):
                s, m = L % 2, L - Z_GATE
                act.wait_ge(z_out[s], 16 * (6 + m // 2) + 16 * i)
                evac(act, zraw[:, s, :], L, 6 * i, ACT.Sigmoid, then=then)
                act.wait_ge(z_free, 6 + 3 * L + 3 + 6 * i)
                act.dma_start(gate_d[:, bass.ds(2 * i + m, 1), :].rearrange("p o n -> p (o n)"), zraw[:, s, :])\
                    .then_inc(z_out[s], 16)

            for L in range(Z_GATE, Z_LOOP):
                gate(L, 0, then=weigh)
            with act.Fori(0, (NZ - Z_LOOP) // 2) as i:
                for k in range(2):
                    gate(Z_LOOP + k, i)

        def m1_dve(dve):
            norm_wait(dve, "m", "lo", 6)
            dve.memset(qib[:, :, :, :], 0.0).then_inc(si_prep, 1)
            dve.wait_ge(rope_tab, 32)
            for L in range(Z_Q):
                s, n = L % 2, HD if L == 0 else P
                dst = kiw[0:HD, :] if L == 0 else qi[:, L - 1, :]
                dve.wait_ge(swap_in[s], SWAPS[L])
                dve.tensor_tensor(zsw[0:n, s, :], zsw[0:n, s, :], rot[0:n, 1, :], ALU.mult).then_inc(rope_a, 1)
                dve.wait_ge(z_free, 6 + 3 * L + 3)
                dve.tensor_tensor(dst, zraw[0:n, s, :], rot[0:n, 0, :], ALU.mult).then_inc(rope_a, 1)
                dve.wait_ge(rope_a, 3 * L + 2)
                dve.tensor_tensor(dst, dst, zsw[0:n, s, :], ALU.add).then_inc(rope_a, 1)
                if L == 3:
                    dve.wait_ge(kib_in, 16)
                    for i in range(2):
                        dve.tensor_copy(kis[0:HD, i, PAST:SKEYS], kiw[0:HD, SEQ:TOK]).then_inc(si_prep, 1)
                        dve.tensor_copy(kis[HD:P, i, PAST:SKEYS], ki_b[HD:P, SEQ:TOK]).then_inc(si_prep, 1)
                if L:
                    c = L - 1
                    dve.wait_ge(si_prep, 1)
                    dve.wait_ge(rope_a, 3 * L + 3)
                    for p in range(2):
                        r, hh = slice(HD * p, HD * p + HD), 2 * c + p
                        dve.tensor_copy(qib[r, c, :, SNEW * hh:SNEW * (hh + 1)],
                                        qi[r, c, SEQ:TOK].rearrange("p (b s) -> p b s", b=NSEQ)).then_inc(si_prep, 1)
            scale = float(np.float32((H * HD) ** -0.5))
            dve.wait_ge(wr_in, 16)
            dve.scalar_tensor_tensor(wra[:, :], wr[:, :], -1.0, wr[:, :], ALU.mult, ALU.max).then_inc(si_prep, 1)
            dve.tensor_scalar(wrs[:, :], wr[:, :], 0.0, 2.0 * scale, ALU.is_ge, ALU.mult).then_inc(si_prep, 1)
            dve.wait_ge(si_prep, 15)
            dve.tensor_scalar(wrs[:, :], wrs[:, :], scale, None, ALU.subtract).then_inc(si_prep, 1)
            dve.wait_ge(kw_e, 2)
            dve.scalar_tensor_tensor(wabs[:, :, :], kw_tok[:, 0:8, HD:72], -1.0, kw_tok[:, 0:8, HD:72],
                                     ALU.mult, ALU.max)\
                .then_inc(wprep, 1)
            dve.tensor_scalar(wsgn[:, :, :], kw_tok[:, 0:8, HD:72], 0.0, 2.0 * scale, ALU.is_ge, ALU.mult).then_inc(wprep, 1)
            dve.wait_ge(wprep, 5)
            dve.tensor_scalar(wsgn[:, :, :], wsgn[:, :, :], scale, None, ALU.subtract).then_inc(wprep, 1)
            dve.wait_ge(si_prep, 16)
            for half in range(2):
                dve.wait_ge(si_r, half + 1)
                dve.tensor_scalar(rs[:, half, :], rs[:, half, :], wrs[:, half:half + 1], None, ALU.mult)\
                    .then_inc(si_s, 1)
            dve.wait_ge(si_sel, 1)
            dve.tensor_tensor(pick_s[:, :], main[0:NSAMP, 0, 0:SKEYS], ki_b[0:NSAMP, 0:SKEYS], ALU.add)\
                .then_inc(si_sel, 1)
            dve.memset(pick[:, :], 0.0).then_inc(idx_set, 1)
            dve.wait_ge(idx_set, 1)
            for b in range(8):
                dve.tensor_copy(pick[:, off(b) + P * b:off(b + 1)], cst[:, C_CAUSAL:C_CAUSAL + P]).then_inc(idx_set, 1)
            dve.wait_ge(wprep, 6)
            dve.wait_ge(idx_set, 9)
            dve.drain().then_inc(idx_sum, 1)

            def add_piece(b, head, n, slot, c0, w):
                dst = pick[:, off(b) + c0:off(b) + c0 + w]
                dve.wait_ge(idx_act, n + 1)
                dve.wait_ge(idx_sum, n + 1)
                dve.scalar_tensor_tensor(dst, rbuf[:, slot, 0:w], wsgn[:, b, head], dst, ALU.mult, ALU.add)\
                    .then_inc(idx_sum, 1)

            for n, (b, hh, c0, w) in enumerate(PIECES[:PIECE0[3]]):
                add_piece(b, slice(hh, hh + 1), n, n % 2, c0, w)
            dve.drain().then_inc(tk, 1)
            base = 1

            def round8(scores, n, count):
                dve.wait_ge(tk, count)
                dve.nop(nofuse=True)
                dve.max(top8[0:n, :], scores).then_inc(tk, 1)
                dve.wait_ge(tk, count + 1)
                dve.nop(nofuse=True)

            for b in range(2, 8):
                scores = pick[:, off(b):off(b + 1)]
                dve.wait_ge(idx_sum, 1 + (PIECE0[b + 1] if b < 7 else len(PIECES)))
                with dve.Fori(0, H // 2) as i:
                    for half in range(2):
                        for k in range(TOPK // 8 // H):
                            round8(scores, P, base + 2 * (TOPK // 8 // (H // 2) * i + TOPK // 8 // H * half + k))
                            dve.match_replace(scores, top8[:, :], scores, TAKEN).then_inc(tk, 1)
                        if b < 7:
                            mine = pieces(b + 1, half)
                            for n, c0, w in mine:
                                add_piece(b + 1, bass.ds(2 * i + half, 1), n + 2 * len(mine) * i, n % 2, c0, w)
                base += 2 * (TOPK // 8)
                dve.wait_ge(tk, base)
                dve.tensor_scalar(scores, scores, IS_TAKEN, NEG, ALU.is_gt, ALU.mult).then_inc(tk, 1)
                base += 1
            dve.wait_ge(si_sel, 2)
            with dve.Fori(0, TOPK_S // 8) as i:
                round8(pick_s[:, :], NSAMP, base + 2 * i)
                dve.match_replace(pick_s[:, :], top8[0:NSAMP, :], pick_s[:, :], TAKEN).then_inc(tk, 1)
            base += 2 * (TOPK_S // 8)
            round8(pick_s[:, :], NSAMP, base)
            dve.max_index(at8[:, :], top8[0:NSAMP, :], pick_s[:, :]).then_inc(tk, 1)
            dve.wait_ge(tk, base + 2)
            dve.tensor_copy(atf[:, :], at8[:, 0:1]).then_inc(tk, 1)
            dve.wait_ge(tk, base + 3)
            dve.tensor_scalar(one_s[:, :], ki_b[0:NSAMP, SKEYS:2 * SKEYS], atf[:, 0:1], -NEG,
                              ALU.is_equal, ALU.mult).then_inc(tk, 1)
            dve.tensor_scalar(pick_s[:, :], pick_s[:, :], IS_TAKEN, NEG, ALU.is_gt, ALU.mult).then_inc(tk, 1)
            dve.wait_ge(tk, base + 5)
            dve.tensor_tensor(pick_s[:, :], pick_s[:, :], one_s[:, :], ALU.add).then_inc(tk, 1)
            dve.wait_ge(uzero, 1)
            dve.wait_ge(st_e, 2)
            dve.wait_ge(glu, 12)
            for c in range(4):
                ys_ = conv_y[:, c, SEQ:TOK]
                if c:
                    dve.wait_ge(cv, 6 * c - 1)
                for new in range(SNEW):
                    dve.tensor_tensor(conv_p[:, :, new, :], uext_s[:, c, :, new:new + CW],
                                      taps[:, c, :].unsqueeze(1).to_broadcast([P, NSEQ, CW]), ALU.mult)\
                        .then_inc(cv, 1)
                dve.wait_ge(cv, 6 * c + 4)
                dve.tensor_reduce(ys_, conv_p[:, :, :, :].rearrange("p b s k -> p (b s) k"), AX_X, ALU.add)\
                    .then_inc(cv, 1)
                dve.wait_ge(cv, 6 * c + 5)
                dve.tensor_scalar(ys_, ys_, par[:, ROW_BDW + c:ROW_BDW + c + 1], None, ALU.add).then_inc(cv, 1)
            conv_chunk(dve, 0)

        CV_DEC = 4 * 6
        CV_HALF = CV_DEC + 2 * CW

        def conv_chunk(dve, c, k0=0, k1=CW):
            if k0 == 0:
                conv_first(dve, c)
            with dve.Fori(max(k0, 1), k1) as k:
                dve.wait_ge(cv, CV_DEC + CW * c + k)
                conv_tap(dve, c, taps[:, c, bass.ds(k, 1)], bass.ds(k, SEQ))

        def conv_first(dve, c):
            dve.tensor_scalar(conv_y[:, c, 0:SEQ], uext[:, c, 0:SEQ], taps[:, c, 0:1],
                              par[:, ROW_BDW + c:ROW_BDW + c + 1], ALU.mult, ALU.add).then_inc(cv, 1)

        def conv_tap(dve, c, tap, at):
            y = conv_y[:, c, 0:SEQ]
            dve.scalar_tensor_tensor(y, uext[:, c, at], tap, y, ALU.mult, ALU.add).then_inc(cv, 1)

        qa = place("qa", [P, 4, TOK], F32, NB)
        ka = place("ka", [P, 4, TOK], F32, NB + 16896)
        vtok = place("vtok", [P, 8, ATT], F32, NB + 33792)
        vnew = place("vnew", [NSAMP, ATT], F32, NB + 50176)
        lb = place("lb", [P, 2, SEQ], F32, NB + 52224)
        kts = place("kts", [P, 2, 4, SKEYS], F32, NB + 52224)
        sqc = place("sqc", [P, 4, TC], F32, NB + 52224)
        rstd_c = place("rstd_c", [P, TOK], F32, NB + 60416)
        vraw = place("vraw", [P, 4, TOK], F32, HB + 16896)
        kpg = place("kpg", [P, 4, 2, ATT], F32, UB + 16896)
        vpg = [place(f"vpg{b}", [P, 2, ATT], F32, (HB if b < 4 else UB) + 16896 + 4096 * (b % 4)) for b in range(NSEQ)]
        conv_hi = place("conv_hi", [P, 4, TOK], F32R, UB)
        conv_lo = place("conv_lo", [P, 4, TOK], F32R, HB)
        o_hi = place("o_hi", [P, 4, TOK], F32R, HB + 16896)
        o_lo = place("o_lo", [P, 4, TOK], F32R, UB + 16896)
        pt = place("pt", [P, 2, 8, P], F32, UB + 33792)
        kst = place("kst", [P, 2, ATT], F32, UB + 33792)
        ust = place("ust", [NSAMP, 2, D_CONV], F32, UB + 37888)
        osel = place("osel", [P, 2, ATT], F32, UB + 33792)
        qb = place("qb", [P, 4, NSEQ, 32], F32, NB + 61440)
        pts = place("pts", [P, 2, 3, P], F32, UB + 37888)
        otok = place("otok", [P, ATT], F32, UB + 41984)
        ls = place("ls", [P, 2, SKEYS], F32, UB + 41984)
        mx = place("mx", [P, 2], F32, UB + 44320)
        nb = place("nb", [P, 2], F32, UB + 44352)
        sums = place("sums", [P, 2, H], F32, UB + 44384)
        rinv = place("rinv", [P, 2, H], F32, UB + 44448)
        mixt = place("mixt", [P, 2, 2, TC], F32, UB + 33792)
        gates = place("gates", [P, 2, 2, TOK], F32, RB)

        q_in, k_in, v_in = sem("q_in"), sem("k_in"), sem("v_in")
        kv_t, kv_e = sem("kv_t"), sem("kv_e")
        kst_out = [sem("kst_out0"), sem("kst_out1")]
        u_t, u_e, u_out = sem("u_t"), sem("u_e"), sem("u_out")
        sa_q = sem("sa_q")
        kp_in = [sem(f"kp_in{i}") for i in range(4)]
        vp_in = [sem("vp_in0"), sem("vp_in1")]
        kp_t, kp_e, sl_mm = sem("kp_t"), sem("kp_e"), sem("sl_mm")
        ss = sem("ss")
        se = sem("se")
        sp_t, sp_e, so_mm, so_e = sem("sp_t"), sem("sp_e"), sem("so_mm"), sem("so_e")
        so_s, so_t = sem("so_s"), sem("so_t")
        ln_y, ln_s = sem("ln_y"), sem("ln_sum")
        qk_mm, at_l, at_nb, at_e = sem("qk_mm"), sem("at_l"), sem("at_nb"), sem("at_e")
        pt_t, pt_e, pv_mm = sem("pt_t"), sem("pt_e"), sem("pv_mm")
        at_r, at_o, ot_mm, o_c = sem("at_r"), sem("at_o"), sem("ot_mm"), sem("o_c")
        at_m, o_h, o_l = sem("at_m"), sem("o_h"), sem("o_l")
        g_in = [sem("g_in0"), sem("g_in1")]
        mix_free, mix_a, mix_hi, mix_lo = sem("mix_free"), sem("mix_a"), sem("mix_hi"), sem("mix_lo")
        h_in = [sem("h_in0"), sem("h_in1")]
        out_free, out_s = sem("out_free"), sem("out_s")
        NQ = 8 * H
        PARTS = [(n, p) for n in range(NQ) for p in range(1 + (n // H >= 4))]
        LAST_PART = {n: max(i for i, x in enumerate(PARTS) if x[0] == n) + 1 for n in range(NQ)}
        per_pair = [0, 0, 0, 1, 1, 2, 2, 2]
        TAPS_AT, made = [], 0
        for n in range(NQ):
            TAPS_AT.append(range(made, min(made + per_pair[n // H], 2 * CW)))
            made = TAPS_AT[-1].stop
        assert made == 2 * CW
        TAPS_AT += [[]] * 7
        CV_TOTAL = CV_DEC + 4 * CW
        TK_SAMPLE = 1 + 6 * (2 * (TOPK // 8) + 1) + 2 * (TOPK_S // 8) + 6
        ZDONE = ACC_Z + 3 * NZ
        cond_gate = ada[:, 5 * KD:6 * KD, :]

        def mix_load(m):
            def loads(slot):
                v = slot.rearrange("p (k m) -> p k m", k=KD)
                return [(v[:, 4 * i:4 * i + 4, :], w.rearrange("(k p) m -> p k m", p=P)[:, :, bass.ts(m, P)])
                        for i, w in enumerate((L0["w_conv_out"], L0["w_attn_o"]))]
            return loads

        def m2_sp(sp):
            for m in range(3):
                load_tile(sp, T_MIX + m, (T_MIX + m) % RING, mix_load(m))
            def pages(b, cache, dst, done):
                for pg in range(2):
                    page = sp.value_load(a["page_table"][b:b + 1, pg:pg + 1], min_val=0,
                                         max_val=cache.shape[0] - 1)
                    sp.dma_start(dst[:, pg, :], cache[bass.ds(page, 1)].rearrange("o p h d -> (o p) (h d)"))\
                        .then_inc(done, 16)

            def keys_of(b):
                pages(b, L0["cache_k"], kpg[:, b % 4], kp_in[b % 4])

            def values_of(b):
                pages(b, L0["cache_v"], vpg[b], vp_in[b // 4])

            sp.wait_ge(tk, TK_SAMPLE)
            sp.wait_ge(cv, CV_DEC)
            for b in range(4):
                keys_of(b)
            sp.wait_ge(acc_done, ZDONE)
            sp.wait_ge(z_out[0], 16 * 14)
            sp.wait_ge(z_out[1], 16 * 14)
            sp.dma_start(vraw[:, :, :], v_d).then_inc(v_in, 16)
            sp.dma_start(ka[:, :, :], k_d).then_inc(k_in, 16)
            sp.dma_start(qa[:, :, :], q_d).then_inc(q_in, 16)
            sp.dma_start(out[9][0][:, 0:HIST - SNEW, :], L0["state_conv"][:, SNEW:HIST, :]).then_inc(u_out, 16)

            sp.wait_ge(kv_t, 9)
            for b in range(4):
                values_of(b)
            for b in range(4, NSEQ):
                sp.wait_ge(kp_t, 2 * (b - 3))
                keys_of(b)
            for b in range(4, NSEQ):
                sp.wait_ge(kp_t, 2 * (b + 1))
                values_of(b)
            for m in range(3, KD):
                gate_load(sp, m - 3)
                load_tile(sp, T_MIX + m, (T_MIX + m) % RING, mix_load(m))
            for m in range(KD - 3, KD):
                gate_load(sp, m)
                load_tile(sp, T_OUT + m - 5, (T_OUT + m - 5) % RING, cols(L0["w_out"], P * (m - 5)))
            sp.wait_ge(acc_done, ACC_OUT)
            sp.dma_start(h[:, 0:2, :], h_d[:, 0:2, :]).then_inc(h_in[0], 16)
            sp.dma_start(h[:, 2:KD, :], h_d[:, 2:KD, :]).then_inc(h_in[1], 16)
            for m in range(3, KD):
                load_tile(sp, T_OUT + m, (T_OUT + m) % RING, cols(L0["w_out"], P * m))

        def gate_load(sp, m):
            if m < 2:
                sp.wait_ge(pt_t, len(PARTS))
            else:
                sp.wait_ge(mix_free, 3 + 3 * (m - 1))
            for i in range(2):
                sp.dma_start(gates[:, m % 2, i, :], gate_d[:, KD * i + m, :]).then_inc(g_in[m % 2], 16)

        def turn(T):
            return T // RING + len([x for x in range(T_MIX, T_MIX + KD) if x <= T and x % RING == T % RING])

        def m2_pool(pool):
            for m in range(KD):
                T = T_MIX + m
                used = ACC_Z + 3 * (NZ - 3 + m) + 3 if m < 3 else ACC_MIX + 6 * (m - 3) + 6
                split(pool, T, T % RING, turn(T), used)
            for m in range(KD):
                T = T_OUT + m
                used = ACC_MIX + 6 * (KD - 3 + m) + 6 if m < 3 else ACC_OUT + 3 * (m - 3) + 3
                split(pool, T, T % RING, turn(T), used)

        def m2_pe(pe):
            pe.wait_ge(z_free, 6 + 3 * NZ)

            def turn_pages(b):
                pe.wait_ge(kp_in[b % 4], 32 * (b // 4 + 1))
                for pg in range(2):
                    if 2 * b + pg >= 2:
                        pe.wait_ge(kp_e, 2 * b + pg - 1)
                    for c in range(4):
                        last = pe.transpose(main[:, pg, bass.ts(c, P)], kpg[:, b % 4, pg, bass.ts(c, P)], ident)
                    last.then_inc(kp_t, 1)

            for b in range(2):
                turn_pages(b)
            pe.wait_ge(kp_e, 4)
            pe.wait_ge(v_in, 16)
            for g in range(18):
                if g == 9:
                    pe.wait_ge(k_in, 16)
                t, src = g % 9, (vraw, ka)[g // 9]
                n = P if t < 8 else NSAMP
                if g >= NBANK:
                    pe.wait_ge(kv_e, g - NBANK + 1)
                for c in range(4):
                    last = pe.transpose(main[0:n, g % NBANK, bass.ts(c, P)], src[:, c, t * P:t * P + n], ident)
                last.then_inc(kv_t, 1)
            pe.wait_ge(glu, 12)
            pe.wait_ge(kv_e, 14)
            for c in range(4):
                last = pe.transpose(main[0:HIST, 0, bass.ts(c, P)], uext[:, c, SEQ:SEQ + HIST], ident)
            last.then_inc(u_t, 1)
            for c in range(4):
                last = pe.transpose(main[0:NSAMP, 1, bass.ts(c, P)], unew[:, c, :], ident)
            last.then_inc(u_t, 1)
            pe.wait_ge(kv_e, 18)
            pe.wait_ge(u_e, 2)
            pe.wait_ge(sa_q, 17)
            pe.wait_ge(tk, TK_SAMPLE)
            for half in range(2):
                pe.matmul(main[:, 4 + half, 0:SKEYS], cst[0:NSAMP, C_SELT + P * half:C_SELT + P * (half + 1)],
                          pick_s[:, :], start=True, stop=False, skip_group_check=True)
            for b in range(NSEQ):
                pe.wait_ge(kp_e, 2 * b + 2)
                for c in range(4):
                    last = pe.matmul(main[32 * (b % 4):32 * (b % 4) + 32, 4 + b // 4, 0:SKEYS], qb[:, c, b, :],
                                     kts[:, b % 2, c, :], start=False, stop=(c == 3), skip_group_check=True)
                last.then_inc(sl_mm, 1)
                if b + 2 < NSEQ:
                    turn_pages(b + 2)
            for half in range(2):
                pe.wait_ge(ss, 8 * half + 4)
                if half:
                    pe.wait_ge(sp_e, 2)
                for k in range(3):
                    n = P if k < 2 else NSAMP
                    last = pe.transpose(main[0:n, 2, bass.ts(k, P)], ls[:, half, k * P:k * P + n], ident)
                last.then_inc(sp_t, 1)
            pe.wait_ge(sp_e, 4)
            for b in range(NSEQ):
                if b % 4 == 0:
                    pe.wait_ge(vp_in[b // 4], 32 * 4)
                rows = bass.ts(b % 4, 32)
                o = main[32 * (b % 4):32 * (b % 4) + 32, (3, 0)[b // 4], :]
                for k in range(2):
                    pe.matmul(o, pts[:, b // 4, k, rows], vpg[b][:, k, :], start=(k == 0), stop=False)
                pe.matmul(o, pts[0:NSAMP, b // 4, 2, rows], vnew[:, :], start=False, stop=True).then_inc(so_mm, 1)
            pe.wait_ge(so_s, 2)
            for c in range(4):
                for half in range(2):
                    last = pe.matmul(main[:, 1, NSAMP * c:NSAMP * (c + 1)], osel[:, half, bass.ts(c, P)],
                                     cst[:, C_SEL + 32 * half:C_SEL + 32 * half + 32], start=(half == 0),
                                     stop=(half == 1))
            last.then_inc(so_t, 1)
            pe.wait_ge(so_e, 2)

            def logits(n):
                b, hh = n // H, n % H
                lo = HD * (hh % 2)
                if n >= 2:
                    pe.wait_ge(at_l, n - 1)
                for c0 in range(0, P * (b + 1), 512):
                    w = min(512, P * (b + 1) - c0)
                    last = pe.matmul(main[:, 2 * (n % 2) + c0 // 512, 0:w], qa[lo:lo + HD, hh // 2, bass.ts(b, P)],
                                     ka[lo:lo + HD, hh // 2, c0:c0 + w], start=True, stop=True)
                last.then_inc(qk_mm, 1)

            def turn_weights(n):
                b = n // H
                pe.wait_ge(at_e, n + 1)
                for i, (m, part) in enumerate(PARTS):
                    if m != n:
                        continue
                    before = [j for j in range(i) if PARTS[j][1] == part]
                    if before:
                        pe.wait_ge(pt_e, before[-1] + 1)
                    if part == 0 and n % H == 3 and n > H:
                        pe.wait_ge(o_c, n // H)
                    for k in range(4 * part, min(4 * part + 4, b + 1)):
                        last = pe.transpose(main[:, 4 + part, bass.ts(k % 4, P)], lb[:, n % 2, bass.ts(k, P)], ident)
                    last.then_inc(pt_t, 1)

            def values(n):
                b, hh = n // H, n % H
                pe.wait_ge(pt_e, LAST_PART[n])
                if hh == 0 and b >= 2:
                    pe.wait_ge(at_m, b - 1)
                o = aux[HD * (hh % 2):HD * (hh % 2) + HD, b % 2, bass.ts(hh // 2, P)]
                for k in range(b + 1):
                    last = pe.matmul(o, vtok[:, k, bass.ts(hh, HD)], pt[:, n % 2, k, :],
                                     start=(k == 0), stop=(k == b))
                last.then_inc(pv_mm, 1)

            def turn_sums(b, n):
                pe.wait_ge(at_o, b + 1)
                pe.wait_ge(pt_e, LAST_PART[n])
                for c in range(4):
                    last = pe.transpose(main[:, 4, bass.ts(c, P)], otok[:, bass.ts(c, P)], ident)
                last.then_inc(ot_mm, 1)

            logits(0)
            for n in range(NQ + 3):
                if n + 1 < NQ:
                    logits(n + 1)
                if 1 <= n <= NQ:
                    values(n - 1)
                if n < NQ:
                    turn_weights(n)
                if n % H == 2 and n > H:
                    turn_sums(n // H - 1, min(n, NQ - 1))

            for t in range(NTC):
                if t == 0:
                    pe.wait_ge(cv, CV_TOTAL)
                for c in range(4):
                    last = pe.matmul(main[:, t, 0:TC], ones[:, :], conv_y[:, c, tcs(t)], start=(c == 0), stop=(c == 3))
                last.then_inc(ln_s, 1)
            for t in range(NTC):
                pe.wait_ge(ln_sem["sq"], t + 1)
                for c in range(4):
                    last = pe.matmul(main[:, 3 + t, 0:TC], ones[:, :], sqc[:, c, :], start=(c == 0), stop=(c == 3))
                last.then_inc(ln_sem["mm"], 1)
            pe.wait_ge(o_l, 8)
            pe.wait_ge(so_e, 2)

            def mix_tile(T, slot, free):
                pe.wait_ge(split_done, T + 1)
                for i, (xh, xl) in ((1, (o_hi, o_lo)), (0, (conv_hi, conv_lo))):
                    for t in range(NTC):
                        if i == 1:
                            pe.wait_ge(mix_free, free + t + 1)
                        else:
                            pe.wait_ge(ln_sem["lo"], t + 1)
                        product(pe, main[:, (ACC_MIX + 2 * t + i) % NBANK, 0:TC], slot, range(4),
                                lambda c: xh[:, c, tcs(t)], lambda c: xl[:, c, tcs(t)], 0, c0=4 * i)\
                            .then_inc(acc_done, 1)

            with pe.Fori(0, 2) as i:
                for k in range(3):
                    mix_tile(T_MIX + k + 3 * i, (T_MIX + k) % RING, 3 * k + 9 * i)
            for k in (6, 7):
                mix_tile(T_MIX + k, (T_MIX + k) % RING, 3 * k)
            pe.wait_ge(mix_lo, 2 + 3 * KD)

            def out_tile(T, k, m):
                back = (1, 3, 2)[k]
                pe.wait_ge(split_done, T + 1)
                for t in range(NTC):
                    pe.wait_ge(out_free, 9 + 3 * m - 3 * back + t + 1)
                    product(pe, main[:, 3 * (k % 2) + t, 0:TC], (T_OUT + k) % RING, range(KD),
                            lambda c: nhi[:, c, tcs(t)], lambda c: nlo[:, c, tcs(t)], 0).then_inc(acc_done, 1)

            with pe.Fori(0, 2) as i:
                for k in range(3):
                    out_tile(T_OUT + k + 3 * i, k, k + 3 * i)
            for m in (6, 7):
                out_tile(T_OUT + m, m % 3, m)

        def m2_act(act):
            act.wait_ge(tk, TK_SAMPLE)
            act.wait_ge(acc_done, ZDONE)

            def copy_pages(b):
                for pg in range(2):
                    act.wait_ge(kp_t, 2 * b + pg + 1)
                    if b >= 2 and pg == 0:
                        act.wait_ge(sl_mm, b - 1)
                    act.activation(kts[:, b % 2, :, bass.ts(pg, P)], main[:, pg, :].rearrange("p (c n) -> p c n", c=4),
                                   ACT.Copy).then_inc(kp_e, 1)

            for b in range(2):
                copy_pages(b)
            for g in range(18):
                t = g % 9
                n = P if t < 8 else NSAMP
                act.wait_ge(kv_t, g + 1)
                src = main[0:n, g % NBANK, :]
                if g < 9:
                    dst = vtok[:, t, :] if t < 8 else vnew[:, :]
                    act.activation(dst, src, ACT.Copy).then_inc(kv_e, 1)
                    act.wait_ge(kv_e, g + 1)
                    act.dma_start(out[3][0, 0, t * P:(t + 1) * P].rearrange("t h d -> t (h d)") if t < 8 else
                                  out[7][0].rearrange("b s h d -> (b s) (h d)"), dst).then_inc(v_out, 16)
                else:
                    dst = kst[0:n, t % 2, :]
                    if t >= 2:
                        act.wait_ge(kst_out[t % 2], 16 * (t // 2))
                    act.activation(dst, src, ACT.Copy).then_inc(kv_e, 1)
                    act.wait_ge(kv_e, g + 1)
                    act.dma_start(out[2][0, 0, t * P:(t + 1) * P].rearrange("t h d -> t (h d)") if t < 8 else
                                  out[6][0].rearrange("b s h d -> (b s) (h d)"), dst).then_inc(kst_out[t % 2], 16)
            for i, n in enumerate((HIST, NSAMP)):
                act.wait_ge(u_t, i + 1)
                act.activation(ust[0:n, i, :], main[0:n, i, :], ACT.Copy).then_inc(u_e, 1)
            act.wait_ge(u_e, 2)
            act.dma_start(out[5][0, 0], ust[0:HIST, 0, :]).then_inc(u_out, 16)
            for b in range(NSEQ):
                act.dma_start(out[9][0, b, HIST - SNEW:HIST, :], ust[SNEW * b:SNEW * (b + 1), 1, :])\
                    .then_inc(u_out, 16)
            for b in range(2, NSEQ):
                copy_pages(b)
            for half in range(2):
                act.wait_ge(ss, 8 * half + 2)
                act.activation(ls[:, half, :], main[:, 4 + half, 0:SKEYS], ACT.Exp, bias=nb[:, half:half + 1],
                               scale=HD ** -0.5, accum_out=sums[:, 0, half:half + 1]).then_inc(se, 1)
            act.wait_ge(u_out, 16 * (NSEQ + 2))
            for half in range(2):
                act.wait_ge(sp_t, half + 1)
                act.activation(pts[:, half, 0:2, :], main[:, 2, 0:2 * P].rearrange("p (k n) -> p k n", k=2), ACT.Copy)\
                    .then_inc(sp_e, 1)
                act.activation(pts[0:NSAMP, half, 2, :], main[0:NSAMP, 2, 2 * P:3 * P], ACT.Copy).then_inc(sp_e, 1)
            act.wait_ge(so_t, 1)
            act.activation(o_hi[:, :, SEQ:TOK], main[:, 1, 0:4 * NSAMP].rearrange("p (c n) -> p c n", c=4), ACT.Copy)\
                .then_inc(so_e, 1)
            act.wait_ge(kst_out[0], 16 * 5)
            act.wait_ge(kst_out[1], 16 * 4)

            def turned(n):
                for i, (m, part) in enumerate(PARTS):
                    if m != n:
                        continue
                    if part == 0 and n >= 2:
                        act.wait_ge(pv_mm, n - 1)
                    act.wait_ge(pt_t, i + 1)
                    k0, k1 = 4 * part, min(4 * part + 4, n // H + 1)
                    act.activation(pt[:, n % 2, k0:k1, :],
                                   main[:, 4 + part, 0:P * (k1 - k0)].rearrange("p (k n) -> p k n", n=P), ACT.Copy)\
                        .then_inc(pt_e, 1)

            for n in range(NQ + 6):
                if 1 <= n <= NQ:
                    turned(n - 1)
                if n % H == 3 and n > H:
                    act.wait_ge(ot_mm, n // H)
                    act.activation(otok[:, :], main[:, 4, :], ACT.Copy).then_inc(o_c, 1)
                if n < NQ:
                    b, hh = n // H, n % H
                    act.wait_ge(at_nb, n + 1)
                    if hh == 0 and b >= 2:
                        act.wait_ge(at_r, b - 1)
                    act.activation(lb[:, n % 2, 0:P * (b + 1)], lb[:, n % 2, 0:P * (b + 1)], ACT.Exp,
                                   bias=nb[:, n % 2:n % 2 + 1], scale=HD ** -0.5,
                                   accum_out=sums[:, b % 2, hh:hh + 1]).then_inc(at_e, 1)
                if n % H == 5 and n > H:
                    b = n // H - 1
                    act.wait_ge(at_m, b + 1)
                    act.activation(o_hi[:, :, bass.ts(b, P)], otok[:, :].rearrange("p (c n) -> p c n", c=4), ACT.Copy)\
                        .then_inc(o_h, 1)
            for t in range(NTC):
                act.wait_ge(ln_y, t + 1)
                if t:
                    act.wait_ge(ln_sem["mm"], t)
                act.activation(sqc[:, :, :], conv_y[:, :, tcs(t)], ACT.Square).then_inc(ln_sem["sq"], 1)
                act.wait_ge(ln_sem["mm"], t + 1)
                act.activation(rstd_c[:, tcs(t)], main[:, 3 + t, 0:TC], ACT.Sqrt, scale=1.0 / D_CONV, bias=eps)\
                    .then_inc(ln_sem["sd"], 1)
            for t in range(NTC):
                act.wait_ge(ln_sem["ml"], t + 1)
                for c in range(4):
                    last = act.activation(conv_y[:, c, tcs(t)], conv_y[:, c, tcs(t)], ACT.Silu,
                                          scale=par[:, ROW_LNG + c:ROW_LNG + c + 1],
                                          bias=par[:, ROW_LNB + c:ROW_LNB + c + 1])
                last.then_inc(ln_sem["af"], 1)
                act.wait_ge(ln_sem["af"], t + 1)
                act.activation(conv_hi[:, :, tcs(t)], conv_y[:, :, tcs(t)], ACT.Copy).then_inc(ln_sem["hi"], 1)
            with act.Fori(0, KD // 2) as i:
                for k in range(2):
                    for t in range(NTC):
                        act.wait_ge(mix_a, 18 * i + 9 * k + 3 * t + 3)
                        act.activation(nhi[:, bass.ds(2 * i + k, 1), tcs(t)].rearrange("p o n -> p (o n)"),
                                       mixt[:, (3 * k + t) % 2, 0, :], ACT.Copy).then_inc(mix_hi, 1)

        def m2_dve(dve):
            dve.wait_ge(k_in, 16)
            dve.wait_ge(q_in, 16)
            dve.memset(qb[:, :, :, :], 0.0).then_inc(sa_q, 1)
            dve.wait_ge(sa_q, 1)
            for c in range(4):
                for s in range(2):
                    dve.tensor_copy(kts[:, s, c, PAST:SKEYS], ka[:, c, SEQ:TOK]).then_inc(sa_q, 1)
                for p in range(2):
                    r, hh = slice(HD * p, HD * p + HD), 2 * c + p
                    dve.tensor_copy(qb[r, c, :, SNEW * hh:SNEW * (hh + 1)],
                                    qa[r, c, SEQ:TOK].rearrange("p (b s) -> p b s", b=NSEQ)).then_inc(sa_q, 1)
            conv_chunk(dve, 1, 0, 18)
            for half in range(2):
                dve.wait_ge(sl_mm, 4 * half + 4)
                dve.reduce_max(mx[:, half:half + 1], main[:, 4 + half, 0:SKEYS], AX_X).then_inc(ss, 1)
                dve.wait_ge(ss, 8 * half + 1)
                dve.tensor_scalar(nb[:, half:half + 1], mx[:, half:half + 1], -HD ** -0.5, None, ALU.mult)\
                    .then_inc(ss, 1)
                dve.wait_ge(se, half + 1)
                dve.reciprocal(rinv[:, 0, half:half + 1], sums[:, 0, half:half + 1]).then_inc(ss, 1)
                dve.wait_ge(ss, 8 * half + 3)
                dve.tensor_scalar(ls[:, half, :], ls[:, half, :], rinv[:, 0, half:half + 1], None, ALU.mult)\
                    .then_inc(ss, 5 if half == 0 else 1)
            conv_chunk(dve, 1, 18)
            dve.wait_ge(kst_out[0], 16 * 5)
            dve.wait_ge(kst_out[1], 16 * 4)
            for half in range(2):
                dve.wait_ge(so_mm, 4 * half + 4)
                dve.tensor_tensor(osel[:, half, :].rearrange("p (h d) -> p h d", h=H),
                                  main[:, (3, 0)[half], :].rearrange("p (h d) -> p h d", h=H),
                                  cst[:, C_HEAD:C_HEAD + H].unsqueeze(2).to_broadcast([P, H, HD]), ALU.mult)\
                    .then_inc(so_s, 1)
            dve.wait_ge(so_e, 1)
            dve.tensor_tensor(o_lo[:, :, SEQ:TOK], main[:, 1, 0:4 * NSAMP].rearrange("p (c n) -> p c n", c=4),
                              o_hi[:, :, SEQ:TOK].bitcast(F32), ALU.subtract).then_inc(so_e, 1)
            for n in range(NQ + 7):
                if n < NQ:
                    b = n // H
                    w = P * (b + 1)
                    dve.wait_ge(qk_mm, n + 1)
                    if n >= 2:
                        dve.wait_ge(pt_t, LAST_PART[n - 2])
                        dve.wait_ge(at_nb, n - 1)
                    dve.tensor_tensor_reduce(lb[:, n % 2, 0:w],
                                             main[:, 2 * (n % 2):2 * (n % 2) + 2, :].rearrange("p a n -> p (a n)")[:, 0:w],
                                             pick[:, off(b):off(b + 1)], 1.0, 3 * NEG, ALU.add, ALU.max,
                                             mx[:, n % 2:n % 2 + 1]).then_inc(at_l, 1)
                    dve.wait_ge(at_l, n + 1)
                    dve.tensor_scalar(nb[:, n % 2:n % 2 + 1], mx[:, n % 2:n % 2 + 1], -HD ** -0.5, None, ALU.mult)\
                        .then_inc(at_nb, 1)
                for j in TAPS_AT[n]:
                    c, k = 2 + j % 2, j // 2
                    if k == 0:
                        conv_first(dve, c)
                    else:
                        dve.wait_ge(cv, CV_HALF + j - 1)
                        conv_tap(dve, c, taps[:, c, k:k + 1], slice(k, k + SEQ))
                if n % H == 1 and n > H:
                    b = n // H - 1
                    dve.wait_ge(at_e, H * (b + 1))
                    dve.reciprocal(rinv[:, b % 2, :], sums[:, b % 2, :]).then_inc(at_r, 1)
                    dve.wait_ge(at_r, b + 1)
                    if b:
                        dve.wait_ge(o_l, b)
                    dve.tensor_copy(otok[:, :].rearrange("p (h d) -> p h d", h=H),
                                    rinv[:, b % 2, :].unsqueeze(2).to_broadcast([P, H, HD])).then_inc(at_o, 1)
                if n % H == 4 and n > H:
                    b = n // H - 1
                    dve.wait_ge(o_c, b + 1)
                    dve.wait_ge(pv_mm, H * (b + 1))
                    dve.tensor_tensor(otok[:, :], aux[:, b % 2, :], otok[:, :], ALU.mult).then_inc(at_m, 1)
                if n % H == 6 and n > H:
                    b = n // H - 1
                    dve.wait_ge(o_h, b + 1)
                    dve.tensor_tensor(o_lo[:, :, bass.ts(b, P)], otok[:, :].rearrange("p (c n) -> p c n", c=4),
                                      o_hi[:, :, bass.ts(b, P)].bitcast(F32), ALU.subtract).then_inc(o_l, 1)
            for t in range(NTC):
                dve.wait_ge(ln_s, t + 1)
                y = conv_y[:, :, tcs(t)]
                dve.scalar_tensor_tensor(y, main[:, t, 0:TC].unsqueeze(1).to_broadcast([P, 4, TC]), -1.0 / D_CONV, y,
                                         ALU.mult, ALU.add).then_inc(ln_y, 1)
            for t in range(NTC):
                dve.wait_ge(ln_sem["sd"], t + 1)
                dve.reciprocal(rstd_c[:, tcs(t)], rstd_c[:, tcs(t)]).then_inc(ln_sem["rs"], 1)
                dve.wait_ge(ln_sem["rs"], t + 1)
                y = conv_y[:, :, tcs(t)]
                dve.tensor_tensor(y, y, rstd_c[:, tcs(t)].unsqueeze(1).to_broadcast([P, 4, TC]), ALU.mult)\
                    .then_inc(ln_sem["ml"], 1)
            dve.drain().then_inc(mix_free, 3)
            for t in range(NTC):
                dve.wait_ge(ln_sem["hi"], t + 1)
                dve.tensor_tensor(conv_lo[:, :, tcs(t)], conv_y[:, :, tcs(t)], conv_hi[:, :, tcs(t)].bitcast(F32),
                                  ALU.subtract).then_inc(ln_sem["lo"], 1)
            dve.wait_ge(o_l, 8)
            dve.drain().then_inc(mix_lo, 2)
            with dve.Fori(0, KD // 2) as i:
                for k in range(2):
                    dve.wait_ge(g_in[k], 32 * i + 32)
                    for t in range(NTC):
                        s = (3 * k + t) % 2
                        x, y = mixt[:, s, 0, :], mixt[:, s, 1, :]
                        at = 18 * i + 9 * k + 3 * t
                        dve.wait_ge(acc_done, ACC_MIX + 12 * i + 6 * k + 3 + t + 1)
                        dve.wait_ge(mix_lo, 6 * i + 3 * k + t + 1)
                        dve.tensor_tensor(x, main[:, (ACC_MIX + 2 * t) % NBANK, 0:TC], gates[:, k, 0, tcs(t)], ALU.mult)\
                            .then_inc(mix_a, 1)
                        dve.tensor_tensor(y, main[:, (ACC_MIX + 2 * t + 1) % NBANK, 0:TC], gates[:, k, 1, tcs(t)],
                                          ALU.mult).then_inc(mix_free, 1)
                        dve.wait_ge(mix_free, 3 + 6 * i + 3 * k + t + 1)
                        dve.wait_ge(mix_a, at + 1)
                        dve.tensor_tensor(x, x, y, ALU.add).then_inc(mix_a, 2)
                        dve.wait_ge(mix_hi, 6 * i + 3 * k + t + 1)
                        m = 2 * i + k
                        dve.tensor_tensor(nlo[:, bass.ds(m, 1), tcs(t)].rearrange("p o n -> p (o n)"), x,
                                          nhi[:, bass.ds(m, 1), tcs(t)].bitcast(F32).rearrange("p o n -> p (o n)"),
                                          ALU.subtract).then_inc(mix_lo, 1)
            dve.drain().then_inc(out_free, 9)

            def out_tile(k, m, at):
                for t in range(NTC):
                    n = TC if t < 2 else PLAST
                    bank = main[:, 3 * (k % 2) + t, :]
                    dve.wait_ge(acc_done, ACC_OUT + at + t + 1)
                    hm = h[:, bass.ds(m, 1), :].rearrange("p o n -> p (o n)")
                    gm = cond_gate[:, bass.ds(m, 1), :].rearrange("p o n -> p (o n)")
                    sm = small2[:, bass.ds(m, 1), :].rearrange("p o n -> p (o n)")
                    if t == 2:
                        dve.tensor_tensor(sm.rearrange("p (b s) -> p b s", b=NSEQ),
                                          bank[:, PLAST:TC].rearrange("p (b s) -> p b s", b=NSEQ),
                                          gm[:, 1:NCOND].unsqueeze(2).to_broadcast([P, NSEQ, SNEW]), ALU.mult)\
                            .then_inc(out_s, 1)
                        dve.wait_ge(out_s, m + 1)
                        dve.tensor_tensor(hm[:, SEQ:TOK], hm[:, SEQ:TOK], sm, ALU.add)
                    dve.scalar_tensor_tensor(hm[:, t * TC:t * TC + n], bank[:, 0:n], gm[:, 0:1],
                                             hm[:, t * TC:t * TC + n], ALU.mult, ALU.add).then_inc(out_free, 1)

            dve.wait_ge(h_in[0], 16)
            dve.wait_ge(h_in[1], 16)
            with dve.Fori(0, 2) as i:
                for k in range(3):
                    out_tile(k, k + 3 * i, 3 * k + 9 * i)
            for m in (6, 7):
                out_tile(m % 3, m, 3 * m)
            dve.wait_ge(out_free, 9 + 3 * KD)

        small2 = place("small2", [P, KD, NSAMP], F32, UB + 41984)

        ytok = place("ytok", [P, 3, D], F32, NB)
        SEGS = [(0, 128), (128, 128), (256, 96)]
        yp, ys = out[0][0], out[1].rearrange("b s d -> (b s) d")

        def final_pe(pe, t):
            norm_wait(pe, "f", "af", 2 * t + 2)
            for g, (o, n) in enumerate(SEGS):
                for half in range(2):
                    if t:
                        pe.wait_ge((fin_act, fin_dve)[half], 3 * (t - 1) + g + 1)
                    for c in range(4):
                        last = pe.transpose(main[0:n, 2 * g + half, bass.ts(c, P)],
                                            tmp[:, 4 * half + c, o:o + n], ident)
                    last.then_inc(fin_t, 1)

        def final_act(act, t):
            for g, (o, n) in enumerate(SEGS):
                act.wait_ge(fin_t, 6 * t + 2 * g + 1)
                if t:
                    act.wait_ge(y_out[g], 16 * t)
                act.activation(ytok[0:n, g, 0:512], main[0:n, 2 * g, :], ACT.Copy).then_inc(fin_act, 1)

        def final_dve(dve, t):
            for g, (o, n) in enumerate(SEGS):
                dve.wait_ge(fin_t, 6 * t + 2 * g + 2)
                if t:
                    dve.wait_ge(y_out[g], 16 * t)
                dve.tensor_copy(ytok[0:n, g, 512:D], main[0:n, 2 * g + 1, :]).then_inc(fin_dve, 1)

        def final_sp(sp):
            for t in range(NTC):
                for g, (o, n) in enumerate(SEGS):
                    sp.wait_ge(fin_act, 3 * t + g + 1)
                    sp.wait_ge(fin_dve, 3 * t + g + 1)
                    tok = t * TC + o
                    n = min(n, SEQ - tok)
                    sp.dma_start(yp[tok:tok + n, :], ytok[0:n, g, :]).then_inc(y_out[g], 16)
                    if tok + n == SEQ:
                        sp.dma_start(ys, ytok[n:n + NSAMP, g, :]).then_inc(y_out[g], 16)
            for g in range(3):
                sp.wait_ge(y_out[g], 16 * (3 + (g == 2)))
            sp.wait_ge(v_out, 16 * 9)

        def ada_group(eng, g, turn=True):
            if eng is nc.tensor:
                pe_ada(eng, g, g % 2, g // 2 + 1, main[:, 5])
                if turn:
                    pe_ada_turn(eng, g, main[:, 4], ada_rows[0])
            elif eng is nc.scalar:
                act_ada(eng, g, main[:, 5], ada_rows[0])
            else:
                dve_ada(eng, g, main[:, 4])

        def ada_beside(eng, t):
            ada_group(eng, ADA_NORM1 + t)

        def pe_ada_beside(pe, t):
            if t:
                pe_ada_turn(pe, ADA_NORM1 + t - 1, main[:, 4], ada_rows[0])
            ada_group(pe, ADA_NORM1 + t, turn=False)

        def pe_ada_end(pe):
            pe_ada_turn(pe, INIT_ADA // 4 - 1, main[:, 4], ada_rows[0])
            pe.wait_ge(ada_out, INIT_ADA // 4 + 1)

        norm1 = norm("1", 0, beside={"pe": pe_ada_beside, "pe_end": pe_ada_end, "act": ada_beside, "dve": ada_beside})
        norm3, norm_f = norm("2", 2), norm("f", None, final_act, final_dve, final_pe)
        ffn1 = ffn("1", T_FFN1, ACC_FFN1, L0["w1_gate"], L0["w1_up"], L0["w1_down"], 0, norm1, True)
        ffn2 = ffn("2", T_FFN2, ACC_FFN2, L0["w2_gate"], L0["w2_up"], L0["w2_down"], 2, norm3, False)

        block = ctx.enter_context(nc.Block())

        @block.sync
        def _(sp):
            sp_init(sp)
            for g in range(INIT_ADA // 4):
                ada_load(sp, g, g % 2, g // 2 + 1)
            ffn1["sp"](sp)
            m1_sp(sp)
            m2_sp(sp)
            ffn2["sp"](sp)
            final_sp(sp)

        @block.gpsimd
        def _(pool):
            pool.drain().then_inc(split_done, RING)
            ffn1["pool"](pool)
            m1_pool(pool)
            m2_pool(pool)
            ffn2["pool"](pool)

        @block.tensor
        def _(pe):
            pe.drain().then_inc(acc_done, FFN_ACC)
            pe.drain().then_inc(ada_mm, 2)
            pe.drain().then_inc(ada_t, 1)
            pe_init(pe)
            pe.wait_ge(init_e, NINIT)
            for g in range(ADA_NORM1):
                ada_group(pe, g)
            ffn1["pe"](pe)
            m1_pe(pe)
            m2_pe(pe)
            ffn2["pe"](pe)
            norm_f["pe"](pe)

        @block.scalar
        def _(act):
            act.drain().then_inc(ada_copy, 1)
            act_init(act)
            act.wait_ge(init_e, NINIT)
            act.wait_ge(consts_in, 16)
            for g in range(ADA_NORM1):
                ada_group(act, g)
            act.wait_ge(mod_set, 1)
            ffn1["act_free"](act)
            norm1["act"](act)
            ffn1["act"](act)
            ffn_wait(act, "1", "down_free", 24 * NPAIR + 24)
            act.drain().then_inc(z_free, 6)
            act.wait_ge(mod_set, 5)
            norm_m["act"](act)
            m1_act(act)
            m2_act(act)
            act.wait_ge(out_free, 9 + 3 * KD)
            ffn2["act_free"](act)
            norm3["act"](act)
            ffn2["act"](act)
            ffn_wait(act, "2", "down_free", 24 * NPAIR + 24)
            norm_f["act"](act)

        @block.vector
        def _(dve):
            dve.drain().then_inc(ada_out, 1)
            dve_init(dve)
            dve.wait_ge(init_e, NINIT)
            for g in range(ADA_NORM1):
                ada_group(dve, g)
            dve_mod(dve, 0, ROW_G1, ADA_NORM1)
            dve.wait_ge(mod_set, 1)
            ffn1["dve_free"](dve)
            norm1["dve"](dve)
            dve.wait_ge(ada_out, INIT_ADA // 4 + 1)
            dve_half_gate(dve, 0)
            dve.wait_ge(mod_set, 2)
            ffn1["dve"](dve)
            ffn_wait(dve, "1", "down_free", 24 * NPAIR + 24)
            dve_mod(dve, 1, ROW_GM, ADA_TILES // 4)
            dve_mod(dve, 2, ROW_G2, ADA_TILES // 4)
            dve_half_gate(dve, 2)
            dve.wait_ge(mod_set, 5)
            norm_m["dve"](dve)
            m1_dve(dve)
            m2_dve(dve)
            ffn2["dve_free"](dve)
            norm3["dve"](dve)
            ffn2["dve"](dve)
            ffn_wait(dve, "2", "down_free", 24 * NPAIR + 24)
            norm_f["dve"](dve)


_INS = ["x_prompt", "x_sample", "cache_k", "cache_v", "cache_idx_k", "state_conv", "page_table", "c_prompt",
        "c_sample", "w_ada", "b_ada", "g_ffn1", "w1_gate", "w1_up", "w1_down", "g_mix", "w_in", "w_dw", "b_dw",
        "ln_g", "ln_b", "w_conv_out", "w_attn_o", "w_out", "g_ffn2", "w2_gate", "w2_up", "w2_down", "g_final"]
_OUTS = [(1, SEQ, D), (NSEQ, SNEW, D), (1, 1, SEQ, H, HD), (1, 1, SEQ, H, HD), (1, 1, SEQ, HD),
         (1, 1, HIST, D_CONV), (1, NSEQ, SNEW, H, HD), (1, NSEQ, SNEW, H, HD), (1, NSEQ, SNEW, HD),
         (1, NSEQ, HIST, D_CONV)]


def kernel(**inputs):
    import concourse.bacc as bacc
    from concourse.bass_utils import run_bass_kernel_spmd

    nc = bacc.Bacc("TRN2", target_bir_lowering=False, num_devices=1)
    arrays = {f"in_{name}": np.ascontiguousarray(inputs[name]) for name in _INS}
    arrays["in_consts"], arrays["in_rope"] = constants()
    ins = {n: nc.dram_tensor(n, a.shape, mybir.dt.from_np(a.dtype), kind="ExternalInput").ap()
           for n, a in arrays.items()}
    outs = [nc.dram_tensor(f"out_{i}", shape, F32, kind="ExternalOutput").ap() for i, shape in enumerate(_OUTS)]
    build(nc, {n: ins[f"in_{n}"] for n in _INS}, outs, ins["in_consts"], ins["in_rope"])
    r = run_bass_kernel_spmd(nc, [arrays], core_ids=[0])
    return tuple(r.results[0][f"out_{i}"] for i in range(len(_OUTS)))
```
